# Optimizing a Trainium2 kernel written in Bass

```python
import math
import jax
import jax.numpy as jnp
from jax import lax
import numpy as np

D_MODEL = 1024
BATCH = 1
SEQ = 512
DEPTH = 2

CTX_LEN = 256
GRID_W = 64
HEAD_DIM = 64
Q_BLOCK = 128
ROPE_BASE = 10000.0
EPS = 1e-6
NEG_INF = -1e30

WIN = 128
A_HEADS = 8
A_KV_HEADS = 2
A_GROUP = A_HEADS // A_KV_HEADS
B_HEADS = 4
B_NOPE = 64
B_ROPE = 32
B_V = 64
B_Q_RANK = 256
B_KV_RANK = 128
C_HEADS = 4
C_DH = 32
C_V = 2 * C_DH

A_WIDTH = A_HEADS * HEAD_DIM
B_WIDTH = B_HEADS * B_V
C_WIDTH = C_HEADS * C_V
MIX_WIDTH = A_WIDTH + B_WIDTH + C_WIDTH

IN_SPLITS = (A_HEADS * HEAD_DIM, A_KV_HEADS * HEAD_DIM, A_KV_HEADS * HEAD_DIM,
             B_Q_RANK, B_KV_RANK, B_ROPE,
             C_HEADS * 2 * C_DH, C_HEADS * 2 * C_DH, C_HEADS * C_V)
IN_WIDTH = sum(IN_SPLITS)

N_EXPERTS = 16
EC_FACTOR = 2
D_EXPERT = 512

kernel_name = "hybrid_parallel_heads_diffusion_block"

def rmsnorm(x, g):
    xf = x.astype(jnp.float32)
    xf = xf * lax.rsqrt(jnp.mean(xf * xf, axis=-1, keepdims=True) + EPS)
    return xf.astype(x.dtype) * g

def modulate(h, shift, scale):
    return h * (1.0 + scale) + shift

def split_cols(p):
    offs = np.cumsum(IN_SPLITS)[:-1].tolist()
    return jnp.split(p, offs, axis=-1)

def axial_rope(T, rot_dim):
    rows = T // GRID_W
    row = jnp.repeat(jnp.arange(rows), GRID_W)
    col = jnp.tile(jnp.arange(GRID_W), rows)
    n_f = rot_dim // 4
    inv = ROPE_BASE ** (-jnp.arange(n_f, dtype=jnp.float32) / n_f)
    ang = jnp.stack([row[:, None] * inv, col[:, None] * inv], axis=1)
    return jnp.cos(ang), jnp.sin(ang)

def apply_rope(x, cos, sin):
    shape = x.shape
    n_f = shape[-1] // 4
    xr = x.reshape(*shape[:-1], 2, 2, n_f)
    x0, x1 = xr[..., 0, :], xr[..., 1, :]
    bshape = (shape[1],) + (1,) * (x.ndim - 3) + (2, n_f)
    cos = cos.reshape(bshape).astype(x.dtype)
    sin = sin.reshape(bshape).astype(x.dtype)
    return jnp.stack([x0 * cos - x1 * sin, x1 * cos + x0 * sin], axis=-2).reshape(shape)

def map_query_blocks(fn, qs):
    B, T = qs[0].shape[:2]
    nb = T // Q_BLOCK
    blocks = tuple(jnp.moveaxis(a.reshape(B, nb, Q_BLOCK, *a.shape[2:]), 1, 0) for a in qs)
    out = lax.map(fn, blocks)
    return jnp.moveaxis(out, 0, 1).reshape(B, T, *out.shape[3:])

def window_gqa_mixer(qa, ka, va, qa_c, ka_c, va_c, sink, rope, need_ctx):
    B, T = qa.shape[:2]
    L = ka_c.shape[1]
    nb = T // WIN
    scale = HEAD_DIM ** -0.5
    q = apply_rope(qa.reshape(B, T, A_HEADS, HEAD_DIM), *rope)
    k = apply_rope(ka.reshape(B, T, A_KV_HEADS, HEAD_DIM), *rope)
    v = va.reshape(B, T, A_KV_HEADS, HEAD_DIM)
    kc = ka_c.reshape(B, L, A_KV_HEADS, HEAD_DIM)
    vc = va_c.reshape(B, L, A_KV_HEADS, HEAD_DIM)
    sink_f = sink.astype(jnp.float32)

    qb = q.reshape(B, nb, WIN, A_KV_HEADS, A_GROUP, HEAD_DIM)

    def band(a):
        ap = jnp.pad(a, ((0, 0), (WIN, WIN), (0, 0), (0, 0))).reshape(B, nb + 2, WIN, A_KV_HEADS, HEAD_DIM)
        return jnp.concatenate([ap[:, :-2], ap[:, 1:-1], ap[:, 2:]], axis=2)

    kb, vb = band(k), band(v)
    qi = jnp.arange(WIN)[:, None]
    kj = jnp.arange(3 * WIN)[None, :]
    kpos = jnp.arange(nb)[:, None, None] * WIN - WIN + kj
    valid = (kj >= qi) & (kj <= qi + 2 * WIN) & (kpos >= 0) & (kpos < T)
    s_loc = jnp.einsum('bnqhgd,bnkhd->bhgnqk', qb, kb).astype(jnp.float32) * scale
    s_loc = jnp.where(valid, s_loc, NEG_INF)
    s_ctx = jnp.einsum('bnqhgd,bkhd->bhgnqk', qb, kc).astype(jnp.float32) * scale
    s_sink = jnp.broadcast_to(sink_f.reshape(1, A_KV_HEADS, A_GROUP, 1, 1, 1), s_ctx.shape[:-1] + (1,))
    p = jax.nn.softmax(jnp.concatenate([s_loc, s_ctx, s_sink], axis=-1), axis=-1).astype(v.dtype)
    o = (jnp.einsum('bhgnqk,bnkhd->bnqhgd', p[..., :3 * WIN], vb)
         + jnp.einsum('bhgnqk,bkhd->bnqhgd', p[..., 3 * WIN:3 * WIN + L], vc))
    o = o.reshape(B, T, A_WIDTH)

    o_c = None
    if need_ctx:
        qcg = qa_c.reshape(B, L, A_KV_HEADS, A_GROUP, HEAD_DIM)
        s = jnp.einsum('bqhgd,bkhd->bhgqk', qcg, kc).astype(jnp.float32) * scale
        s_sink_c = jnp.broadcast_to(sink_f.reshape(1, A_KV_HEADS, A_GROUP, 1, 1), s.shape[:-1] + (1,))
        pc = jax.nn.softmax(jnp.concatenate([s, s_sink_c], axis=-1), axis=-1)[..., :L].astype(vc.dtype)
        o_c = jnp.einsum('bhgqk,bkhd->bqhgd', pc, vc).reshape(B, L, A_WIDTH)
    return o, o_c

def mla_attend(qn, qr, kn, kr, v):
    s = (jnp.einsum('bqhd,bkhd->bhqk', qn, kn) + jnp.einsum('bqhr,bkr->bhqk', qr, kr)).astype(jnp.float32)
    p = jax.nn.softmax(s * (B_NOPE + B_ROPE) ** -0.5, axis=-1).astype(v.dtype)
    return jnp.einsum('bhqk,bkhd->bqhd', p, v)

def mla_mixer(cq, ckv, kr, cq_c, ckv_c, kr_c, q_norm, w_uq, kv_norm, w_ukv, rope, need_ctx):
    def project(cq_, ckv_, kr_, rope_):
        B_, N = cq_.shape[:2]
        q = (rmsnorm(cq_, q_norm) @ w_uq).reshape(B_, N, B_HEADS, B_NOPE + B_ROPE)
        kv = (rmsnorm(ckv_, kv_norm) @ w_ukv).reshape(B_, N, B_HEADS, B_NOPE + B_V)
        qn, qr = q[..., :B_NOPE], q[..., B_NOPE:]
        kn, v = kv[..., :B_NOPE], kv[..., B_NOPE:]
        if rope_ is not None:
            qr = apply_rope(qr, *rope_)
            kr_ = apply_rope(kr_, *rope_)
        return qn, qr, kn, kr_, v

    B, T = cq.shape[:2]
    qn, qr, kn, krl, v = project(cq, ckv, kr, rope)
    qn_c, qr_c, kn_c, kr_cc, v_c = project(cq_c, ckv_c, kr_c, None)
    kn_all = jnp.concatenate([kn, kn_c], axis=1)
    kr_all = jnp.concatenate([krl, kr_cc], axis=1)
    v_all = jnp.concatenate([v, v_c], axis=1)
    o = map_query_blocks(lambda a: mla_attend(a[0], a[1], kn_all, kr_all, v_all), (qn, qr))
    o = o.reshape(B, T, B_WIDTH)
    o_c = None
    if need_ctx:
        o_c = mla_attend(qn_c, qr_c, kn_c, kr_cc, v_c).reshape(B, -1, B_WIDTH)
    return o, o_c

def diff_attend(q, k, v, lam):
    s = jnp.einsum('bqhmd,bkhmd->bhmqk', q, k).astype(jnp.float32) * C_DH ** -0.5
    p = jax.nn.softmax(s, axis=-1)
    a = p[:, :, 0] - lam * p[:, :, 1]
    return jnp.einsum('bhqk,bkhd->bqhd', a.astype(v.dtype), v)

def diff_mixer(qd, kd, vd, qd_c, kd_c, vd_c, lam_q1, lam_k1, lam_q2, lam_k2, sub_norm, lam_init, rope, need_ctx):
    B, T = qd.shape[:2]
    L = qd_c.shape[1]
    lam = (jnp.exp(jnp.sum((lam_q1 * lam_k1).astype(jnp.float32)))
           - jnp.exp(jnp.sum((lam_q2 * lam_k2).astype(jnp.float32))) + lam_init)
    q = apply_rope(qd.reshape(B, T, C_HEADS, 2, C_DH), *rope)
    k = apply_rope(kd.reshape(B, T, C_HEADS, 2, C_DH), *rope)
    v = vd.reshape(B, T, C_HEADS, C_V)
    qc = qd_c.reshape(B, L, C_HEADS, 2, C_DH)
    kc = kd_c.reshape(B, L, C_HEADS, 2, C_DH)
    vc = vd_c.reshape(B, L, C_HEADS, C_V)
    k_all = jnp.concatenate([k, kc], axis=1)
    v_all = jnp.concatenate([v, vc], axis=1)
    o = map_query_blocks(lambda a: diff_attend(a[0], k_all, v_all, lam), (q,))
    o = (rmsnorm(o, sub_norm) * (1.0 - lam_init)).reshape(B, T, C_WIDTH)
    o_c = None
    if need_ctx:
        o_c = (rmsnorm(diff_attend(qc, kc, vc, lam), sub_norm) * (1.0 - lam_init)).reshape(B, L, C_WIDTH)
    return o, o_c

def expert_choice_ffn(h, w_router, w_gate, w_up, w_down):
    B, N, D = h.shape
    cap = EC_FACTOR * N // N_EXPERTS
    aff = jax.nn.softmax((h @ w_router).astype(jnp.float32), axis=-1)
    gate_val, tok = lax.top_k(jnp.swapaxes(aff, 1, 2), cap)
    xg = jax.vmap(lambda hb, ib: hb[ib])(h, tok)
    hid = jax.nn.silu(jnp.einsum('becd,edf->becf', xg, w_gate)) * jnp.einsum('becd,edf->becf', xg, w_up)
    y = jnp.einsum('becf,efd->becd', hid, w_down) * gate_val[..., None].astype(h.dtype)
    return jax.vmap(lambda ib, yb: jnp.zeros((N, D), yb.dtype).at[ib.reshape(-1)].add(yb.reshape(-1, D)))(tok, y)

def setup_inputs(seed: int = 0) -> dict:
    key = jax.random.key(seed)
    ks = jax.random.split(key, 25)

    def nrm(k, shape, s):
        return jax.random.normal(k, shape, jnp.float32) * s

    def gain(k, shape):
        return 1.0 + nrm(k, shape, 0.02)

    return {
        "x": nrm(ks[0], (BATCH, SEQ, D_MODEL), 1.0),
        "c": nrm(ks[1], (BATCH, D_MODEL), 1.0),
        "ctx": nrm(ks[2], (BATCH, CTX_LEN, D_MODEL), 1.0),
        "c_ctx": nrm(ks[3], (D_MODEL,), 1.0),
        "norm1": gain(ks[4], (DEPTH, D_MODEL)),
        "norm2": gain(ks[5], (DEPTH, D_MODEL)),
        "w_ada": nrm(ks[6], (DEPTH, D_MODEL, 6 * D_MODEL), 0.5 * D_MODEL ** -0.5),
        "b_ada": nrm(ks[7], (DEPTH, 6 * D_MODEL), 0.02),
        "w_in": nrm(ks[8], (DEPTH, D_MODEL, IN_WIDTH), D_MODEL ** -0.5),
        "sink": nrm(ks[9], (DEPTH, A_HEADS), 0.5),
        "mla_q_norm": gain(ks[10], (DEPTH, B_Q_RANK)),
        "w_uq": nrm(ks[11], (DEPTH, B_Q_RANK, B_HEADS * (B_NOPE + B_ROPE)), B_Q_RANK ** -0.5),
        "mla_kv_norm": gain(ks[12], (DEPTH, B_KV_RANK)),
        "w_ukv": nrm(ks[13], (DEPTH, B_KV_RANK, B_HEADS * (B_NOPE + B_V)), B_KV_RANK ** -0.5),
        "lam_q1": nrm(ks[14], (DEPTH, C_DH), 0.1),
        "lam_k1": nrm(ks[15], (DEPTH, C_DH), 0.1),
        "lam_q2": nrm(ks[16], (DEPTH, C_DH), 0.1),
        "lam_k2": nrm(ks[17], (DEPTH, C_DH), 0.1),
        "diff_norm": gain(ks[18], (DEPTH, C_V)),
        "w_out": nrm(ks[19], (DEPTH, MIX_WIDTH, D_MODEL), MIX_WIDTH ** -0.5),
        "w_router": nrm(ks[20], (DEPTH, D_MODEL, N_EXPERTS), D_MODEL ** -0.5),
        "w_gate": nrm(ks[21], (DEPTH, N_EXPERTS, D_MODEL, D_EXPERT), D_MODEL ** -0.5),
        "w_up": nrm(ks[22], (DEPTH, N_EXPERTS, D_MODEL, D_EXPERT), D_MODEL ** -0.5),
        "w_down": nrm(ks[23], (DEPTH, N_EXPERTS, D_EXPERT, D_MODEL), D_EXPERT ** -0.5),
        "final_norm": gain(ks[24], (D_MODEL,)),
    }

def reference(x, c, ctx, c_ctx, norm1, norm2, w_ada, b_ada, w_in, sink, mla_q_norm, w_uq, mla_kv_norm, w_ukv,
              lam_q1, lam_k1, lam_q2, lam_k2, diff_norm, w_out, w_router, w_gate, w_up, w_down, final_norm):
    T = x.shape[1]
    rope_a = axial_rope(T, HEAD_DIM)
    rope_bc = axial_rope(T, B_ROPE)
    xc = ctx
    for l in range(DEPTH):
        need_ctx = l < DEPTH - 1
        mod = jax.nn.silu(c) @ w_ada[l] + b_ada[l]
        mod_c = jax.nn.silu(c_ctx) @ w_ada[l] + b_ada[l]
        sh1, sc1, g1, sh2, sc2, g2 = jnp.split(mod[:, None, :], 6, axis=-1)
        csh1, csc1, cg1, csh2, csc2, cg2 = jnp.split(mod_c, 6, axis=-1)

        p = modulate(rmsnorm(x, norm1[l]), sh1, sc1) @ w_in[l]
        pc = modulate(rmsnorm(xc, norm1[l]), csh1, csc1) @ w_in[l]
        qa, ka, va, cq, ckv, kr, qd, kd, vd = split_cols(p)
        qa_c, ka_c, va_c, cq_c, ckv_c, kr_c, qd_c, kd_c, vd_c = split_cols(pc)
        oa, oa_c = window_gqa_mixer(qa, ka, va, qa_c, ka_c, va_c, sink[l], rope_a, need_ctx)
        ob, ob_c = mla_mixer(cq, ckv, kr, cq_c, ckv_c, kr_c, mla_q_norm[l], w_uq[l], mla_kv_norm[l], w_ukv[l],
                             rope_bc, need_ctx)
        lam_init = 0.8 - 0.6 * math.exp(-0.3 * l)
        od, od_c = diff_mixer(qd, kd, vd, qd_c, kd_c, vd_c, lam_q1[l], lam_k1[l], lam_q2[l], lam_k2[l],
                              diff_norm[l], lam_init, rope_bc, need_ctx)
        x = x + g1 * (jnp.concatenate([oa, ob, od], axis=-1) @ w_out[l])

        x = x + g2 * expert_choice_ffn(modulate(rmsnorm(x, norm2[l]), sh2, sc2),
                                       w_router[l], w_gate[l], w_up[l], w_down[l])
        if need_ctx:
            xc = xc + cg1 * (jnp.concatenate([oa_c, ob_c, od_c], axis=-1) @ w_out[l])
            xc = xc + cg2 * expert_choice_ffn(modulate(rmsnorm(xc, norm2[l]), csh2, csc2),
                                              w_router[l], w_gate[l], w_up[l], w_down[l])
    return rmsnorm(x, final_norm)


_drawn_inputs = setup_inputs


def setup_inputs(seed=0):
    import zlib

    import numpy as np

    out = dict(_drawn_inputs(seed))
    spreads = {}
    factors = {'norm1': 8.0,
     'norm2': 6.01,
     'sink': 8.0,
     'mla_q_norm': 8.0,
     'mla_kv_norm': 8.0,
     'lam_q1': 8.0,
     'lam_k1': 7.033,
     'lam_q2': 5.636,
     'lam_k2': 3.757,
     'diff_norm': 8.0,
     'final_norm': 2.85}
    for name, (base, spread) in spreads.items():
        noise = np.random.default_rng([zlib.crc32(name.encode()), seed]).standard_normal(out[name].shape)
        drawn = base * np.exp(spread * noise) if base else spread * noise
        out[name] = jnp.asarray(drawn.astype(out[name].dtype))
    for name, factor in factors.items():
        out[name] = (out[name] * factor).astype(out[name].dtype)
    return out
```

```python
from contextlib import ExitStack

import numpy as np

import concourse.bass as bass
from concourse import mybir

F32 = mybir.dt.float32
U32 = mybir.dt.uint32
ALU = mybir.AluOpType
ACT = mybir.ActivationFunctionType
AX_X = mybir.AxisListType.X

P = 128
D = 1024
KT = D // P
SEQ, CTX = 512, 256
TOK = SEQ + CTX
LT, CT = SEQ // P, CTX // P
NT = LT + CT
DEPTH = 2
EPS = 1e-6
NEG_INF = -1e30
GRID_W = 64
ROPE_BASE = 10000.0

A_HEADS, A_KV, HD = 8, 2, 64
B_HEADS, B_NOPE, B_ROPE, B_V, B_QR, B_KVR = 4, 64, 32, 64, 256, 128
B_QK = B_NOPE + B_ROPE
C_HEADS, C_DH, C_V = 4, 32, 64
IN_W = 1952
QA, KA, VA, CQ, CKV, KR, QD, KD, VD = 0, 512, 640, 768, 1024, 1152, 1184, 1440, 1696
IN_CHUNK = [(0, 512), (512, 1024), (1024, 1440), (1440, 1952)]
NCH = len(IN_CHUNK)

NE, FE = 16, 512
CAP_L, CAP_C = 2 * SEQ // NE, 2 * CTX // NE
NSLOT = 4
SLOT = KT * 512

N_ADA = 6 * D // 512
ADA_FIRST = 4

STEPS = [("A", h, 0) for h in range(A_HEADS)] + [("B", h, 0) for h in range(B_HEADS)]
STEPS += [("C", h, m) for h in range(C_HEADS) for m in range(2)]
NS = len(STEPS)
NI = A_HEADS + B_HEADS + C_HEADS
ITEM = [j if j < 12 else 12 + (j - 12) // 2 for j in range(NS)]
LASTSTEP = [j < 12 or j % 2 == 1 for j in range(NS)]
B_AQ, B_AK, B_CQ, B_CK, B_BQ, B_BK, NBLK = 0, 4, 5, 7, 9, 13, 17
OT_BLOCK = [0, 1, 2, 3, 5, 6, 9, 10]

K_ID, K_MASK, K_SEL, K_CA, K_SA, K_CB, K_SB = 0, 128, 384, 416, 672, 928, 1056
NCONST = 1184


def shape_constants():
    k = np.zeros((P, NCONST), np.float32)
    k[:, K_ID:K_ID + P] = np.eye(P)
    q, j = np.arange(P)[:, None], np.arange(P)[None, :]
    k[:, K_MASK:K_MASK + P] = np.where(j >= q, 0.0, NEG_INF)
    k[:, K_MASK + P:K_MASK + 2 * P] = np.where(j <= q, 0.0, NEG_INF)
    for g in range(4):
        for i in range(2):
            k[32 * g + i, K_SEL + i] = 1.0
    for c0, s0, rot in ((K_CA, K_SA, HD), (K_CB, K_SB, B_ROPE)):
        nf = rot // 4
        inv = (np.float32(ROPE_BASE) ** (-np.arange(nf, dtype=np.float32) / np.float32(nf))).astype(np.float32)
        for t in range(LT):
            tok = t * P + np.arange(P)
            for axis, pos in enumerate((tok // GRID_W, tok % GRID_W)):
                ang = pos[:, None].astype(np.float32) * inv
                cos, sin = np.cos(ang), np.sin(ang)
                o = t * rot + axis * 2 * nf
                k[:, c0 + o:c0 + o + 2 * nf] = np.concatenate([cos, cos], 1)
                k[:, s0 + o:s0 + o + 2 * nf] = np.concatenate([-sin, sin], 1)
    return k


def lam_init(l):
    return 0.8 - 0.6 * float(np.exp(-0.3 * l))


def nq(l):
    return NT if l < DEPTH - 1 else LT


def wait_in_loop(eng, regs, known, count, *waits):
    values = []
    for reg, (sem, value) in zip(regs, waits):
        if not isinstance(value, int):
            eng.reg_mov(reg, value)
            value = eng.snap(reg)
        values.append((sem, value))
    eng.wait_ge(known, count)
    for sem, value in values:
        eng.wait_ge(sem, value)


class Steps:

    def __init__(self, eng, sem):
        self.eng, self.sem, self.base, self.n = eng, sem, 0, 0

    def did(self, ins):
        ins.then_inc(self.sem, 1)
        self.n += 1
        self.eng.wait_ge(self.sem, self.base + self.n)


def key_tiles(l, qi, kind):
    if qi >= LT:
        lat = []
    elif kind == "A":
        lat = list(range(max(0, qi - 1), min(LT - 1, qi + 1) + 1))
    else:
        lat = list(range(LT))
    c0 = SEQ - P * len(lat)
    return [(t, c0 + P * n) for n, t in enumerate(lat)] + [(LT + c, SEQ + P * c) for c in range(CT)]


def ring_plan():
    plan = [("ada", 0, c) for c in range(ADA_FIRST)] + [("in", 0, c) for c in range(NCH)]
    plan += [("ada", 0, c) for c in range(ADA_FIRST, N_ADA)] + [("ada", 1, c) for c in range(N_ADA)]
    for l in range(DEPTH):
        if l:
            plan += [("in", l, c) for c in range(NCH)]
        plan += [("out", l, h) for h in range(2)]
        plan += [("g", l, 0), ("u", l, 0), ("g", l, 1), ("u", l, 1)]
        for e in range(2, NE):
            plan += [("d", l, e - 2), ("g", l, e), ("u", l, e)]
        plan += [("d", l, NE - 2), ("d", l, NE - 1)]
    return plan


def build(nc, x, c, ctx_in, c_ctx, norm1, norm2, w_ada, b_ada, w_in, sink, q_norm, w_uq, kv_norm, w_ukv,
          lam_q1, lam_k1, lam_q2, lam_k2, diff_norm, w_out, w_router, w_gate, w_up, w_down, final_norm,
          consts, out):
    es = ExitStack()

    def sb(name, n, dt=F32):
        return es.enter_context(nc.sbuf_tensor(name, [P, n], dt))

    def sem(name):
        return es.enter_context(nc.semaphore(name))

    x_s = nc.dram_tensor("x_s", (TOK, D), F32).ap()
    h2_s = nc.dram_tensor("h2_s", (TOK, D), F32).ap()
    mod_s = nc.dram_tensor("mod_s", (DEPTH, 2, 6 * D), F32).ap()

    ring = sb("ring", NSLOT * SLOT)
    qz = sb("qz", 2 * 16 * P)
    store = sb("store", NBLK * TOK + TOK + 2 * 2 * TOK)
    work = sb("work", 7744)
    xt = sb("xt", 2 * D)
    hx = sb("hx", D)
    kc = sb("kc", NCONST)
    wuq = sb("wuq", 2 * 384)
    wukv = sb("wukv", 512)
    wr = sb("wr", KT * NE)
    modrow = sb("modrow", 512)
    msum = sb("msum", 512)
    csil = sb("csil", KT * 32)
    ctmp = sb("ctmp", 3 * 16)
    modc = sb("modc", 4 * 2 * KT)
    ncol = sb("ncol", 2 * DEPTH * KT)
    gcol = sb("gcol", 2 + 1)
    dgain = sb("dgain", C_V)
    sinkb = sb("sinkb", 2 * DEPTH * A_HEADS)
    lamb = sb("lamb", 4 * C_DH + 8)
    half = sb("half", 8)
    st = sb("st", 160)
    gval = sb("gval", NE)
    gidx = sb("gidx", NE, U32)
    ix = sb("ix", 4, U32)

    ps = es.enter_context(nc.psum_tensor("ps", [P, 8, 512], F32))

    def bank(b, n=1):
        return ps[:, b:b + n, :].rearrange("p b n -> p (b n)")

    ident = kc[:, K_ID:K_ID + P]
    sel = kc[:, K_SEL:K_SEL + 32]

    def slot(r):
        o = (r % NSLOT) * SLOT
        return ring[:, o:o + SLOT]

    qk_t = store[:, 0:NBLK * TOK].rearrange("p (b t) -> p b t", b=NBLK)
    o = NBLK * TOK
    va = store[:, o:o + TOK].rearrange("p (t n) -> p t n", t=NT)
    vb = store[:, o + TOK:o + 3 * TOK].rearrange("p (t n) -> p t n", t=NT)
    vc = store[:, o + 3 * TOK:o + 5 * TOK].rearrange("p (t n) -> p t n", t=NT)
    xg = [store[:, n * D:(n + 1) * D] for n in range(2)]
    xg_t = [store[:, (2 + n) * D:(3 + n) * D].rearrange("p (k t) -> p k t", k=KT) for n in range(2)]
    y = [store[:, (4 + n) * D:(5 + n) * D] for n in range(2)]
    hid = [store[:, 6 * D + n * 512:6 * D + (n + 1) * 512] for n in range(2)]
    hid_t = [store[:, 7 * D + n * 512:7 * D + (n + 1) * 512].rearrange("p (k t) -> p k t", k=4) for n in range(2)]
    sg = store[:, 8 * D:8 * D + 512]
    g2 = store[:, 9 * D:10 * D]
    h_t = [work[:, n * D:(n + 1) * D].rearrange("p (k t) -> p k t", k=KT) for n in range(2)]
    pt = [work[:, 2048 + n * IN_W:2048 + (n + 1) * IN_W] for n in range(2)]
    o = 2048 + 2 * IN_W
    c_t = work[:, o:o + 384].rearrange("p (k t) -> p k t", k=3)
    q96 = work[:, o + 384:o + 768].rearrange("p (h d) -> p h d", h=B_HEADS)
    k96 = work[:, o + 768:o + 1152].rearrange("p (h d) -> p h d", h=B_HEADS)
    rtmp = work[:, o + 1152:o + 1152 + 640]
    prob = [work[:, n * TOK:(n + 1) * TOK] for n in range(3)]
    prob_t = [work[:, (3 + n) * TOK:(4 + n) * TOK].rearrange("p (b t) -> p b t", b=NT) for n in range(2)]
    ob = [work[:, 5 * TOK + n * D:5 * TOK + (n + 1) * D] for n in range(2)]
    csq = work[:, 5 * TOK + 2 * D:5 * TOK + 2 * D + 256]
    g1 = work[:, 0:2 * D].rearrange("p (i n) -> p i n", i=2)
    h2_t = work[:, 2 * D:3 * D].rearrange("p (k t) -> p k t", k=KT)
    aff = work[:, 3 * D:3 * D + NE]
    aff_e = work[:, 3 * D + 32:3 * D + 32 + NE]
    rtop = work[:, 3 * D + 64:3 * D + 64 + TOK]
    sval = work[:, 4 * D:4 * D + P]
    sidx_f = work[:, 4 * D + P:4 * D + 2 * P]
    sidx = work[:, 4 * D + 2 * P:4 * D + 3 * P].bitcast(U32)
    tmpo = work[:, 5 * D:5 * D + 512]
    fgain = work[:, 0:D]

    ss, msq, rstd = st[:, 0:2], st[:, 2:4], st[:, 4:6]
    ss2, ms2, rs2 = st[:, 6:8], st[:, 8:10], st[:, 10:12]
    mx, negm = st[:, 12:14], st[:, 14:34]
    sums, esink, rinv = st[:, 34:54], st[:, 54:62], st[:, 62:78]
    r1, cc, tot = st[:, 78:82], st[:, 82:86], st[:, 86:94]
    css, cms, crs = st[:, 94:98], st[:, 98:102], st[:, 102:106]
    rmx, rsum, rrec = st[:, 106:107], st[:, 107:108], st[:, 108:109]

    setup_in = sem("setup_in")
    ring_in = [sem(f"ring_in{n}") for n in range(NSLOT)]
    mod_init, mod_stored = sem("mod_init"), sem("mod_stored")
    modc_in, wproj_in = sem("modc_in"), sem("wproj_in")
    g1_in, g2_in = sem("g1_in"), sem("g2_in")
    x_in = [sem(f"x_in{n}") for n in range(2)]
    xo_in = [sem(f"xo_in{n}") for n in range(2)]
    xg_in = [sem(f"xg_in{n}") for n in range(2)]
    xs_stored, h2_stored, scattered, out_stored = (
        sem("xs_stored"), sem("h2_stored"), sem("scattered"), sem("out_stored"))
    pool_did, act_did, dve_did = sem("pool_did"), sem("act_did"), sem("dve_did")
    zeroed, csil_e, csil_done, cols_done = sem("zeroed"), sem("csil_e"), sem("csil_done"), sem("cols_done")
    lam_e, lam_p = sem("lam_e"), sem("lam_p")
    ada_mm, ada_row, ada_sum, ada_out = sem("ada_mm"), sem("ada_row"), sem("ada_sum"), sem("ada_out")
    modc_done = sem("modc_done")
    sumsq, ms_done, rstd_done, xhat, t1_mm, h_done = (
        sem("sumsq"), sem("ms_done"), sem("rstd_done"), sem("xhat"), sem("t1_mm"), sem("h_done"))
    main_mm, main_ev, sq2, ms2_done, rs2_done, cqn = (
        sem("main_mm"), sem("main_ev"), sem("sq2"), sem("ms2_done"), sem("rs2_done"), sem("cqn"))
    small_mm, small_ev, rope_ac, rope_b = sem("small_mm"), sem("small_ev"), sem("rope_ac"), sem("rope_b")
    qz_done, s_mm, neg_done, exp_done, sink_e, comb = (
        sem("qz_done"), sem("s_mm"), sem("neg_done"), sem("exp_done"), sem("sink_e"), sem("comb"))
    t_mm, pta_ev, ptd_ev, pv_mm, o_ev = sem("t_mm"), sem("pta_ev"), sem("ptd_ev"), sem("pv_mm"), sem("o_ev")
    cms_done, crs_done, on_done, ot_mm, ota_ev, otd_ev = (
        sem("cms_done"), sem("crs_done"), sem("on_done"), sem("ot_mm"), sem("ota_ev"), sem("otd_ev"))
    wo_mm, xo_done, lg_mm, rmax_done, rexp_done, aff_done, at_mm, at_ev = (
        sem("wo_mm"), sem("xo_done"), sem("lg_mm"), sem("rmax_done"), sem("rexp_done"), sem("aff_done"),
        sem("at_mm"), sem("at_ev"))
    top_done, gt_mm, gv_done, gi_done = sem("top_done"), sem("gt_mm"), sem("gv_done"), sem("gi_done")
    xgt_mm, xgt_ev, gate_mm, silu_done, up_mm, hid_done = (
        sem("xgt_mm"), sem("xgt_ev"), sem("gate_mm"), sem("silu_done"), sem("up_mm"), sem("hid_done"))
    hidt_mm, hidt_ev, down_mm, y_done, out_done = (
        sem("hidt_mm"), sem("hidt_ev"), sem("down_mm"), sem("y_done"), sem("out_done"))

    plan = ring_plan()
    place = {item: r for r, item in enumerate(plan)}
    ada_items = [it for it in plan if it[0] == "ada"]
    ada_no = {(it[1], it[2]): n for n, it in enumerate(ada_items)}

    def wait_slot(eng, item):
        r = place[item]
        eng.wait_ge(ring_in[r % NSLOT], 16 * (r // NSLOT + 1))

    def tile_no(l, t):
        return l * NT + t

    def step_no(l, qi, j):
        return (l * NT + qi) * NS + j

    def item_no(l, qi, i):
        return (l * NT + qi) * NI + i

    ATT = [(l, qi) for l in range(DEPTH) for qi in range(nq(l))]
    LOOP_E, BODY = 4, 4

    def ada_at(l, qi, j):
        n = (qi * NS + j) // 5
        if l == 0 and j % 5 == 4 and n < len(ada_items) - ADA_FIRST:
            return ADA_FIRST + n
        return None

    def ada_sum_at(l, qi, j):
        s = qi * NS + j - 2
        return ada_at(l, s // NS, s % NS) if s >= 0 else None

    with nc.Block() as block:

        @block.sync
        def _(sp):
            def source(item):
                kind, l, n = item
                if kind == "ada":
                    return w_ada[l].rearrange("(p k) n -> p k n", k=KT)[:, :, 512 * n:512 * n + 512], 512
                if kind == "in":
                    a, b = IN_CHUNK[n]
                    return w_in[l].rearrange("(p k) n -> p k n", k=KT)[:, :, a:b], b - a
                if kind == "out":
                    return w_out[l].rearrange("(p k) n -> p k n", k=KT)[:, :, 512 * n:512 * n + 512], 512

            def freed(item):
                kind, l, n = item
                if kind == "ada":
                    sp.wait_ge(ada_mm, ada_no[(l, n)] + 1)
                elif kind == "in":
                    sp.wait_ge(main_mm, NCH * tile_no(l, NT - 1) + n + 1)
                elif kind == "out":
                    sp.wait_ge(wo_mm, 2 * tile_no(l, nq(l) - 1) + n + 1)
                else:
                    sp.wait_ge({"g": gate_mm, "u": up_mm, "d": down_mm}[kind], l * NE + n + 1)

            def expert_weights(kind, l, e):
                if kind == "d":
                    return w_down[l, e].rearrange("(p k) n -> p (k n)", k=4)
                return (w_gate if kind == "g" else w_up)[l, e].rearrange("(p k) n -> p (k n)", k=KT)

            def load(r):
                if r >= NSLOT:
                    freed(plan[r - NSLOT])
                kind, l, n = plan[r]
                if kind in "gud":
                    sp.dma_start(slot(r), expert_weights(kind, l, n)).then_inc(ring_in[r % NSLOT], 16)
                else:
                    src, width = source(plan[r])
                    dst = slot(r)[:, 0:KT * width].rearrange("p (k n) -> p k n", k=KT)
                    sp.dma_start(dst, src).then_inc(ring_in[r % NSLOT], 16)

            r = 0
            for l in range(DEPTH):
                first = place[("d", l, LOOP_E - 2)]
                while r < first:
                    load(r)
                    r += 1
                with sp.Fori(0, (NE - LOOP_E) // BODY) as it:
                    for b in range(BODY):
                        e = BODY * it + (LOOP_E + b)
                        for n, (kind, src, back, seen) in enumerate((
                                ("d", -2, up_mm, -1),
                                ("g", 0, down_mm, -2),
                                ("u", 0, gate_mm, 0))):
                            q = r + 3 * b + n
                            sp.wait_ge(back, e + (l * NE + seen))
                            w = {"d": w_down, "g": w_gate, "u": w_up}[kind][l, bass.ds(e + src, 1)]
                            k = 4 if kind == "d" else KT
                            sp.dma_start(slot(q), w.rearrange("e (p k) n -> (e p) (k n)", k=k)
                                         ).then_inc(ring_in[q % NSLOT], 16)
                r += 3 * (NE - LOOP_E)
                load(r)
                load(r + 1)
                r += 2

        @block.gpsimd
        def _(pool):
            own = Steps(pool, pool_did)
            counts = [pool.alloc_register(f"pool_count{n}") for n in range(2)]

            def power(dst, src, n):
                return pool.tensor_tensor(dst, src, half[:, 0:n], ALU.pow)

            pool.memset(half[:], -0.5).then_inc(zeroed, 1)
            pool.memset(csil[:], 0.0).then_inc(zeroed, 1)
            pool.memset(qz[:], 0.0).then_inc(zeroed, 1)
            col = "(p k) -> p k"
            cv = ctmp[:, 0:2 * KT].rearrange("p (k i) -> p k i", i=2)
            with nc.allow_non_contiguous_dma(reason="a few columns"):
                pool.dma_start(cv[:, :, 0], c[0].rearrange(col, k=KT)).then_inc(setup_in, 16)
                pool.dma_start(cv[:, :, 1], c_ctx.rearrange(col, k=KT)).then_inc(setup_in, 16)
            for i in range(2):
                for l in range(DEPTH):
                    pool.dma_start(mod_s[l, i:i + 1, :], b_ada[l:l + 1, :]).then_inc(mod_init, 16)
            pool.dma_start(kc[:], consts[:, :]).then_inc(setup_in, 16)
            for i, w in enumerate((norm1, norm2)):
                for l in range(DEPTH):
                    pool.dma_start(ncol[:, (2 * i + l) * KT:(2 * i + l + 1) * KT],
                                   w[l].rearrange(col, k=KT)).then_inc(setup_in, 16)
            pool.dma_start(sinkb[:, 0:DEPTH * A_HEADS],
                           sink.rearrange("l h -> (l h)").partition_broadcast(P)).then_inc(setup_in, 16)

            def projection_weights(l):
                with nc.allow_non_contiguous_dma(reason="a few columns"):
                    pool.dma_start(wuq[:].rearrange("p (k n) -> p k n", k=2),
                                   w_uq[l].rearrange("(p k) n -> p k n", k=2)).then_inc(wproj_in, 16)
                    pool.dma_start(wukv[:], w_ukv[l]).then_inc(wproj_in, 16)
                    pool.dma_start(gcol[:, 0:2], q_norm[l].rearrange(col, k=2)).then_inc(wproj_in, 16)
                    pool.dma_start(gcol[:, 2:3], kv_norm[l].rearrange(col, k=1)).then_inc(wproj_in, 16)
                    pool.dma_start(dgain[:], diff_norm[l].partition_broadcast(P)).then_inc(wproj_in, 16)
                    for n, v in enumerate((lam_q1, lam_k1, lam_q2, lam_k2)):
                        pool.dma_start(lamb[:, n * C_DH:(n + 1) * C_DH],
                                       v[l].partition_broadcast(P)).then_inc(wproj_in, 16)

            def modulation_columns(l, part):
                for n in range(2):
                    for i in range(2):
                        m = 3 * part + n
                        pool.dma_start(modc[:, ((2 * part + n) * 2 + i) * KT:((2 * part + n) * 2 + i + 1) * KT],
                                       mod_s[l, i, m * D:(m + 1) * D].rearrange(col, k=KT)).then_inc(modc_in, 16)

            def store_modulation(n):
                l, ch = ada_items[n][1:]
                pool.wait_ge(ada_out, n + 1)
                if n == 0:
                    pool.wait_ge(mod_init, 64)
                pool.dma_start(mod_s[l, :, 512 * ch:512 * ch + 512], msum[0:2, :],
                               accum_op=ALU.add).then_inc(mod_stored, 16)

            def norm_power(n):
                pool.wait_ge(ms_done, n + 1)
                power(rstd[:, n % 2:n % 2 + 1], msq[:, n % 2:n % 2 + 1], 1).then_inc(rstd_done, 1)

            def tile_rows(l, t):
                if l:
                    return x_s[t * P:(t + 1) * P, :]
                return x[0, t * P:(t + 1) * P, :] if t < LT else ctx_in[0, (t - LT) * P:(t - LT + 1) * P, :]

            norms = 0
            projection_weights(0)
            for l in range(DEPTH):
                if l == 0:
                    for n in range(ADA_FIRST):
                        store_modulation(n)
                    pool.wait_ge(mod_stored, 16 * ADA_FIRST)
                else:
                    pool.wait_ge(o_ev, item_no(0, NT - 1, NI - 1) + 1)
                    projection_weights(l)
                modulation_columns(l, 0)
                for t in range(NT + 1):
                    if t < NT:
                        if l and t == 0:
                            pool.wait_ge(scattered, 16 * NE)
                        if norms + t >= 2:
                            pool.wait_ge(xhat, norms + t - 1)
                        pool.dma_start(xt[:, (t % 2) * D:(t % 2 + 1) * D], tile_rows(l, t)).then_inc(x_in[t % 2], 16)
                        norm_power(norms + t)
                    if t >= 1:
                        n = tile_no(l, t - 1)
                        pool.wait_ge(ms2_done, n + 1)
                        power(rs2, ms2, 2).then_inc(rs2_done, 1)
                norms += NT

                pool.wait_ge(zeroed, 3)
                pool.wait_ge(small_ev, 8 * tile_no(l, NT - 1) + 8)
                def pad_queries(qi):
                    g = ATT.index((l, qi))
                    if g >= 2:
                        pl, pq = ATT[g - 2]
                        pool.wait_ge(s_mm, step_no(pl, pq, NS - 1) + 1)
                    z = qz[:, (g % 2) * 16 * P:(g % 2 + 1) * 16 * P].rearrange("p (h t) -> p h t", h=16)
                    cols = slice(qi * P, (qi + 1) * P)
                    for k in range(2):
                        own.did(pool.tensor_copy(z[64 * k:64 * k + 64, 4 * k:4 * k + 4, :],
                                                 qk_t[64 * k:64 * k + 64, B_AQ:B_AQ + 4, cols]))
                    for r in range(4):
                        last = pool.tensor_copy(z[32 * r:32 * r + 32, 8 + r:16:4, :],
                                                qk_t[32 * r:32 * r + 32, B_CQ:B_CQ + 2, cols])
                        if r < 3:
                            own.did(last)
                    last.then_inc(qz_done, 1)

                pad_queries(0)
                for qi in range(nq(l)):
                    g = ATT.index((l, qi))
                    if qi + 1 < nq(l):
                        pad_queries(qi + 1)
                    for j in range(NS):
                        n = ada_sum_at(l, qi, j)
                        if n is not None:
                            store_modulation(n)
                    pool.wait_ge(cms_done, g + 1)
                    power(crs, cms, 4).then_inc(crs_done, 1)

                pool.wait_ge(mod_stored, 16 * len(ada_items))
                modulation_columns(l, 1)
                pool.wait_ge(otd_ev, len([a for a in ATT if a[0] <= l]))
                pool.wait_ge(ota_ev, len([a for a in ATT if a[0] <= l]))
                for i in range(2):
                    pool.dma_start(g1[:, i, :], mod_s[l, i, 2 * D:3 * D].partition_broadcast(P)).then_inc(g1_in, 16)
                pool.dma_start(wr[:].rearrange("p (k n) -> p k n", k=KT),
                               w_router[l].rearrange("(p k) n -> p k n", k=KT)).then_inc(g1_in, 16)
                for t in range(nq(l) + 1):
                    g = tile_no(l, t)
                    if t < nq(l):
                        pool.wait_ge(xhat, norms + max(0, t - 1))
                        if t >= 2:
                            pool.wait_ge(xs_stored, 16 * (g - 1))
                        pool.dma_start(xt[:, (t % 2) * D:(t % 2 + 1) * D], tile_rows(l, t)).then_inc(xo_in[t % 2], 16)
                    if t >= 1:
                        g = tile_no(l, t - 1)
                        b = (t - 1) % 2
                        pool.wait_ge(xo_done, g + 1)
                        pool.dma_start(x_s[(t - 1) * P:t * P, :], xt[:, b * D:(b + 1) * D]).then_inc(xs_stored, 16)
                        norm_power(norms + t - 1)
                        pool.wait_ge(xhat, norms + t)
                        pool.dma_start(h2_s[(t - 1) * P:t * P, :], hx[:]).then_inc(h2_stored, 16)
                norms += nq(l)

                pool.wait_ge(wo_mm, 2 * tile_no(l, nq(l) - 1) + 2)
                pool.dma_start(g2[0:CAP_L, :], mod_s[l, 0, 5 * D:6 * D].partition_broadcast(CAP_L)).then_inc(g2_in, 16)
                pool.dma_start(g2[CAP_L:CAP_L + CAP_C, :],
                               mod_s[l, 1, 5 * D:6 * D].partition_broadcast(CAP_C)).then_inc(g2_in, 16)
                pool.wait_ge(h2_stored, 16 * (tile_no(l, nq(l) - 1) + 1))
                pool.wait_ge(xs_stored, 16 * (tile_no(l, nq(l) - 1) + 1))
                pool.wait_ge(gi_done, l + 1)
                rows = CAP_L + (CAP_C if nq(l) > LT else 0)

                def step(e, n, bidx, first):
                    if bidx < NE:
                        if not (l == 0 and first and bidx < 2):
                            pool.wait_ge(xgt_mm, n - 1)
                        if not (l == 0 and first and bidx < 4):
                            pool.wait_ge(scattered, (n - 3) * 16)
                        ic = ix[0:rows, bidx % 4:bidx % 4 + 1]
                        ins = pool.tensor_copy(ic, gidx[0:rows, bass.ds(e, 1)])
                        ins.then_inc(pool_did, 1)
                        own.n += 1
                        wait_in_loop(pool, counts, gi_done, l + 1, (pool_did, own.base + own.n))
                        pool.indirect_dma_start(
                            out=xg[bidx % 2][0:rows, :], out_offset=None, in_=h2_s[:, :],
                            in_offset=bass.IndirectOffsetOnAxis(ap=ic, axis=0)).then_inc(xg_in[bidx % 2], 16)
                    if not first or bidx >= 3:
                        before = [] if l == 0 and first and bidx == 3 else [(scattered, (n - 3) * 16)]
                        wait_in_loop(pool, counts, gi_done, l + 1, (y_done, n - 2), *before)
                        pool.indirect_dma_start(
                            out=x_s[:, :],
                            out_offset=bass.IndirectOffsetOnAxis(
                                ap=ix[0:rows, (bidx - 3) % 4:(bidx - 3) % 4 + 1], axis=0),
                            in_=y[(bidx - 3) % 2][0:rows, :], in_offset=None, compute_op=ALU.add
                        ).then_inc(scattered, 16)

                for e in range(LOOP_E):
                    step(e, l * NE + e, e, True)
                start = own.n
                with pool.Fori(0, (NE - LOOP_E) // BODY) as it:
                    own.base = it * BODY
                    for b in range(BODY):
                        e = BODY * it + (LOOP_E + b)
                        step(e, e + l * NE, LOOP_E + b, False)
                own.base, own.n = 0, start + NE - LOOP_E
                for e in range(NE, NE + 3):
                    step(e, l * NE + e, e, False)

            pool.wait_ge(at_ev, tile_no(DEPTH - 1, LT - 1) + 1)
            pool.wait_ge(gt_mm, DEPTH)
            pool.dma_start(fgain, final_norm.partition_broadcast(P)).then_inc(g1_in, 16)
            pool.wait_ge(scattered, 16 * NE * DEPTH)
            for t in range(LT + 1):
                if t < LT:
                    if t >= 2:
                        pool.wait_ge(out_stored, 16 * (t - 1))
                    pool.dma_start(xt[:, (t % 2) * D:(t % 2 + 1) * D], x_s[t * P:(t + 1) * P, :]
                                   ).then_inc(x_in[t % 2], 16)
                    norm_power(norms + t)
                if t >= 1:
                    b = (t - 1) % 2
                    pool.wait_ge(out_done, t)
                    pool.dma_start(out[0, (t - 1) * P:t * P, :], xt[:, b * D:(b + 1) * D]).then_inc(out_stored, 16)
            pool.wait_ge(out_stored, 16 * LT)

        @block.scalar
        def _(act):
            own = Steps(act, act_did)

            act.wait_ge(setup_in, 16 * 8)
            act.activation(ctmp[:, 16:32], ctmp[:, 0:16], ACT.Exp, scale=-1.0).then_inc(csil_e, 1)

            def row_sum(n, buf, sem_in, value):
                act.wait_ge(sem_in, value)
                if n >= 1:
                    act.wait_ge(t1_mm if False else sumsq, n)
                act.activation(hx_junk(n), xt[:, buf * D:(buf + 1) * D], ACT.Square,
                               accum_out=ss[:, n % 2:n % 2 + 1]).then_inc(sumsq, 1)

            def hx_junk(n):
                return junk_bank[0]

            junk_bank = [None]

            def ada_evacuate(n):
                act.wait_ge(ada_sum, n + 1)
                if n >= 1:
                    act.wait_ge(mod_stored, 16 * n)
                act.copy(msum[0:2, :], ps[0:2, 7, :]).then_inc(ada_out, 1)

            for n in range(ADA_FIRST):
                ada_evacuate(n)

            def lambda_exps(l):
                act.wait_ge(lam_p, l + 1)
                act.activation(lamb[:, 4 * C_DH + 2:4 * C_DH + 4], lamb[:, 4 * C_DH:4 * C_DH + 2],
                               ACT.Exp).then_inc(lam_e, 1)

            norms = 0
            for l in range(DEPTH):
                lambda_exps(l)
                def square(t):
                    act.wait_ge(x_in[t % 2], 16 * (l * NT // 2 + t // 2 + 1))
                    if norms + t >= 2:
                        act.wait_ge(ms_done, norms + t - 1)
                    if norms + t >= 1:
                        act.wait_ge(xhat, norms + t)
                        act.wait_ge(t1_mm, norms + t)
                    if l and t == 0:
                        act.wait_ge(h2_stored, 16 * tile_no(0, NT))
                    act.activation(hx[:], xt[:, (t % 2) * D:(t % 2 + 1) * D], ACT.Square,
                                   accum_out=ss[:, (norms + t) % 2:(norms + t) % 2 + 1]).then_inc(sumsq, 1)

                def main_evacuate(t, ch):
                    n = tile_no(l, t)
                    p = pt[n % 2]
                    act.wait_ge(main_mm, NCH * n + ch + 1)
                    if ch == 0 and n >= 2:
                        act.wait_ge(small_mm, 8 * (n - 1))
                    if ch == 0 and l and t < 2:
                        act.wait_ge(gt_mm, l)
                    if l and t == 0 and ch == 1:
                        act.wait_ge(down_mm, l * NE)
                        act.wait_ge(scattered, 16 * NE * l)
                    src = ps[:, ch, :]
                    if ch == 0:
                        last = act.copy(p[:, QA:KA].rearrange("p (h k d) -> p k h d", k=2, d=HD),
                                        src.rearrange("p (k h d) -> p k h d", k=2, d=HD))
                    elif ch == 1:
                        act.copy(p[:, KA:VA], src[:, 0:VA - 512])
                        act.copy(va[:, t, :], src[:, VA - 512:CQ - 512])
                        last = act.copy(p[:, CQ:CKV], src[:, CQ - 512:512])
                    elif ch == 2:
                        last = act.copy(p[:, CKV:KD], src[:, 0:KD - CKV])
                    else:
                        act.copy(p[:, KD:VD], src[:, 0:VD - KD])
                        last = act.copy(vc[:, t, :], src[:, VD - KD:512])
                    last.then_inc(main_ev, 1)

                def squares2(t):
                    n = tile_no(l, t)
                    p = pt[n % 2]
                    act.wait_ge(main_ev, NCH * n + 4)
                    if n >= 1:
                        act.wait_ge(ms2_done, n)
                        act.wait_ge(sq2, 2 * n)
                        act.wait_ge(rope_b, n - 1) if n >= 2 else None
                    act.activation(ps[:, 3, 0:256], p[:, CQ:CKV], ACT.Square,
                                   accum_out=ss2[:, 0:1]).then_inc(sq2, 1)
                    act.activation(ps[:, 3, 256:384], p[:, CKV:KR], ACT.Square,
                                   accum_out=ss2[:, 1:2]).then_inc(sq2, 1)

                def small_evacuate(t, u):
                    n = tile_no(l, t)
                    act.wait_ge(small_mm, 8 * n + u + 1)
                    src = ps[:, 6 + u % 2, :]
                    cols = slice(t * P, (t + 1) * P)
                    if u == 0:
                        if t == 0:
                            act.wait_ge(wproj_in, 16 * 9 * (l + 1))
                        if n >= 1:
                            act.wait_ge(small_mm, 8 * (n - 1) + 3)
                        for k in range(3):
                            last = act.activation(c_t[:, k, :], src[:, k * P:(k + 1) * P], ACT.Identity,
                                                  scale=gcol[:, k:k + 1])
                    elif u == 1:
                        if n >= 1:
                            act.wait_ge(small_mm, 8 * n)
                        last = act.copy(q96, src[:, 0:384].rearrange("p (h d) -> p h d", h=B_HEADS))
                    elif u == 2:
                        kv = src.rearrange("p (h d) -> p h d", h=B_HEADS)
                        act.copy(k96[:, :, 0:B_NOPE], kv[:, :, 0:B_NOPE])
                        last = act.copy(vb[:, t, :].rearrange("p (h d) -> p h d", h=B_HEADS), kv[:, :, B_NOPE:])
                    else:
                        b0, nb, rows = [(0, 4, P), (4, 4, P), (8, 1, P), (9, 4, B_QK), (13, 4, B_QK)][u - 3]
                        last = act.copy(qk_t[0:rows, b0:b0 + nb, cols],
                                        src[0:rows, 0:nb * P].rearrange("p (b t) -> p b t", b=nb))
                    last.then_inc(small_ev, 1)

                square(0)
                for t in range(NT + 1):
                    if t + 1 < NT:
                        square(t + 1)
                    for ch in range(NCH):
                        if t < NT:
                            main_evacuate(t, ch)
                        if t >= 1:
                            if ch == 0:
                                small_evacuate(t - 1, 0)
                            elif ch == 1:
                                small_evacuate(t - 1, 1)
                                small_evacuate(t - 1, 2)
                            elif ch == 2:
                                for u in range(3, 8):
                                    small_evacuate(t - 1, u)
                        if t < NT and ch == 3:
                            squares2(t)
                norms += NT

                def softmax(s):
                    ll, qi, j = s
                    n = step_no(ll, qi, j)
                    kind, h, m = STEPS[j]
                    kt = key_tiles(ll, qi, kind)
                    c0, c1 = kt[0][1], TOK
                    scale = {"A": HD, "B": B_QK, "C": C_DH}[kind] ** -0.5
                    act.wait_ge(neg_done, n + 1)
                    if n >= 3:
                        pl, pq, pj = sprev(s, 3)
                        act.wait_ge(t_mm, item_no(pl, pq, ITEM[pj]) + 1)
                    act.activation(prob[n % 3][:, c0:c1], bank(2 * (n % 2), 2)[:, c0:c1], ACT.Exp,
                                   bias=negm[:, j:j + 1], scale=scale,
                                   accum_out=sums[:, j:j + 1]).then_inc(exp_done, 1)
                    if kind == "A":
                        act.activation(esink[:, h:h + 1], sinkb[:, ll * A_HEADS + h:ll * A_HEADS + h + 1], ACT.Exp,
                                       bias=negm[:, j:j + 1]).then_inc(sink_e, 1)

                seq = [(l, qi, j) for qi in range(nq(l)) for j in range(NS)]

                def sprev(s, k):
                    full = [(a, b, jj) for a, b in ATT for jj in range(NS)]
                    return full[full.index(s) - k]

                softmax(seq[0])
                softmax(seq[1])
                for k, s in enumerate(seq):
                    _, qi, j = s
                    kind = STEPS[j][0]
                    if LASTSTEP[j]:
                        i = item_no(l, qi, ITEM[j])
                        kt = key_tiles(l, qi, kind)
                        nb = len(kt) // 2
                        act.wait_ge(t_mm, i + 1)
                        if i >= 2:
                            act.wait_ge(pv_mm, i - 1)
                        act.copy(prob_t[i % 2][:, 0:nb, :],
                                 bank(4)[:, 0:nb * P].rearrange("p (b t) -> p b t", b=nb)).then_inc(pta_ev, 1)
                    if k + 2 < len(seq):
                        softmax(seq[k + 2])
                    n = ada_sum_at(l, qi, j)
                    if n is not None:
                        ada_evacuate(n)
                    if j == NS - 1:
                        g = ATT.index((l, qi))
                        act.wait_ge(ot_mm, g + 1)
                        for b in range(4):
                            last = act.copy(qk_t[:, OT_BLOCK[b], qi * P:(qi + 1) * P], bank(4, 2)[:, b * P:(b + 1) * P])
                        last.then_inc(ota_ev, 1)

                def square_o(t):
                    n = norms + t
                    act.wait_ge(xo_done, tile_no(l, t) + 1)
                    act.wait_ge(ms_done, n - 1)
                    act.wait_ge(t1_mm, n)
                    if t:
                        act.wait_ge(h2_stored, 16 * tile_no(l, t))
                    act.activation(hx[:], xt[:, (t % 2) * D:(t % 2 + 1) * D], ACT.Square,
                                   accum_out=ss[:, n % 2:n % 2 + 1]).then_inc(sumsq, 1)

                def router_exp(t):
                    act.wait_ge(rmax_done, tile_no(l, t) + 1)
                    act.activation(aff_e, ps[:, 6, 0:NE], ACT.Exp, bias=rmx, accum_out=rsum).then_inc(rexp_done, 1)

                def affinity_store(t):
                    g = tile_no(l, t)
                    act.wait_ge(at_mm, g + 1)
                    act.copy(rtop[0:NE, t * P:(t + 1) * P], ps[0:NE, 7, 0:P]).then_inc(at_ev, 1)

                for t in range(nq(l)):
                    square_o(t)
                    router_exp(t)
                    affinity_store(t)
                norms += nq(l)
                rows = CAP_L + (CAP_C if nq(l) > LT else 0)
                act.wait_ge(gt_mm, l + 1)
                if l:
                    act.wait_ge(y_done, NE)
                act.copy(gval[0:rows, :], ps[0:rows, 6, 0:NE]).then_inc(gv_done, 1)

                def step(n, b, first):
                    if b < NE:
                        act.wait_ge(gate_mm, n + 1)
                        if not (l == 0 and first and b == 0):
                            act.wait_ge(hid_done, n)
                        act.activation(sg[0:rows, :], ps[0:rows, 2, :], ACT.Silu).then_inc(silu_done, 1)
                    if not first or b >= 1:
                        act.wait_ge(hidt_mm, n)
                        if not (l == 0 and first and b < 3):
                            act.wait_ge(down_mm, n - 2)
                        act.copy(hid_t[(b - 1) % 2][:, :, 0:rows],
                                 ps[:, 4, 0:4 * rows].rearrange("p (k t) -> p k t", k=4)).then_inc(hidt_ev, 1)

                for e in range(LOOP_E):
                    step(l * NE + e, e, True)
                with act.Fori(0, (NE - LOOP_E) // BODY) as it:
                    for b in range(BODY):
                        step(BODY * it + (l * NE + LOOP_E + b), LOOP_E + b, False)
                step(l * NE + NE, NE, False)

            for t in range(LT):
                n = norms + t
                act.wait_ge(x_in[t % 2], 16 * (DEPTH * NT // 2 + t // 2 + 1))
                act.wait_ge(ms_done, n - 1)
                act.wait_ge(xhat, n) if t == 0 else None
                act.wait_ge(t1_mm, norms) if t == 0 else None
                act.wait_ge(h2_stored, 16 * (tile_no(DEPTH - 1, LT - 1) + 1))
                if t:
                    act.wait_ge(sumsq, n)
                act.activation(hx[:], xt[:, (t % 2) * D:(t % 2 + 1) * D], ACT.Square,
                               accum_out=ss[:, n % 2:n % 2 + 1]).then_inc(sumsq, 1)

        @block.vector
        def _(dve):
            own = Steps(dve, dve_did)

            dve.wait_ge(csil_e, 1)
            own.did(dve.tensor_scalar(ctmp[:, 16:32], ctmp[:, 16:32], 1.0, None, ALU.add))
            own.did(dve.reciprocal(ctmp[:, 32:48], ctmp[:, 16:32]))
            dve.wait_ge(zeroed, 2)
            dve.tensor_tensor(csil[:].rearrange("p (k i) -> p k i", k=KT)[:, :, 0:2],
                              ctmp[:, 0:16].rearrange("p (k i) -> p k i", i=2),
                              ctmp[:, 32:48].rearrange("p (k i) -> p k i", i=2), ALU.mult).then_inc(csil_done, 1)
            NSK = DEPTH * A_HEADS
            dve.tensor_scalar(sinkb[:, NSK:2 * NSK], sinkb[:, 0:NSK], -1.0, None, ALU.mult).then_inc(cols_done, 1)

            def ada_copy(n):
                dve.wait_ge(ada_mm, n + 1)
                if n >= 1:
                    dve.wait_ge(ada_sum, n)
                dve.tensor_copy(modrow[:], ps[:, 7, :]).then_inc(ada_row, 1)

            for n in range(ADA_FIRST):
                ada_copy(n)

            def lambda_products(l):
                dve.wait_ge(wproj_in, 16 * 9 * (l + 1))
                q = lamb[:, 0:4 * C_DH].rearrange("p (n d) -> p n d", n=4)
                s = lamb[:, 4 * C_DH:]
                own.did(dve.tensor_tensor(q[:, 0:4:2, :], q[:, 0:4:2, :], q[:, 1:4:2, :], ALU.mult))
                dve.tensor_reduce(s[:, 0:2], q[:, 0:4:2, :], AX_X, ALU.add).then_inc(lam_p, 1)
                dve.wait_ge(lam_e, l + 1)
                own.did(dve.tensor_tensor(s[:, 4:5], s[:, 3:4], s[:, 2:3], ALU.subtract))
                own.did(dve.tensor_scalar(s[:, 5:6], s[:, 4:5], -lam_init(l), None, ALU.add))
                own.did(dve.tensor_scalar(dgain[:], dgain[:], 1.0 - lam_init(l), None, ALU.mult))

            neg_lam = lamb[:, 4 * C_DH + 5:4 * C_DH + 6]
            mc = modc[:].rearrange("p (v i k) -> p v i k", v=4, i=2)

            def modulation(l, part):
                dve.wait_ge(modc_in, 16 * 4 * (2 * l + part + 1))
                gain = ncol[:, (2 * part + l) * KT:(2 * part + l + 1) * KT].unsqueeze(1).to_broadcast([P, 2, KT])
                dve.scalar_tensor_tensor(out=mc[:, 2 * part + 1], in0=mc[:, 2 * part + 1], scalar=1.0, in1=gain,
                                         op0=ALU.add, op1=ALU.mult).then_inc(modc_done, 1)
                dve.wait_ge(modc_done, 2 * l + part + 1)

            def mean_square(n):
                dve.wait_ge(sumsq, n + 1)
                if n >= 2:
                    dve.wait_ge(rstd_done, n - 1)
                dve.tensor_scalar(msq[:, n % 2:n % 2 + 1], ss[:, n % 2:n % 2 + 1], 1.0 / D, EPS,
                                  ALU.mult, ALU.add).then_inc(ms_done, 1)

            def normalise(n, buf, dst):
                dve.wait_ge(rstd_done, n + 1)
                return dve.tensor_scalar(dst, xt[:, buf * D:(buf + 1) * D], rstd[:, n % 2:n % 2 + 1], None, ALU.mult)

            def modulate(dst, src, part, i, width):
                a = mc[:, 2 * part + 1, i, :].unsqueeze(2).to_broadcast([P, KT, width])
                b = mc[:, 2 * part, i, :].unsqueeze(2).to_broadcast([P, KT, width])
                own.did(dve.tensor_tensor(dst, src, a, ALU.mult))
                return dve.tensor_tensor(dst, dst, b, ALU.add)

            def rope(v, units, nf, cos, sin):
                w = 4 * nf
                vv = v.rearrange("p (u w) -> p u w", w=w)
                v4 = v.rearrange("p (u a r f) -> p u a r f", a=2, r=2, f=nf)
                tm = rtmp[:, 0:units * w].rearrange("p (u a r f) -> p u a r f", a=2, r=2, f=nf)
                s4 = sin.rearrange("p (a r f) -> p a r f", a=2, r=2)
                for r in range(2):
                    own.did(dve.tensor_tensor(tm[:, :, :, r, :], v4[:, :, :, 1 - r, :],
                                              s4[:, :, r, :].unsqueeze(1).to_broadcast([P, units, 2, nf]), ALU.mult))
                own.did(dve.tensor_tensor(vv, vv, cos.unsqueeze(1).to_broadcast([P, units, w]), ALU.mult))
                return dve.tensor_tensor(v, v, rtmp[:, 0:units * w], ALU.add)

            norms = 0
            for l in range(DEPTH):
                lambda_products(l)
                modulation(l, 0)

                def prepare(t):
                    n = norms + t
                    mean_square(n)
                    if n >= 1:
                        dve.wait_ge(t1_mm, n)
                    if l and t == 0:
                        dve.wait_ge(h2_stored, 16 * tile_no(0, NT))
                    normalise(n, t % 2, hx[:]).then_inc(xhat, 1)

                def modulated(t):
                    n = tile_no(l, t)
                    dve.wait_ge(t1_mm, norms + t + 1)
                    if n >= 2:
                        dve.wait_ge(main_mm, NCH * (n - 1))
                    if l and t < 2:
                        dve.wait_ge(gt_mm, l)
                    modulate(h_t[n % 2], bank(4, 2).rearrange("p (k t) -> p k t", k=KT), 0, int(t >= LT),
                             P).then_inc(h_done, 1)

                def finish_b(t):
                    n = tile_no(l, t)
                    p = pt[n % 2]
                    dve.wait_ge(small_ev, 8 * n + 3)
                    if t < LT:
                        tm = rtmp[:, 0:B_HEADS * B_ROPE].rearrange("p (h a r f) -> p h a r f", a=2, r=2, f=8)
                        cos = kc[:, K_CB + t * 32:K_CB + t * 32 + 32]
                        sin = kc[:, K_SB + t * 32:K_SB + t * 32 + 32].rearrange("p (a r f) -> p a r f", a=2, r=2)
                        qr = q96[:, :, B_NOPE:]
                        q5 = qr.rearrange("p h (a r f) -> p h a r f", a=2, r=2)
                        for r in range(2):
                            own.did(dve.tensor_tensor(
                                tm[:, :, :, r, :], q5[:, :, :, 1 - r, :],
                                sin[:, :, r, :].unsqueeze(1).to_broadcast([P, B_HEADS, 2, 8]), ALU.mult))
                        own.did(dve.tensor_tensor(qr, qr, cos.unsqueeze(1).to_broadcast([P, B_HEADS, 32]), ALU.mult))
                        own.did(dve.tensor_tensor(
                            qr, qr, rtmp[:, 0:B_HEADS * B_ROPE].rearrange("p (h d) -> p h d", h=B_HEADS), ALU.add))
                    dve.tensor_copy(k96[:, :, B_NOPE:], p[:, KR:QD].unsqueeze(1).to_broadcast([P, B_HEADS, B_ROPE])
                                    ).then_inc(rope_b, 1)

                def finish_main(t):
                    n = tile_no(l, t)
                    p = pt[n % 2]
                    dve.wait_ge(sq2, 2 * n + 2)
                    if n >= 1:
                        dve.wait_ge(rs2_done, n)
                    own.did(dve.tensor_scalar(ms2[:, 0:1], ss2[:, 0:1], 1.0 / B_QR, EPS, ALU.mult, ALU.add))
                    dve.tensor_scalar(ms2[:, 1:2], ss2[:, 1:2], 1.0 / B_KVR, EPS, ALU.mult, ALU.add
                                      ).then_inc(ms2_done, 1)
                    dve.wait_ge(rs2_done, n + 1)
                    dve.tensor_scalar(p[:, CQ:CKV], p[:, CQ:CKV], rs2[:, 0:1], None, ALU.mult)
                    dve.tensor_scalar(p[:, CKV:KR], p[:, CKV:KR], rs2[:, 1:2], None, ALU.mult).then_inc(cqn, 1)
                    if t < LT:
                        own.did(rope(p[:, QA:VA], A_HEADS + A_KV, 16, kc[:, K_CA + t * 64:K_CA + t * 64 + 64],
                                     kc[:, K_SA + t * 64:K_SA + t * 64 + 64]))
                    dve.wait_ge(main_ev, NCH * n + 4)
                    if t < LT:
                        rope(p[:, KR:VD], 1 + 2 * 2 * C_HEADS, 8, kc[:, K_CB + t * 32:K_CB + t * 32 + 32],
                             kc[:, K_SB + t * 32:K_SB + t * 32 + 32]).then_inc(rope_ac, 1)
                        dve.wait_ge(rope_ac, n + 1)
                    else:
                        dve.tensor_copy(rtmp[:, 0:2], p[:, KR:KR + 2]).then_inc(rope_ac, 1)
                        dve.wait_ge(rope_ac, n + 1)

                prepare(0)
                modulated(0)
                for t in range(NT + 1):
                    if t + 1 < NT:
                        prepare(t + 1)
                    if t >= 1:
                        finish_b(t - 1)
                    if t + 1 < NT:
                        modulated(t + 1)
                    if t < NT:
                        finish_main(t)
                norms += NT

                NSKL = NSK + l * A_HEADS

                def row_max(s):
                    _, qi, j = s
                    n = step_no(l, qi, j)
                    kind, h, m = STEPS[j]
                    kt = key_tiles(l, qi, kind)
                    c0 = kt[0][1]
                    scale = {"A": HD, "B": B_QK, "C": C_DH}[kind] ** -0.5
                    sc = bank(2 * (n % 2), 2)
                    dve.wait_ge(s_mm, n + 1)
                    if kind == "A" and qi < LT:
                        if 0 < qi < LT - 1:
                            v = sc[:, 0:512].rearrange("p (b t) -> p b t", b=4)[:, 1:4:2, :]
                            mk = kc[:, K_MASK:K_MASK + 2 * P].rearrange("p (b t) -> p b t", b=2)
                        elif qi:
                            v, mk = sc[:, c0:c0 + P], kc[:, K_MASK:K_MASK + P]
                        else:
                            v, mk = sc[:, SEQ - P:SEQ], kc[:, K_MASK + P:K_MASK + 2 * P]
                        own.did(dve.tensor_tensor(v, v, mk, ALU.add))
                    own.did(dve.tensor_reduce(mx[:, 0:1], sc[:, c0:TOK], AX_X, ALU.max))
                    if kind == "A":
                        dve.tensor_scalar(negm[:, j:j + 1], mx[:, 0:1], -scale, sinkb[:, NSKL + h:NSKL + h + 1],
                                          ALU.mult, ALU.min).then_inc(neg_done, 1)
                    else:
                        dve.tensor_scalar(negm[:, j:j + 1], mx[:, 0:1], -scale, None, ALU.mult).then_inc(neg_done, 1)

                seq = [(l, qi, j) for qi in range(nq(l)) for j in range(NS)]
                row_max(seq[0])
                row_max(seq[1])
                for k, s in enumerate(seq):
                    _, qi, j = s
                    g = ATT.index((l, qi))
                    n = step_no(l, qi, j)
                    kind, h, m = STEPS[j]
                    i = ITEM[j]
                    it = item_no(l, qi, i)
                    if kind == "C" and m == 1:
                        dve.wait_ge(exp_done, n + 1)
                        own.did(dve.reciprocal(r1[:, h:h + 1], sums[:, j:j + 1]))
                        own.did(dve.scalar_tensor_tensor(out=cc[:, h:h + 1], in0=sums[:, j - 1:j], scalar=r1[:, h:h + 1],
                                                         in1=neg_lam, op0=ALU.mult, op1=ALU.mult))
                        c0 = key_tiles(l, qi, kind)[0][1]
                        dve.scalar_tensor_tensor(out=prob[(n - 1) % 3][:, c0:TOK], in0=prob[n % 3][:, c0:TOK],
                                                 scalar=cc[:, h:h + 1], in1=prob[(n - 1) % 3][:, c0:TOK],
                                                 op0=ALU.mult, op1=ALU.add).then_inc(comb, 1)
                    if LASTSTEP[j]:
                        kt = key_tiles(l, qi, kind)
                        nb = len(kt)
                        a = nb // 2
                        dve.wait_ge(t_mm, it + 1)
                        if it >= 2:
                            dve.wait_ge(pv_mm, it - 1)
                        dve.tensor_copy(prob_t[it % 2][:, a:nb, :],
                                        bank(5)[:, 0:(nb - a) * P].rearrange("p (b t) -> p b t", b=nb - a)
                                        ).then_inc(ptd_ev, 1)
                    if k + 2 < len(seq):
                        row_max(seq[k + 2])
                    if LASTSTEP[j]:
                        dve.wait_ge(exp_done, n + 1)
                        if kind == "A":
                            dve.wait_ge(sink_e, A_HEADS * (l * NT + qi) + h + 1)
                            own.did(dve.tensor_tensor(tot[:, h:h + 1], sums[:, j:j + 1], esink[:, h:h + 1], ALU.add))
                            own.did(dve.reciprocal(rinv[:, i:i + 1], tot[:, h:h + 1]))
                        elif kind == "B":
                            own.did(dve.reciprocal(rinv[:, i:i + 1], sums[:, j:j + 1]))
                        else:
                            own.did(dve.reciprocal(rinv[:, i:i + 1], sums[:, j - 1:j]))
                        dve.wait_ge(pv_mm, it + 1)
                        if i == 0 and g >= 2:
                            dve.wait_ge(ot_mm, g - 1)
                        dve.tensor_scalar(ob[g % 2][:, i * 64:(i + 1) * 64],
                                          ps[:, 6, 0:64],
                                          rinv[:, i:i + 1], None, ALU.mult).then_inc(o_ev, 1)
                    a = ada_at(l, qi, j)
                    if a is not None:
                        ada_copy(a)
                    if j == NS - 1:
                        dve.wait_ge(o_ev, it + 1)
                        oc = ob[g % 2][:, 768:1024].rearrange("p (h d) -> p h d", h=C_HEADS)
                        cq3 = csq.rearrange("p (h d) -> p h d", h=C_HEADS)
                        own.did(dve.tensor_tensor(cq3, oc, oc, ALU.mult))
                        own.did(dve.tensor_reduce(css, cq3, AX_X, ALU.add))
                        dve.tensor_scalar(cms, css, 1.0 / C_V, EPS, ALU.mult, ALU.add).then_inc(cms_done, 1)
                        own.did(dve.tensor_tensor(oc, oc, dgain[:].unsqueeze(1).to_broadcast([P, C_HEADS, C_V]),
                                                  ALU.mult))
                        dve.wait_ge(crs_done, g + 1)
                        dve.tensor_tensor(oc, oc, crs.unsqueeze(2).to_broadcast([P, C_HEADS, C_V]), ALU.mult
                                          ).then_inc(on_done, 1)
                        dve.wait_ge(ot_mm, g + 1)
                        for b in range(4, 8):
                            last = dve.tensor_copy(qk_t[:, OT_BLOCK[b], qi * P:(qi + 1) * P],
                                                   bank(4, 2)[:, b * P:(b + 1) * P])
                        last.then_inc(otd_ev, 1)

                modulation(l, 1)
                dve.wait_ge(g1_in, 16 * 3 * (l + 1))

                for t in range(nq(l)):
                    g = tile_no(l, t)
                    n = norms + t
                    dve.wait_ge(xo_in[t % 2], 16 * (g // 2 + 1))
                    x2 = xt[:, (t % 2) * D:(t % 2 + 1) * D]
                    for h in range(2):
                        dve.wait_ge(wo_mm, 2 * g + h + 1)
                        own.did(dve.tensor_tensor(tmpo, ps[:, 2 * (g % 2) + h, :],
                                                  g1[:, int(t >= LT), h * 512:(h + 1) * 512], ALU.mult))
                        last = dve.tensor_tensor(x2[:, h * 512:(h + 1) * 512], x2[:, h * 512:(h + 1) * 512], tmpo,
                                                 ALU.add)
                        if h == 0:
                            own.did(last)
                        else:
                            last.then_inc(xo_done, 1)
                            dve.wait_ge(xo_done, g + 1)
                    mean_square(n)
                    normalise(n, t % 2, hx[:]).then_inc(xhat, 1)
                    dve.wait_ge(t1_mm, n + 1)
                    if t:
                        dve.wait_ge(lg_mm, g)
                    modulate(h2_t, bank(4, 2).rearrange("p (k t) -> p k t", k=KT), 1, int(t >= LT),
                             P).then_inc(h_done, 1)
                    dve.wait_ge(lg_mm, g + 1)
                    own.did(dve.tensor_reduce(rmx, ps[:, 6, 0:NE], AX_X, ALU.max))
                    dve.tensor_scalar(rmx, rmx, -1.0, None, ALU.mult).then_inc(rmax_done, 1)
                    dve.wait_ge(rexp_done, g + 1)
                    own.did(dve.reciprocal(rrec, rsum))
                    if t:
                        dve.wait_ge(at_mm, g)
                    dve.tensor_scalar(aff, aff_e, rrec, None, ALU.mult).then_inc(aff_done, 1)
                norms += nq(l)

                rows = CAP_L + (CAP_C if nq(l) > LT else 0)
                dve.wait_ge(at_ev, tile_no(l, nq(l) - 1) + 1)
                sets = [(0, SEQ, 0, CAP_L)] + ([(SEQ, TOK, CAP_L, CAP_C)] if nq(l) > LT else [])
                for a, b, c0, cap in sets:
                    for r in range(cap // 8):
                        o8 = slice(c0 + 8 * r, c0 + 8 * r + 8)
                        own.did(dve.max(sval[0:NE, o8], rtop[0:NE, a:b]))
                        own.did(dve.max_index(sidx[0:NE, o8], sval[0:NE, o8], rtop[0:NE, a:b]))
                        own.did(dve.match_replace(rtop[0:NE, a:b], sval[0:NE, o8], rtop[0:NE, a:b], -1.0))
                last = dve.tensor_copy(sidx_f[0:NE, 0:CAP_L], sidx[0:NE, 0:CAP_L])
                if nq(l) > LT:
                    own.did(dve.tensor_copy(sidx_f[0:NE, CAP_L:rows], sidx[0:NE, CAP_L:rows]))
                    last = dve.tensor_scalar(sidx_f[0:NE, CAP_L:rows], sidx_f[0:NE, CAP_L:rows], float(SEQ), None,
                                             ALU.add)
                last.then_inc(top_done, 1)
                dve.wait_ge(gt_mm, l + 1)
                if l:
                    dve.wait_ge(scattered, 16 * NE)
                dve.wait_ge(gv_done, l + 1)
                dve.tensor_copy(gidx[0:rows, :], ps[0:rows, 6, NE:2 * NE]).then_inc(gi_done, 1)
                dve.wait_ge(g2_in, 32 * (l + 1))

                before = own.base + own.n
                per = [0]

                def step(n, e, b, first):
                    if b < NE:
                        dve.wait_ge(xgt_mm, n + 1)
                        if not (l == 0 and first and b < 2):
                            dve.wait_ge(up_mm, n - 1)
                        for i, (r0, r1_) in enumerate([(0, CAP_L), (CAP_L, rows)][:1 + (rows > CAP_L)]):
                            src = ps[:, 0:2, 0:4 * rows].rearrange("p b (k t) -> p b k t", k=4)[:, :, :, r0:r1_]
                            dst = xg_t[b % 2].rearrange("p (b k) t -> p b k t", b=2)[:, :, :, r0:r1_]
                            w = r1_ - r0
                            for bb in range(2):
                                a_ = mc[:, 3, i, 4 * bb:4 * bb + 4].unsqueeze(2).to_broadcast([P, 4, w])
                                own.did(dve.tensor_tensor(dst[:, bb], src[:, bb], a_, ALU.mult))
                            d = xg_t[b % 2][:, :, r0:r1_]
                            last = dve.tensor_tensor(d, d, mc[:, 2, i, :].unsqueeze(2).to_broadcast([P, KT, w]),
                                                     ALU.add)
                            if i == 0 and rows > CAP_L:
                                own.did(last)
                        last.then_inc(xgt_ev, 1)
                    if not first or b >= 2:
                        dve.wait_ge(down_mm, n - 1)
                        if not (l == 0 and first and b < 4):
                            dve.wait_ge(scattered, (n - 3) * 16)
                        gv = gval[0:rows, bass.ds(e - 2, 1)] if not isinstance(e, int) else gval[0:rows, e - 2:e - 1]
                        dve.scalar_tensor_tensor(out=y[b % 2][0:rows, :], in0=bank(5, 2)[0:rows, :], scalar=gv,
                                                 in1=g2[0:rows, :], op0=ALU.mult, op1=ALU.mult).then_inc(y_done, 1)
                    if b < NE:
                        dve.wait_ge(up_mm, n + 1)
                        dve.wait_ge(silu_done, n + 1)
                        if not (l == 0 and first and b < 2):
                            dve.wait_ge(hidt_mm, n - 1)
                        dve.tensor_tensor(hid[b % 2][0:rows, :], ps[0:rows, 3, :], sg[0:rows, :], ALU.mult
                                          ).then_inc(hid_done, 1)

                for e in range(LOOP_E):
                    step(l * NE + e, e, e, True)
                per = 6 if rows > CAP_L else 0
                per = (3 if rows > CAP_L else 0) + 2
                start = own.n
                with dve.Fori(0, (NE - LOOP_E) // BODY) as it:
                    own.base = it * (per * BODY)
                    for b in range(BODY):
                        step(BODY * it + (l * NE + LOOP_E + b), BODY * it + (LOOP_E + b), LOOP_E + b, False)
                    assert own.n - start == per * BODY
                own.base = 0
                own.n = start + per * (NE - LOOP_E)
                for e in range(NE, NE + 2):
                    step(l * NE + e, e, e, False)

            dve.wait_ge(g1_in, 16 * (3 * DEPTH + 1))
            for t in range(LT):
                n = norms + t
                mean_square(n)
                x2 = xt[:, (t % 2) * D:(t % 2 + 1) * D]
                own.did(normalise(n, t % 2, x2))
                dve.tensor_tensor(x2, x2, fgain, ALU.mult).then_inc(out_done, 1)

        @block.tensor
        def _(pe):
            def weights(item, width=512, k=KT):
                return slot(place[item])[:, 0:k * width].rearrange("p (k n) -> p k n", k=k)

            def ada_product(n):
                item = ada_items[n]
                if n:
                    pe.wait_ge(ada_out, n)
                wait_slot(pe, item)
                w = weights(item)
                for r in range(2):
                    for j in range(4):
                        k = 2 * j + r
                        last = pe.matmul(ps[32 * j:32 * j + 32, 7, :], csil[:, k * 32:(k + 1) * 32], w[:, k, :],
                                         start=(r == 0), stop=(r == 1))
                last.then_inc(ada_mm, 1)

            def ada_total(n):
                pe.wait_ge(ada_row, n + 1)
                pe.matmul(ps[0:32, 7, :], sel, modrow[:], start=True, stop=True).then_inc(ada_sum, 1)

            counts = [pe.alloc_register(f"pe_count{n}") for n in range(2)]
            pe.wait_ge(csil_done, 1)
            for n in range(ADA_FIRST):
                ada_product(n)
                ada_total(n)

            norms = 0
            for l in range(DEPTH):
                def transpose_x(t):
                    n = norms + t
                    pe.wait_ge(xhat, n + 1)
                    if n:
                        pe.wait_ge(h_done, n)
                    for k in range(KT):
                        last = pe.transpose(bank(4, 2)[:, k * P:(k + 1) * P], hx[:, k:D:KT], ident)
                    last.then_inc(t1_mm, 1)

                def main(t, ch):
                    n = tile_no(l, t)
                    a, b = IN_CHUNK[ch]
                    w = weights(("in", l, ch), b - a)
                    if ch == 0:
                        pe.wait_ge(h_done, norms + t + 1)
                    if t == 0:
                        wait_slot(pe, ("in", l, ch))
                    if n:
                        pe.wait_ge(main_ev, NCH * (n - 1) + ch + 1)
                        if ch == 3:
                            pe.wait_ge(sq2, 2 * n)
                    if l and t == 0:
                        pe.wait_ge(y_done, l * NE)
                    for k in range(KT):
                        last = pe.matmul(ps[:, ch, 0:b - a], h_t[n % 2][:, k, :], w[:, k, :], start=(k == 0),
                                         stop=(k == KT - 1))
                    last.then_inc(main_mm, 1)

                def small(t, u):
                    n = tile_no(l, t)
                    p = pt[n % 2]
                    if 8 * n + u >= 2:
                        pe.wait_ge(small_ev, 8 * n + u - 1)
                    dst = ps[:, 6 + u % 2, :]
                    if u == 0:
                        if n == 0:
                            pe.wait_ge(ada_out, ADA_FIRST)
                        pe.wait_ge(cqn, n + 1)
                        for k in range(2):
                            pe.transpose(dst[:, k * P:(k + 1) * P], p[:, CQ + k:CKV:2], ident)
                        last = pe.transpose(dst[:, 2 * P:3 * P], p[:, CKV:KR], ident)
                    elif u == 1:
                        pe.wait_ge(small_ev, 8 * n + 1)
                        if t == 0:
                            pe.wait_ge(wproj_in, 16 * 9 * (l + 1))
                        for k in range(2):
                            last = pe.matmul(dst[:, 0:384], c_t[:, k, :], wuq[:, k * 384:(k + 1) * 384],
                                             start=(k == 0), stop=(k == 1))
                    elif u == 2:
                        last = pe.matmul(dst, c_t[:, 2, :], wukv[:], start=True, stop=True)
                    else:
                        if u == 3:
                            pe.wait_ge(rope_ac, n + 1)
                        if u == 6:
                            pe.wait_ge(rope_b, n + 1)
                        if u == 3:
                            srcs = [p[:, QA + P * b:QA + P * (b + 1)] for b in range(4)]
                        elif u == 4:
                            srcs = [p[:, KA:VA], p[:, QD:QD + P], p[:, QD + P:KD], p[:, KD:KD + P]]
                        elif u == 5:
                            srcs = [p[:, KD + P:VD]]
                        else:
                            srcs = [(q96 if u == 6 else k96)[:, h] for h in range(B_HEADS)]
                        rows = P if u < 6 else B_QK
                        for b, s in enumerate(srcs):
                            last = pe.transpose(dst[0:rows, b * P:(b + 1) * P], s, ident)
                    last.then_inc(small_mm, 1)

                transpose_x(0)
                for t in range(NT + 1):
                    for ch in range(NCH):
                        if t < NT:
                            main(t, ch)
                        if t >= 1:
                            for u in ([0], [1, 2], [3, 4, 5, 6, 7], [])[ch]:
                                small(t - 1, u)
                        if ch == 1 and t + 1 < NT:
                            transpose_x(t + 1)
                norms += NT

                def scores(s):
                    _, qi, j = s
                    n = step_no(l, qi, j)
                    g = ATT.index((l, qi))
                    kind, h, m = STEPS[j]
                    if j == 0:
                        pe.wait_ge(qz_done, g + 1)
                    if n >= 2:
                        pe.wait_ge(exp_done, n - 1)
                    z = qz[:, (g % 2) * 16 * P:(g % 2 + 1) * 16 * P].rearrange("p (h t) -> p h t", h=16)
                    cols = slice(qi * P, (qi + 1) * P)
                    if kind == "A":
                        lhs, kb, rows = z[:, h, :], B_AK, P
                    elif kind == "B":
                        lhs, kb, rows = qk_t[0:B_QK, B_BQ + h, cols], B_BK + h, B_QK
                    else:
                        mm = 2 * h + m
                        lhs, kb, rows = z[:, 8 + mm, :], B_CK + mm // 4, P
                    kt = [t for t, _ in key_tiles(l, qi, kind)]
                    dst = bank(2 * (n % 2), 2)
                    lat = [t for t in kt if t < LT]
                    if lat:
                        w = len(lat) * P
                        pe.matmul(dst[:, SEQ - w:SEQ], lhs, qk_t[0:rows, kb, lat[0] * P:lat[0] * P + w],
                                  start=True, stop=True)
                    pe.matmul(dst[:, SEQ:TOK], lhs, qk_t[0:rows, kb, SEQ:TOK], start=True, stop=True
                              ).then_inc(s_mm, 1)

                seq = [(l, qi, j) for qi in range(nq(l)) for j in range(NS)]
                pe.wait_ge(main_ev, NCH * (tile_no(l, NT - 1) + 1))
                pe.wait_ge(sq2, 2 * (tile_no(l, NT - 1) + 1))
                pe.wait_ge(small_ev, 8 * (tile_no(l, NT - 1) + 1))
                scores(seq[0])
                scores(seq[1])
                for k, s in enumerate(seq):
                    _, qi, j = s
                    g = ATT.index((l, qi))
                    n = step_no(l, qi, j)
                    kind, h, m = STEPS[j]
                    kt = key_tiles(l, qi, kind)
                    it = item_no(l, qi, ITEM[j])
                    if LASTSTEP[j]:
                        if kind == "C":
                            pe.wait_ge(comb, C_HEADS * (l * NT + qi) + h + 1)
                            src = prob[(n - 1) % 3]
                        else:
                            pe.wait_ge(exp_done, n + 1)
                            src = prob[n % 3]
                        if j == 0 and g:
                            pe.wait_ge(ota_ev, g)
                            pe.wait_ge(otd_ev, g)
                        for b, (_, c0) in enumerate(kt):
                            a = len(kt) // 2
                            last = pe.transpose(ps[:, 4 + (b >= a), (b - a * (b >= a)) * P:][:, 0:P],
                                                src[:, c0:c0 + P], ident)
                        last.then_inc(t_mm, 1)
                    if k + 2 < len(seq):
                        scores(seq[k + 2])
                    if LASTSTEP[j]:
                        pe.wait_ge(pta_ev, it + 1)
                        pe.wait_ge(ptd_ev, it + 1)
                        if it:
                            pe.wait_ge(o_ev, it)
                        for b, (t, _) in enumerate(kt):
                            if kind == "A":
                                v = va[:, t, (h // 4) * HD:(h // 4 + 1) * HD]
                            else:
                                v = (vb if kind == "B" else vc)[:, t, h * 64:(h + 1) * 64]
                            last = pe.matmul(ps[:, 6, 0:64], prob_t[it % 2][:, b, :], v,
                                             start=(b == 0), stop=(b == len(kt) - 1))
                        last.then_inc(pv_mm, 1)
                    a = ada_at(l, qi, j)
                    if a is not None:
                        ada_product(a)
                    a = ada_sum_at(l, qi, j)
                    if a is not None:
                        ada_total(a)
                    if j == NS - 1:
                        pe.wait_ge(on_done, g + 1)
                        for kk in range(KT):
                            last = pe.transpose(bank(4, 2)[:, kk * P:(kk + 1) * P], ob[g % 2][:, kk:D:KT], ident)
                        last.then_inc(ot_mm, 1)

                def logits(t):
                    g = tile_no(l, t)
                    n = norms + t
                    transpose_x(t)
                    pe.wait_ge(h_done, n + 1)
                    if t == 0:
                        pe.wait_ge(g1_in, 16 * 3 * (l + 1))
                    for k in range(KT):
                        last = pe.matmul(ps[:, 6, 0:NE], h2_t[:, k, :], wr[:, k * NE:(k + 1) * NE],
                                         start=(k == 0), stop=(k == KT - 1))
                    last.then_inc(lg_mm, 1)

                def affinities(t):
                    g = tile_no(l, t)
                    pe.wait_ge(aff_done, g + 1)
                    if t:
                        pe.wait_ge(at_ev, g)
                    pe.transpose(ps[0:NE, 7, 0:P], aff, ident).then_inc(at_mm, 1)

                ng = len([a for a in ATT if a[0] <= l])
                pe.wait_ge(ota_ev, ng)
                pe.wait_ge(otd_ev, ng)
                pe.wait_ge(o_ev, item_no(l, nq(l) - 1, NI - 1) + 1)
                if l == 0:
                    pe.wait_ge(ada_out, len(ada_items))
                for t in range(nq(l) + 1):
                    g = tile_no(l, t)
                    for h in range(2):
                        if t < nq(l):
                            if t >= 2:
                                pe.wait_ge(xo_done, g - 1)
                            if t == 0:
                                wait_slot(pe, ("out", l, h))
                            w = weights(("out", l, h))
                            for k in range(KT):
                                last = pe.matmul(ps[:, 2 * (g % 2) + h, :], qk_t[:, OT_BLOCK[k], t * P:(t + 1) * P],
                                                 w[:, k, :], start=(k == 0), stop=(k == KT - 1))
                            last.then_inc(wo_mm, 1)
                        if t >= 1:
                            (logits if h == 0 else affinities)(t - 1)
                norms += nq(l)

                rows = CAP_L + (CAP_C if nq(l) > LT else 0)
                pe.wait_ge(top_done, l + 1)
                pe.transpose(ps[0:rows, 6, 0:NE], sval[0:NE, 0:rows], ident[0:NE, 0:NE])
                pe.transpose(ps[0:rows, 6, NE:2 * NE], sidx_f[0:NE, 0:rows], ident[0:NE, 0:NE]).then_inc(gt_mm, 1)

                def step(n, b, r, first, pair):
                    def landed(q, pos):
                        pe.wait_ge(ring_in[q % NSLOT], pos)
                    if b < NE:
                        before = [] if l == 0 and first and b == 0 else [(xgt_ev, n)]
                        wait_in_loop(pe, counts, gt_mm, l + 1, (xg_in[b % 2], pair * 16 + 16), *before)
                        for k in range(KT):
                            last = pe.transpose(ps[:, k // 4, (k % 4) * rows:(k % 4 + 1) * rows],
                                                xg[b % 2][0:rows, k:D:KT], ident[0:rows, 0:rows])
                        last.then_inc(xgt_mm, 1)
                    if not first or b >= 2:
                        pe.wait_ge(hidt_ev, n - 1)
                        if not (l == 0 and first and b == 2):
                            pe.wait_ge(y_done, n - 2)
                        landed(*r[0])
                        w = slot(r[0][0]).rearrange("p (k n) -> p k n", k=4)
                        for h in range(2):
                            for k in range(4):
                                last = pe.matmul(ps[0:rows, 5 + h, :], hid_t[b % 2][:, k, 0:rows],
                                                 w[:, k, h * 512:(h + 1) * 512], start=(k == 0), stop=(k == 3))
                        last.then_inc(down_mm, 1)
                    if b < NE:
                        pe.wait_ge(xgt_ev, n + 1)
                        if not (l == 0 and first and b == 0):
                            pe.wait_ge(silu_done, n)
                        landed(*r[1])
                        w = slot(r[1][0]).rearrange("p (k n) -> p k n", k=KT)
                        for k in range(KT):
                            last = pe.matmul(ps[0:rows, 2, :], xg_t[b % 2][:, k, 0:rows], w[:, k, :],
                                             start=(k == 0), stop=(k == KT - 1))
                        last.then_inc(gate_mm, 1)
                    if not first or b >= 1:
                        if b <= NE:
                            before = [] if l == 0 and first and b == 1 else [(hidt_ev, n - 1)]
                            wait_in_loop(pe, counts, gt_mm, l + 1, (hid_done, n), *before)
                            for k in range(4):
                                last = pe.transpose(ps[:, 4, k * rows:(k + 1) * rows],
                                                    hid[(b - 1) % 2][0:rows, k:512:4], ident[0:rows, 0:rows])
                            last.then_inc(hidt_mm, 1)
                    if b < NE:
                        if not (l == 0 and first and b == 0):
                            pe.wait_ge(hid_done, n)
                        landed(*r[2])
                        w = slot(r[2][0]).rearrange("p (k n) -> p k n", k=KT)
                        for k in range(KT):
                            last = pe.matmul(ps[0:rows, 3, :], xg_t[b % 2][:, k, 0:rows], w[:, k, :],
                                             start=(k == 0), stop=(k == KT - 1))
                        last.then_inc(up_mm, 1)

                def at(item):
                    r_ = place.get(item)
                    return None if r_ is None else (r_, 16 * (r_ // NSLOT + 1))

                for e in range(LOOP_E):
                    step(l * NE + e, e, [at(("d", l, e - 2)), at(("g", l, e)), at(("u", l, e))], True,
                         (l * NE + e) // 2)
                turns = 3 * BODY // NSLOT
                with pe.Fori(0, (NE - LOOP_E) // BODY) as itr:
                    for b in range(BODY):
                        e = LOOP_E + b
                        where = [at(("d", l, e - 2)), at(("g", l, e)), at(("u", l, e))]
                        step(BODY * itr + (l * NE + e), e,
                             [(q, itr * (16 * turns) + v) for q, v in where], False,
                             itr * (BODY // 2) + (l * NE + e) // 2)
                step(l * NE + NE, NE, [at(("d", l, NE - 2)), None, None], False, None)
                step(l * NE + NE + 1, NE + 1, [at(("d", l, NE - 1)), None, None], False, None)
    es.close()


_INS = ["x", "c", "ctx", "c_ctx", "norm1", "norm2", "w_ada", "b_ada", "w_in", "sink", "mla_q_norm", "w_uq",
        "mla_kv_norm", "w_ukv", "lam_q1", "lam_k1", "lam_q2", "lam_k2", "diff_norm", "w_out", "w_router",
        "w_gate", "w_up", "w_down", "final_norm"]


def kernel(**inputs):
    import concourse.bacc as _bacc
    from concourse.bass_utils import run_bass_kernel_spmd as _run

    nc = _bacc.Bacc("TRN2", target_bir_lowering=False, num_devices=1)
    arrays = {f"in_{name}_dram": np.ascontiguousarray(inputs[name]) for name in _INS}
    arrays["shape_constants"] = shape_constants()
    args = [nc.dram_tensor(name, a.shape, mybir.dt.from_np(a.dtype), kind="ExternalInput").ap()
            for name, a in arrays.items()]
    args.append(nc.dram_tensor("out_0_dram", (1, SEQ, D), F32, kind="ExternalOutput").ap())
    build(nc, *args)
    r = _run(nc, [arrays], core_ids=[0])
    return r.results[0]["out_0_dram"]
```

```python
from contextlib import ExitStack

import numpy as np

import concourse.bass as bass
from concourse import mybir

F32 = mybir.dt.float32
U32 = mybir.dt.uint32
ALU = mybir.AluOpType
ACT = mybir.ActivationFunctionType
AX_X = mybir.AxisListType.X

P = 128
D = 1024
KT = D // P
SEQ, CTX = 512, 256
TOK = SEQ + CTX
LT, CT = SEQ // P, CTX // P
NT = LT + CT
DEPTH = 2
EPS = 1e-6
NEG_INF = -1e30
GRID_W = 64
ROPE_BASE = 10000.0

A_HEADS, A_KV, HD = 8, 2, 64
B_HEADS, B_NOPE, B_ROPE, B_V, B_QR, B_KVR = 4, 64, 32, 64, 256, 128
B_QK = B_NOPE + B_ROPE
C_HEADS, C_DH, C_V = 4, 32, 64
IN_W = 1952
QA, KA, VA, CQ, CKV, KR, QD, KD, VD = 0, 512, 640, 768, 1024, 1152, 1184, 1440, 1696
IN_CHUNK = [(0, 512), (512, 1024), (1024, 1440), (1440, 1952)]
NCH = len(IN_CHUNK)

NE, FE = 16, 512
CAP_L, CAP_C = 2 * SEQ // NE, 2 * CTX // NE
NSLOT = 4
PAIRS = NE // 2
SLOT = KT * 512

N_ADA = 6 * D // 512
ADA_FIRST = 4

STEPS = [("A", h, 0) for h in range(A_HEADS)] + [("B", h, 0) for h in range(B_HEADS)]
STEPS += [("C", h, m) for h in range(C_HEADS) for m in range(2)]
NS = len(STEPS)
NI = A_HEADS + B_HEADS + C_HEADS
ITEM = [j if j < 12 else 12 + (j - 12) // 2 for j in range(NS)]
LASTSTEP = [j < 12 or j % 2 == 1 for j in range(NS)]
B_AQ, B_AK, B_CQ, B_CK, B_BQ, B_BK, NBLK = 0, 4, 5, 7, 9, 13, 17
OT_AFTER = 3
OT_BLOCK = [0, 1, 2, 3, 5, 6, 9, 10]

K_ID, K_MASK, K_SEL, K_CA, K_SA, K_CB, K_SB = 0, 128, 384, 416, 672, 928, 1056
NCONST = 1184


def shape_constants():
    k = np.zeros((P, NCONST), np.float32)
    k[:, K_ID:K_ID + P] = np.eye(P)
    q, j = np.arange(P)[:, None], np.arange(P)[None, :]
    k[:, K_MASK:K_MASK + P] = np.where(j >= q, 0.0, NEG_INF)
    k[:, K_MASK + P:K_MASK + 2 * P] = np.where(j <= q, 0.0, NEG_INF)
    for g in range(4):
        for i in range(2):
            k[32 * g + i, K_SEL + i] = 1.0
    for c0, s0, rot in ((K_CA, K_SA, HD), (K_CB, K_SB, B_ROPE)):
        nf = rot // 4
        inv = (np.float32(ROPE_BASE) ** (-np.arange(nf, dtype=np.float32) / np.float32(nf))).astype(np.float32)
        for t in range(LT):
            tok = t * P + np.arange(P)
            for axis, pos in enumerate((tok // GRID_W, tok % GRID_W)):
                ang = pos[:, None].astype(np.float32) * inv
                cos, sin = np.cos(ang), np.sin(ang)
                o = t * rot + axis * 2 * nf
                k[:, c0 + o:c0 + o + 2 * nf] = np.concatenate([cos, cos], 1)
                k[:, s0 + o:s0 + o + 2 * nf] = np.concatenate([-sin, sin], 1)
    return k


def lam_init(l):
    return 0.8 - 0.6 * float(np.exp(-0.3 * l))


def nq(l):
    return NT if l < DEPTH - 1 else LT


def wait_in_loop(eng, regs, known, count, *waits):
    values = []
    for reg, (sem, value) in zip(regs, waits):
        if not isinstance(value, int):
            eng.reg_mov(reg, value)
            value = eng.snap(reg)
        values.append((sem, value))
    eng.wait_ge(known, count)
    for sem, value in values:
        eng.wait_ge(sem, value)


class Steps:

    def __init__(self, eng, sem):
        self.eng, self.sem, self.base, self.n = eng, sem, 0, 0

    def did(self, ins):
        ins.then_inc(self.sem, 1)
        self.n += 1
        self.eng.wait_ge(self.sem, self.base + self.n)


def key_tiles(l, qi, kind):
    if qi >= LT:
        lat = []
    elif kind == "A":
        lat = list(range(max(0, qi - 1), min(LT - 1, qi + 1) + 1))
    else:
        lat = list(range(LT))
    c0 = SEQ - P * len(lat)
    return [(t, c0 + P * n) for n, t in enumerate(lat)] + [(LT + c, SEQ + P * c) for c in range(CT)]


def keys_only(l, t):
    return l == DEPTH - 1 and t >= LT


def chunk_cols(l, t, ch):
    a, b = IN_CHUNK[ch]
    if keys_only(l, t):
        b = {0: a, 1: CQ, 2: QD, 3: b}[ch]
    return a, b


def small_uses(l, t):
    return [0, 2, 4, 5, 7] if keys_only(l, t) else list(range(8))


MAIN = [(l, t, ch) for l in range(DEPTH) for t in range(NT) for ch in range(NCH)]
SMALL = [(l, t, u) for l in range(DEPTH) for t in range(NT) for u in small_uses(l, t)]


def main_count(l, t, ch):
    return sum(1 for m in MAIN if m <= (l, t, ch) and chunk_cols(*m)[1] > chunk_cols(*m)[0])


def small_count(l, t, u=7):
    return sum(1 for m in SMALL if m <= (l, t, u))


def small_before(l, t, u):
    return max([n + 1 for n, m in enumerate(SMALL) if m < (l, t, u) and m[2] % 2 == u % 2], default=0)


def tile_before(l, t, k=1):
    n = l * NT + t - k
    return n // NT, n % NT


def ring_plan():
    plan = [("ada", 0, c) for c in range(ADA_FIRST)] + [("in", 0, c) for c in range(NCH)]
    plan += [("ada", 0, c) for c in range(ADA_FIRST, N_ADA)] + [("ada", 1, c) for c in range(N_ADA)]
    for l in range(DEPTH):
        if l:
            plan += [("in", l, c) for c in range(NCH)]
        plan += [("out", l, h) for h in range(2)]
        if l == DEPTH - 1:
            break
        plan += [("g", l, 0), ("u", l, 0), ("g", l, 1), ("u", l, 1)]
        for e in range(2, NE):
            plan += [("d", l, e - 2), ("g", l, e), ("u", l, e)]
        plan += [("d", l, NE - 2), ("d", l, NE - 1)]
    return plan


def build(nc, x, c, ctx_in, c_ctx, norm1, norm2, w_ada, b_ada, w_in, sink, q_norm, w_uq, kv_norm, w_ukv,
          lam_q1, lam_k1, lam_q2, lam_k2, diff_norm, w_out, w_router, w_gate, w_up, w_down, final_norm,
          consts, out):
    es = ExitStack()

    def sb(name, n, dt=F32):
        return es.enter_context(nc.sbuf_tensor(name, [P, n], dt))

    def sem(name):
        return es.enter_context(nc.semaphore(name))

    x_s = nc.dram_tensor("x_s", (TOK, D), F32).ap()
    h2_s = nc.dram_tensor("h2_s", (TOK, D), F32).ap()
    mod_s = nc.dram_tensor("mod_s", (DEPTH, 2, 6 * D), F32).ap()

    ring = sb("ring", NSLOT * SLOT)
    qz = sb("qz", 2 * 16 * P)
    store = sb("store", NBLK * TOK + TOK + 2 * 2 * TOK)
    work = sb("work", 7744)
    xt = sb("xt", 2 * D)
    hx = sb("hx", D)
    kc = sb("kc", NCONST)
    wuq = sb("wuq", 2 * 384)
    wukv = sb("wukv", 512)
    wr = sb("wr", KT * NE)
    modrow = sb("modrow", 512)
    msum = sb("msum", 512)
    csil = sb("csil", KT * 32)
    ctmp = sb("ctmp", 3 * 16)
    modc = sb("modc", 4 * 2 * KT)
    ncol = sb("ncol", 2 * DEPTH * KT)
    bcol = sb("bcol", 2 * KT)
    gcol = sb("gcol", 2 + 1)
    dgain = sb("dgain", C_V)
    sinkb = sb("sinkb", 2 * DEPTH * A_HEADS)
    lamb = sb("lamb", 4 * C_DH + 8)
    half = sb("half", 8)
    st = sb("st", 160)
    gval = sb("gval", NE)
    gidx = sb("gidx", NE, U32)
    ix = sb("ix", 2 * PAIRS, U32)

    ps = es.enter_context(nc.psum_tensor("ps", [P, 8, 512], F32))

    def bank(b, n=1):
        return ps[:, b:b + n, :].rearrange("p b n -> p (b n)")

    ident = kc[:, K_ID:K_ID + P]
    sel = kc[:, K_SEL:K_SEL + 32]

    def slot(r):
        o = (r % NSLOT) * SLOT
        return ring[:, o:o + SLOT]

    spare = store[:, 10 * D:10 * D + SLOT]

    qk_t = store[:, 0:NBLK * TOK].rearrange("p (b t) -> p b t", b=NBLK)
    o = NBLK * TOK
    va = store[:, o:o + TOK].rearrange("p (t n) -> p t n", t=NT)
    vb = store[:, o + TOK:o + 3 * TOK].rearrange("p (t n) -> p t n", t=NT)
    vc = store[:, o + 3 * TOK:o + 5 * TOK].rearrange("p (t n) -> p t n", t=NT)
    xg = [store[:, n * D:(n + 1) * D] for n in range(2)]
    xg_t = [store[:, (2 + n) * D:(3 + n) * D].rearrange("p (k t) -> p k t", k=KT) for n in range(2)]
    y = [store[:, (4 + n) * D:(5 + n) * D] for n in range(2)]
    hid = [store[:, 6 * D + n * 512:6 * D + (n + 1) * 512] for n in range(2)]
    hid_t = [store[:, 7 * D + n * 512:7 * D + (n + 1) * 512].rearrange("p (k t) -> p k t", k=4) for n in range(2)]
    sg = store[:, 8 * D:8 * D + 512]
    g2 = store[:, 9 * D:10 * D]
    h_t = [work[:, n * D:(n + 1) * D].rearrange("p (k t) -> p k t", k=KT) for n in range(2)]
    pt = [work[:, 2048 + n * IN_W:2048 + (n + 1) * IN_W] for n in range(2)]
    o = 2048 + 2 * IN_W
    c_t = work[:, o:o + 384].rearrange("p (k t) -> p k t", k=3)
    q96 = work[:, o + 384:o + 768].rearrange("p (h d) -> p h d", h=B_HEADS)
    k96 = work[:, o + 768:o + 1152].rearrange("p (h d) -> p h d", h=B_HEADS)
    rtmp = work[:, o + 1152:o + 1152 + 640]
    prob = [work[:, n * TOK:(n + 1) * TOK] for n in range(3)]
    prob_t = [work[:, (3 + n) * TOK:(4 + n) * TOK].rearrange("p (b t) -> p b t", b=NT) for n in range(2)]
    ob = [work[:, 5 * TOK + n * D:5 * TOK + (n + 1) * D] for n in range(2)]
    csq = work[:, 5 * TOK + 2 * D:5 * TOK + 2 * D + 256]
    g1 = work[:, 0:2 * D].rearrange("p (i n) -> p i n", i=2)
    h2_t = work[:, 2 * D:3 * D].rearrange("p (k t) -> p k t", k=KT)
    aff = work[:, 3 * D:3 * D + NE]
    aff_e = work[:, 3 * D + 32:3 * D + 32 + NE]
    rtop = work[:, 3 * D + 64:3 * D + 64 + TOK]
    sval = work[:, 4 * D:4 * D + P]
    sidx_f = work[:, 4 * D + P:4 * D + 2 * P]
    sidx = work[:, 4 * D + 2 * P:4 * D + 3 * P].bitcast(U32)
    tmpo = work[:, 5 * D:5 * D + 512]
    fgain = work[:, 0:D]

    ss, msq, rstd = st[:, 0:2], st[:, 2:4], st[:, 4:6]
    ss2, ms2, rs2 = st[:, 6:8], st[:, 8:10], st[:, 10:12]
    mx, negm = st[:, 12:14], st[:, 14:34]
    sums, esink, rinv = st[:, 34:54], st[:, 54:62], st[:, 62:78]
    r1, cc, tot = st[:, 78:82], st[:, 82:86], st[:, 86:94]
    css, cms, crs = st[:, 94:98], st[:, 98:102], st[:, 102:106]
    rmx, rsum, rrec = st[:, 106:107], st[:, 107:108], st[:, 108:109]

    c_in, consts_in, cols_in, sink_in = sem("c_in"), sem("consts_in"), sem("cols_in"), sem("sink_in")
    ring_in = [sem(f"ring_in{n}") for n in range(NSLOT)]
    qz_in, spare_in = sem("qz_in"), sem("spare_in")
    mod_init, mod_stored = sem("mod_init"), sem("mod_stored")
    modc_in, wproj_in = sem("modc_in"), sem("wproj_in")
    g1_in, g2_in = sem("g1_in"), sem("g2_in")
    x_first = sem("x_first")
    x_in = [sem(f"x_in{n}") for n in range(2)]
    xo_in = [sem(f"xo_in{n}") for n in range(2)]
    xg_in = [sem(f"xg_in{n}") for n in range(2)]
    xs_stored, h2_stored, scattered, out_stored = (
        sem("xs_stored"), sem("h2_stored"), sem("scattered"), sem("out_stored"))
    pool_did, act_did, dve_did = sem("pool_did"), sem("act_did"), sem("dve_did")
    zeroed, csil_e, csil_done, first_cols = sem("zeroed"), sem("csil_e"), sem("csil_done"), sem("first_cols")
    lam_e, lam_p = sem("lam_e"), sem("lam_p")
    ada_mm, ada_row, ada_sum, ada_out = sem("ada_mm"), sem("ada_row"), sem("ada_sum"), sem("ada_out")
    modc_done = sem("modc_done")
    sumsq, ms_done, rstd_done, xhat, t1_mm, h_done = (
        sem("sumsq"), sem("ms_done"), sem("rstd_done"), sem("xhat"), sem("t1_mm"), sem("h_done"))
    main_mm, main_ev, sq2, ms2_done, rs2_done, cqn = (
        sem("main_mm"), sem("main_ev"), sem("sq2"), sem("ms2_done"), sem("rs2_done"), sem("cqn"))
    small_mm, small_ev, rope_ac, rope_b = sem("small_mm"), sem("small_ev"), sem("rope_ac"), sem("rope_b")
    qz_done, s_mm, neg_done, exp_done, sink_e, comb = (
        sem("qz_done"), sem("s_mm"), sem("neg_done"), sem("exp_done"), sem("sink_e"), sem("comb"))
    t_mm, pta_ev, ptd_ev, pv_mm, o_ev = sem("t_mm"), sem("pta_ev"), sem("ptd_ev"), sem("pv_mm"), sem("o_ev")
    cms_done, crs_done, on_done, ot_mm, ota_ev, otd_ev = (
        sem("cms_done"), sem("crs_done"), sem("on_done"), sem("ot_mm"), sem("ota_ev"), sem("otd_ev"))
    wo_mm, xo_done, lg_mm, rmax_done, rexp_done, aff_done, at_mm, at_ev = (
        sem("wo_mm"), sem("xo_done"), sem("lg_mm"), sem("rmax_done"), sem("rexp_done"), sem("aff_done"),
        sem("at_mm"), sem("at_ev"))
    top_done, gt_mm, gv_done, gi_done = sem("top_done"), sem("gt_mm"), sem("gv_done"), sem("gi_done")
    xgt_mm, xgt_ev, gate_mm, silu_done, up_mm, hid_done = (
        sem("xgt_mm"), sem("xgt_ev"), sem("gate_mm"), sem("silu_done"), sem("up_mm"), sem("hid_done"))
    hidt_mm, hidt_ev, down_mm, y_done, out_done = (
        sem("hidt_mm"), sem("hidt_ev"), sem("down_mm"), sem("y_done"), sem("out_done"))

    plan = ring_plan()
    place = {item: r for r, item in enumerate(plan)}
    ada_items = [it for it in plan if it[0] == "ada"]
    ada_no = {(it[1], it[2]): n for n, it in enumerate(ada_items)}

    def wait_slot(eng, item):
        r = place[item]
        eng.wait_ge(ring_in[r % NSLOT], 16 * (r // NSLOT + 1))

    def tile_no(l, t):
        return l * NT + t

    def step_no(l, qi, j):
        return (l * NT + qi) * NS + j

    def item_no(l, qi, i):
        return (l * NT + qi) * NI + i

    def wait_x(eng, g):
        if g:
            eng.wait_ge(x_in[g % 2], 16 * (g // 2 + g % 2))
        else:
            eng.wait_ge(x_first, 16)

    ATT = [(l, qi) for l in range(DEPTH) for qi in range(nq(l))]
    R = len(plan)
    PAIR_SLOTS = [("g", 0, slot(R), ring_in[R % NSLOT], R // NSLOT, gate_mm),
                  ("g", 1, slot(R + 1), ring_in[(R + 1) % NSLOT], (R + 1) // NSLOT, gate_mm),
                  ("u", 0, qz[:], qz_in, 0, up_mm),
                  ("u", 1, spare, spare_in, 0, up_mm),
                  ("d", 0, slot(R + 2), ring_in[(R + 2) % NSLOT], (R + 2) // NSLOT, down_mm),
                  ("d", 1, slot(R + 3), ring_in[(R + 3) % NSLOT], (R + 3) // NSLOT, down_mm)]
    PAIR_BASE = (DEPTH - 1) * NE
    LOOP_E, BODY = 4, 4

    def ada_at(l, qi, j):
        n = (qi * NS + j) // 5
        if l == 0 and j % 5 == 4 and n < len(ada_items) - ADA_FIRST:
            return ADA_FIRST + n
        return None

    def ada_sum_at(l, qi, j):
        s = qi * NS + j - 2
        return ada_at(l, s // NS, s % NS) if s >= 0 else None

    with nc.Block() as block:

        @block.sync
        def _(sp):
            def source(item):
                kind, l, n = item
                if kind == "ada":
                    return w_ada[l].rearrange("(p k) n -> p k n", k=KT)[:, :, 512 * n:512 * n + 512], 512
                if kind == "in":
                    a, b = IN_CHUNK[n]
                    return w_in[l].rearrange("(p k) n -> p k n", k=KT)[:, :, a:b], b - a
                if kind == "out":
                    return w_out[l].rearrange("(p k) n -> p k n", k=KT)[:, :, 512 * n:512 * n + 512], 512

            def freed(item):
                kind, l, n = item
                if kind == "ada":
                    sp.wait_ge(ada_mm, ada_no[(l, n)] + 1)
                elif kind == "in":
                    sp.wait_ge(main_mm, main_count(l, NT - 1, n))
                elif kind == "out":
                    sp.wait_ge(wo_mm, 2 * tile_no(l, nq(l) - 1) + n + 1)
                else:
                    sp.wait_ge({"g": gate_mm, "u": up_mm, "d": down_mm}[kind], l * NE + n + 1)

            def expert_weights(kind, l, e):
                if kind == "d":
                    return w_down[l, e].rearrange("(p k) n -> p (k n)", k=4)
                return (w_gate if kind == "g" else w_up)[l, e].rearrange("(p k) n -> p (k n)", k=KT)

            def load(r):
                if r >= NSLOT:
                    freed(plan[r - NSLOT])
                kind, l, n = plan[r]
                if kind in "gud":
                    sp.dma_start(slot(r), expert_weights(kind, l, n)).then_inc(ring_in[r % NSLOT], 16)
                else:
                    src, width = source(plan[r])
                    dst = slot(r)[:, 0:KT * width].rearrange("p (k n) -> p k n", k=KT)
                    sp.dma_start(dst, src).then_inc(ring_in[r % NSLOT], 16)

            counts = [sp.alloc_register(f"sp_count{n}") for n in range(2)]
            with nc.allow_non_contiguous_dma(reason="a few columns"):
                sp.dma_start(ctmp[:, 0:KT], c[0].rearrange("(p k) -> p k", k=KT)).then_inc(c_in, 16)
                sp.dma_start(ctmp[:, KT:2 * KT], c_ctx.rearrange("(p k) -> p k", k=KT)).then_inc(c_in, 16)
            load(0)
            sp.dma_start(kc[:], consts[:, :]).then_inc(consts_in, 16)
            load(1)
            sp.dma_start(xt[:, 0:D], x[0, 0:P, :]).then_inc(x_first, 16)
            load(2)
            with nc.allow_non_contiguous_dma(reason="a few columns"):
                sp.dma_start(bcol[:].rearrange("p (v k) -> p v k", v=2),
                             b_ada[0, 0:2 * D].rearrange("(v p k) -> p v k", v=2, k=KT)).then_inc(cols_in, 16)
                for i, w in enumerate((norm1, norm2)):
                    sp.dma_start(ncol[:, i * DEPTH * KT:(i + 1) * DEPTH * KT].rearrange("p (l k) -> p l k", k=KT),
                                 w.rearrange("l (p k) -> p l k", k=KT)).then_inc(cols_in, 16)
            load(3)

            r = 4
            for l in range(DEPTH - 1):
                first = place[("d", l, LOOP_E - 2)]
                while r < first:
                    load(r)
                    r += 1
                with sp.Fori(0, (NE - LOOP_E) // BODY) as it:
                    for b in range(BODY):
                        e = BODY * it + (LOOP_E + b)
                        for n, (kind, src, back, seen) in enumerate((
                                ("d", -2, up_mm, -1),
                                ("g", 0, down_mm, -2),
                                ("u", 0, gate_mm, 0))):
                            q = r + 3 * b + n
                            sp.wait_ge(back, e + (l * NE + seen))
                            w = {"d": w_down, "g": w_gate, "u": w_up}[kind][l, bass.ds(e + src, 1)]
                            k = 4 if kind == "d" else KT
                            sp.dma_start(slot(q), w.rearrange("e (p k) n -> (e p) (k n)", k=k)
                                         ).then_inc(ring_in[q % NSLOT], 16)
                r += 3 * (NE - LOOP_E)
            while r < len(plan):
                load(r)
                r += 1

            for n, (kind, half_, dst, landed, _, _) in enumerate(PAIR_SLOTS):
                if kind == "u":
                    sp.wait_ge(pv_mm, item_no(DEPTH - 1, LT - 1, NI - 1) + 1)
                else:
                    freed(plan[R - NSLOT + (n if kind == "g" else n - 2)])
                sp.dma_start(dst, expert_weights(kind, DEPTH - 1, half_)).then_inc(landed, 16)
            with sp.Fori(0, PAIRS - 1) as it:
                for n, (kind, half_, dst, landed, _, read) in enumerate(PAIR_SLOTS):
                    older, loads = PAIR_SLOTS[n - 2][3:5]
                    wait_in_loop(sp, counts, c_in, 32, (read, it + (PAIR_BASE + 1)),
                                 (older, 16 * it + 16 * (loads + (2 if n >= 2 else 1))))
                    w = {"d": w_down, "g": w_gate, "u": w_up}[kind][DEPTH - 1, bass.ds(2 * it + (2 + half_), 1)]
                    k = 4 if kind == "d" else KT
                    sp.dma_start(dst, w.rearrange("e (p k) n -> (e p) (k n)", k=k)).then_inc(landed, 16)

        @block.gpsimd
        def _(pool):
            own = Steps(pool, pool_did)
            counts = [pool.alloc_register(f"pool_count{n}") for n in range(2)]

            def power(dst, src, n):
                return pool.tensor_tensor(dst, src, half[:, 0:n], ALU.pow)

            pool.memset(half[:], -0.5).then_inc(zeroed, 1)
            pool.memset(csil[:], 0.0).then_inc(zeroed, 1)
            pool.memset(qz[:], 0.0).then_inc(zeroed, 1)
            col = "(p k) -> p k"
            def projection_weights(l):
                with nc.allow_non_contiguous_dma(reason="a few columns"):
                    pool.dma_start(wuq[:].rearrange("p (k n) -> p k n", k=2),
                                   w_uq[l].rearrange("(p k) n -> p k n", k=2)).then_inc(wproj_in, 16)
                    pool.dma_start(wukv[:], w_ukv[l]).then_inc(wproj_in, 16)
                    pool.dma_start(gcol[:, 0:2], q_norm[l].rearrange(col, k=2)).then_inc(wproj_in, 16)
                    pool.dma_start(gcol[:, 2:3], kv_norm[l].rearrange(col, k=1)).then_inc(wproj_in, 16)
                    pool.dma_start(dgain[:], diff_norm[l].partition_broadcast(P)).then_inc(wproj_in, 16)
                    for n, v in enumerate((lam_q1, lam_k1, lam_q2, lam_k2)):
                        pool.dma_start(lamb[:, n * C_DH:(n + 1) * C_DH],
                                       v[l].partition_broadcast(P)).then_inc(wproj_in, 16)

            def later_inputs():
                pool.dma_start(sinkb[:, 0:DEPTH * A_HEADS],
                               sink.rearrange("l h -> (l h)").partition_broadcast(P)).then_inc(sink_in, 16)
                for i in range(2):
                    for l in range(DEPTH):
                        pool.dma_start(mod_s[l, i:i + 1, :], b_ada[l:l + 1, :]).then_inc(mod_init, 16)

            def modulation_columns(l, part):
                for n in range(2):
                    for i in range(2):
                        m = 3 * part + n
                        pool.dma_start(modc[:, ((2 * part + n) * 2 + i) * KT:((2 * part + n) * 2 + i + 1) * KT],
                                       mod_s[l, i, m * D:(m + 1) * D].rearrange(col, k=KT)).then_inc(modc_in, 16)

            def load_x(l, t):
                pool.dma_start(xt[:, (t % 2) * D:(t % 2 + 1) * D], tile_rows(l, t)).then_inc(x_in[t % 2], 16)

            def store_modulation(n):
                l, ch = ada_items[n][1:]
                pool.wait_ge(ada_out, n - ADA_FIRST + 1)
                if n == ADA_FIRST:
                    pool.wait_ge(mod_init, 64)
                pool.dma_start(mod_s[l, :, 512 * ch:512 * ch + 512], msum[0:2, :],
                               accum_op=ALU.add).then_inc(mod_stored, 16)

            def norm_power(n):
                pool.wait_ge(ms_done, n + 1)
                power(rstd[:, n % 2:n % 2 + 1], msq[:, n % 2:n % 2 + 1], 1).then_inc(rstd_done, 1)

            def tile_rows(l, t):
                if l:
                    return x_s[t * P:(t + 1) * P, :]
                return x[0, t * P:(t + 1) * P, :] if t < LT else ctx_in[0, (t - LT) * P:(t - LT + 1) * P, :]

            norms = 0
            for l in range(DEPTH):
                if l == 0:
                    norm_power(0)
                    load_x(0, 1)
                    projection_weights(0)
                    later_inputs()
                else:
                    pool.wait_ge(o_ev, item_no(0, NT - 1, NI - 1) + 1)
                    projection_weights(l)
                    modulation_columns(l, 0)
                for t in range(NT + 1):
                    if t < NT:
                        if l and t == 0:
                            pool.wait_ge(scattered, 16 * NE)
                        if norms + t >= 2:
                            pool.wait_ge(xhat, norms + t - 1)
                            load_x(l, t)
                        if norms + t:
                            norm_power(norms + t)
                    if t >= 1:
                        n = tile_no(l, t - 1)
                        pool.wait_ge(ms2_done, n + 1)
                        a = int(keys_only(l, t - 1))
                        power(rs2[:, a:2], ms2[:, a:2], 2 - a).then_inc(rs2_done, 1)
                norms += NT

                pool.wait_ge(zeroed, 3)
                pool.wait_ge(small_ev, small_count(l, NT - 1))
                def pad_queries(qi):
                    g = ATT.index((l, qi))
                    if g >= 2:
                        pl, pq = ATT[g - 2]
                        pool.wait_ge(s_mm, step_no(pl, pq, NS - 1) + 1)
                    z = qz[:, (g % 2) * 16 * P:(g % 2 + 1) * 16 * P].rearrange("p (h t) -> p h t", h=16)
                    cols = slice(qi * P, (qi + 1) * P)
                    for k in range(2):
                        own.did(pool.tensor_copy(z[64 * k:64 * k + 64, 4 * k:4 * k + 4, :],
                                                 qk_t[64 * k:64 * k + 64, B_AQ:B_AQ + 4, cols]))
                    for r in range(4):
                        last = pool.tensor_copy(z[32 * r:32 * r + 32, 8 + r:16:4, :],
                                                qk_t[32 * r:32 * r + 32, B_CQ:B_CQ + 2, cols])
                        if r < 3:
                            own.did(last)
                    last.then_inc(qz_done, 1)

                pad_queries(0)
                for qi in range(nq(l)):
                    g = ATT.index((l, qi))
                    if qi + 1 < nq(l):
                        pad_queries(qi + 1)
                    for j in range(NS):
                        n = ada_sum_at(l, qi, j)
                        if n is not None:
                            store_modulation(n)
                    pool.wait_ge(cms_done, g + 1)
                    power(crs, cms, 4).then_inc(crs_done, 1)

                pool.wait_ge(mod_stored, 16 * (len(ada_items) - ADA_FIRST))
                modulation_columns(l, 1)
                pool.wait_ge(otd_ev, len([a for a in ATT if a[0] <= l]))
                pool.wait_ge(ota_ev, len([a for a in ATT if a[0] <= l]))
                for i in range(2):
                    pool.dma_start(g1[:, i, :], mod_s[l, i, 2 * D:3 * D].partition_broadcast(P)).then_inc(g1_in, 16)
                pool.dma_start(wr[:].rearrange("p (k n) -> p k n", k=KT),
                               w_router[l].rearrange("(p k) n -> p k n", k=KT)).then_inc(g1_in, 16)
                for t in range(nq(l) + 1):
                    g = tile_no(l, t)
                    if t < nq(l):
                        pool.wait_ge(xhat, norms + max(0, t - 1))
                        if t >= 2:
                            pool.wait_ge(xs_stored, 16 * (g - 1))
                        pool.dma_start(xt[:, (t % 2) * D:(t % 2 + 1) * D], tile_rows(l, t)).then_inc(xo_in[t % 2], 16)
                    if t >= 1:
                        g = tile_no(l, t - 1)
                        b = (t - 1) % 2
                        pool.wait_ge(xo_done, g + 1)
                        pool.dma_start(x_s[(t - 1) * P:t * P, :], xt[:, b * D:(b + 1) * D]).then_inc(xs_stored, 16)
                        norm_power(norms + t - 1)
                        pool.wait_ge(xhat, norms + t)
                        pool.dma_start(h2_s[(t - 1) * P:t * P, :], hx[:]).then_inc(h2_stored, 16)
                norms += nq(l)

                pool.wait_ge(wo_mm, 2 * tile_no(l, nq(l) - 1) + 2)
                pool.dma_start(g2[0:CAP_L, :], mod_s[l, 0, 5 * D:6 * D].partition_broadcast(CAP_L)).then_inc(g2_in, 16)
                more, i = (CAP_C, 1) if nq(l) > LT else (CAP_L, 0)
                pool.dma_start(g2[CAP_L:CAP_L + more, :],
                               mod_s[l, i, 5 * D:6 * D].partition_broadcast(more)).then_inc(g2_in, 16)
                pool.wait_ge(h2_stored, 16 * (tile_no(l, nq(l) - 1) + 1))
                pool.wait_ge(xs_stored, 16 * (tile_no(l, nq(l) - 1) + 1))
                pool.wait_ge(gi_done, l + 1)
                rows = CAP_L + (CAP_C if nq(l) > LT else 0)

                def step(e, n, bidx, first):
                    if bidx < NE:
                        if not (l == 0 and first and bidx < 2):
                            pool.wait_ge(xgt_mm, n - 1)
                        if not (l == 0 and first and bidx < 4):
                            pool.wait_ge(scattered, (n - 3) * 16)
                        ic = ix[0:rows, bidx % 4:bidx % 4 + 1]
                        ins = pool.tensor_copy(ic, gidx[0:rows, bass.ds(e, 1)])
                        ins.then_inc(pool_did, 1)
                        own.n += 1
                        wait_in_loop(pool, counts, gi_done, l + 1, (pool_did, own.base + own.n))
                        pool.indirect_dma_start(
                            out=xg[bidx % 2][0:rows, :], out_offset=None, in_=h2_s[:, :],
                            in_offset=bass.IndirectOffsetOnAxis(ap=ic, axis=0)).then_inc(xg_in[bidx % 2], 16)
                    if not first or bidx >= 3:
                        before = [] if l == 0 and first and bidx == 3 else [(scattered, (n - 3) * 16)]
                        wait_in_loop(pool, counts, gi_done, l + 1, (y_done, n - 2), *before)
                        pool.indirect_dma_start(
                            out=x_s[:, :],
                            out_offset=bass.IndirectOffsetOnAxis(
                                ap=ix[0:rows, (bidx - 3) % 4:(bidx - 3) % 4 + 1], axis=0),
                            in_=y[(bidx - 3) % 2][0:rows, :], in_offset=None, compute_op=ALU.add
                        ).then_inc(scattered, 16)

                if l == DEPTH - 1:
                    break
                for e in range(LOOP_E):
                    step(e, l * NE + e, e, True)
                start = own.n
                with pool.Fori(0, (NE - LOOP_E) // BODY) as it:
                    own.base = it * BODY
                    for b in range(BODY):
                        e = BODY * it + (LOOP_E + b)
                        step(e, e + l * NE, LOOP_E + b, False)
                own.base, own.n = 0, start + NE - LOOP_E
                for e in range(NE, NE + 3):
                    step(e, l * NE + e, e, False)

            def gather(p):
                ic = ix[:, 2 * p:2 * p + 1]
                pool.tensor_copy(ic, gidx[:, p:p + 1])
                own.did(pool.tensor_copy(ix[0:CAP_L, 2 * p + 1:2 * p + 2], gidx[0:CAP_L, PAIRS + p:PAIRS + p + 1]))
                pool.wait_ge(xgt_mm, PAIR_BASE + p - 1)
                pool.indirect_dma_start(
                    out=xg[p % 2], out_offset=None, in_=h2_s[:, :],
                    in_offset=bass.IndirectOffsetOnAxis(ap=ic, axis=0)).then_inc(xg_in[p % 2], 16)

            def scatter(p):
                for h in range(2):
                    pool.wait_ge(y_done, PAIR_BASE + p + 1)
                    pool.wait_ge(scattered, 16 * (PAIR_BASE + 2 * p + h))
                    pool.indirect_dma_start(
                        out=x_s[:, :],
                        out_offset=bass.IndirectOffsetOnAxis(ap=ix[0:CAP_L, 2 * p + h:2 * p + h + 1], axis=0),
                        in_=y[p % 2][CAP_L * h:CAP_L * (h + 1), :], in_offset=None, compute_op=ALU.add
                    ).then_inc(scattered, 16)

            gather(0)
            gather(1)
            for p in range(PAIRS):
                scatter(p)
                if p + 2 < PAIRS:
                    gather(p + 2)

            pool.wait_ge(at_ev, tile_no(DEPTH - 1, LT - 1) + 1)
            pool.wait_ge(gt_mm, DEPTH)
            pool.dma_start(fgain, final_norm.partition_broadcast(P)).then_inc(g1_in, 16)
            pool.wait_ge(scattered, 16 * NE * DEPTH)
            for t in range(LT + 1):
                if t < LT:
                    if t >= 2:
                        pool.wait_ge(out_stored, 16 * (t - 1))
                    pool.dma_start(xt[:, (t % 2) * D:(t % 2 + 1) * D], x_s[t * P:(t + 1) * P, :]
                                   ).then_inc(x_in[t % 2], 16)
                    norm_power(norms + t)
                if t >= 1:
                    b = (t - 1) % 2
                    pool.wait_ge(out_done, t)
                    pool.dma_start(out[0, (t - 1) * P:t * P, :], xt[:, b * D:(b + 1) * D]).then_inc(out_stored, 16)
            pool.wait_ge(out_stored, 16 * LT)

        @block.scalar
        def _(act):
            own = Steps(act, act_did)

            act.wait_ge(c_in, 32)
            act.activation(ctmp[:, 16:32], ctmp[:, 0:16], ACT.Exp, scale=-1.0).then_inc(csil_e, 1)

            def ada_evacuate(n):
                act.wait_ge(ada_sum, n + 1)
                if n > ADA_FIRST:
                    act.wait_ge(mod_stored, 16 * (n - ADA_FIRST))
                act.copy(msum[0:2, :], ps[0:2, 7, :]).then_inc(ada_out, 1)

            def lambda_exps(l):
                act.wait_ge(lam_p, l + 1)
                act.activation(lamb[:, 4 * C_DH + 2:4 * C_DH + 4], lamb[:, 4 * C_DH:4 * C_DH + 2],
                               ACT.Exp).then_inc(lam_e, 1)

            norms = 0
            for l in range(DEPTH):
                def square(t):
                    wait_x(act, tile_no(l, t))
                    if norms + t >= 2:
                        act.wait_ge(ms_done, norms + t - 1)
                    if norms + t >= 1:
                        act.wait_ge(xhat, norms + t)
                        act.wait_ge(t1_mm, norms + t)
                    if l and t == 0:
                        act.wait_ge(h2_stored, 16 * tile_no(0, NT))
                    act.activation(hx[:], xt[:, (t % 2) * D:(t % 2 + 1) * D], ACT.Square,
                                   accum_out=ss[:, (norms + t) % 2:(norms + t) % 2 + 1]).then_inc(sumsq, 1)

                def main_evacuate(t, ch):
                    n = tile_no(l, t)
                    p = pt[n % 2]
                    if ch == 0 and n >= 2:
                        act.wait_ge(small_mm, small_count(*tile_before(l, t, 2)))
                    if chunk_cols(l, t, ch)[0] == chunk_cols(l, t, ch)[1]:
                        return
                    act.wait_ge(main_mm, main_count(l, t, ch))
                    if ch == 0 and l and t < 2:
                        act.wait_ge(gt_mm, l)
                    if l and t == 0 and ch == 1:
                        act.wait_ge(down_mm, l * NE)
                        act.wait_ge(scattered, 16 * NE * l)
                    src = ps[:, ch, :]
                    if ch == 0:
                        last = act.copy(p[:, QA:KA].rearrange("p (h k d) -> p k h d", k=2, d=HD),
                                        src.rearrange("p (k h d) -> p k h d", k=2, d=HD))
                    elif ch == 1:
                        act.copy(p[:, KA:VA], src[:, 0:VA - 512])
                        last = act.copy(va[:, t, :], src[:, VA - 512:CQ - 512])
                        if not keys_only(l, t):
                            last = act.copy(p[:, CQ:CKV], src[:, CQ - 512:512])
                    elif ch == 2:
                        b = chunk_cols(l, t, ch)[1]
                        last = act.copy(p[:, CKV:b], src[:, 0:b - CKV])
                    else:
                        act.copy(p[:, KD:VD], src[:, 0:VD - KD])
                        last = act.copy(vc[:, t, :], src[:, VD - KD:512])
                    last.then_inc(main_ev, 1)

                def squares2(t):
                    n = tile_no(l, t)
                    p = pt[n % 2]
                    act.wait_ge(main_ev, main_count(l, t, 3))
                    if n >= 1:
                        act.wait_ge(ms2_done, n)
                        act.wait_ge(sq2, n)
                    last = act.activation(ps[:, 3, 256:384], p[:, CKV:KR], ACT.Square, accum_out=ss2[:, 1:2])
                    if not keys_only(l, t):
                        last = act.activation(ps[:, 3, 0:256], p[:, CQ:CKV], ACT.Square, accum_out=ss2[:, 0:1])
                    last.then_inc(sq2, 1)

                def small_evacuate(t, u):
                    if u not in small_uses(l, t):
                        return
                    n = tile_no(l, t)
                    act.wait_ge(small_mm, small_count(l, t, u))
                    src = ps[:, 6 + u % 2, :]
                    cols = slice(t * P, (t + 1) * P)
                    if u == 0:
                        if t == 0:
                            act.wait_ge(wproj_in, 16 * 9 * (l + 1))
                        if n >= 1:
                            act.wait_ge(small_mm, small_count(*tile_before(l, t), 2))
                        for k in range(2 if keys_only(l, t) else 0, 3):
                            last = act.activation(c_t[:, k, :], src[:, k * P:(k + 1) * P], ACT.Identity,
                                                  scale=gcol[:, k:k + 1])
                    elif u == 1:
                        if n >= 1:
                            act.wait_ge(small_mm, small_count(*tile_before(l, t)))
                        last = act.copy(q96, src[:, 0:384].rearrange("p (h d) -> p h d", h=B_HEADS))
                    elif u == 2:
                        if keys_only(l, t):
                            act.wait_ge(small_mm, small_count(*tile_before(l, t)))
                        kv = src.rearrange("p (h d) -> p h d", h=B_HEADS)
                        act.copy(k96[:, :, 0:B_NOPE], kv[:, :, 0:B_NOPE])
                        last = act.copy(vb[:, t, :].rearrange("p (h d) -> p h d", h=B_HEADS), kv[:, :, B_NOPE:])
                    else:
                        b0, nb, rows = [(0, 4, P), (4, 4, P), (8, 1, P), (9, 4, B_QK), (13, 4, B_QK)][u - 3]
                        gap = 3 if u == 4 and keys_only(l, t) else 1
                        last = act.copy(qk_t[0:rows, b0:b0 + nb:gap, cols],
                                        src[0:rows, 0:nb * P].rearrange("p (b t) -> p b t", b=nb)[:, ::gap, :])
                    last.then_inc(small_ev, 1)

                square(0)
                lambda_exps(l)
                for t in range(NT + 1):
                    if t + 1 < NT:
                        square(t + 1)
                    for ch in range(NCH):
                        if t < NT:
                            main_evacuate(t, ch)
                        if t >= 1:
                            if ch == 0:
                                small_evacuate(t - 1, 0)
                            elif ch == 1:
                                small_evacuate(t - 1, 1)
                                small_evacuate(t - 1, 2)
                            elif ch == 2:
                                for u in range(3, 8):
                                    small_evacuate(t - 1, u)
                        if t < NT and ch == 3:
                            squares2(t)
                norms += NT

                def softmax(s):
                    ll, qi, j = s
                    n = step_no(ll, qi, j)
                    kind, h, m = STEPS[j]
                    kt = key_tiles(ll, qi, kind)
                    c0, c1 = kt[0][1], TOK
                    scale = {"A": HD, "B": B_QK, "C": C_DH}[kind] ** -0.5
                    act.wait_ge(neg_done, n + 1)
                    if n >= 3:
                        pl, pq, pj = sprev(s, 3)
                        act.wait_ge(t_mm, item_no(pl, pq, ITEM[pj]) + 1)
                    act.activation(prob[n % 3][:, c0:c1], bank(2 * (n % 2), 2)[:, c0:c1], ACT.Exp,
                                   bias=negm[:, j:j + 1], scale=scale,
                                   accum_out=sums[:, j:j + 1]).then_inc(exp_done, 1)
                    if kind == "A":
                        act.activation(esink[:, h:h + 1], sinkb[:, ll * A_HEADS + h:ll * A_HEADS + h + 1], ACT.Exp,
                                       bias=negm[:, j:j + 1]).then_inc(sink_e, 1)

                seq = [(l, qi, j) for qi in range(nq(l)) for j in range(NS)]

                def sprev(s, k):
                    full = [(a, b, jj) for a, b in ATT for jj in range(NS)]
                    return full[full.index(s) - k]

                def output_half(qi):
                    g = ATT.index((l, qi))
                    act.wait_ge(ot_mm, g + 1)
                    for b in range(4):
                        last = act.copy(qk_t[:, OT_BLOCK[b], qi * P:(qi + 1) * P], bank(4)[:, b * P:(b + 1) * P])
                    last.then_inc(ota_ev, 1)

                softmax(seq[0])
                softmax(seq[1])
                for k, s in enumerate(seq):
                    _, qi, j = s
                    kind = STEPS[j][0]
                    if k + 2 < len(seq) and kind == "C":
                        softmax(seq[k + 2])
                    if LASTSTEP[j]:
                        i = item_no(l, qi, ITEM[j])
                        nb = len(key_tiles(l, qi, kind)) // 2
                        act.wait_ge(t_mm, i + 1)
                        if i >= 2:
                            act.wait_ge(pv_mm, i - 1)
                        act.copy(prob_t[i % 2][:, 0:nb, :],
                                 bank(4)[:, 0:nb * P].rearrange("p (b t) -> p b t", b=nb)).then_inc(pta_ev, 1)
                    if k + 2 < len(seq) and kind != "C":
                        softmax(seq[k + 2])
                    if qi and LASTSTEP[j] and ITEM[j] == OT_AFTER:
                        output_half(qi - 1)
                    n = ada_sum_at(l, qi, j)
                    if n is not None:
                        ada_evacuate(n)
                output_half(nq(l) - 1)

                def square_o(t):
                    n = norms + t
                    act.wait_ge(xo_done, tile_no(l, t) + 1)
                    act.wait_ge(ms_done, n - 1)
                    act.wait_ge(t1_mm, n)
                    if t:
                        act.wait_ge(h2_stored, 16 * tile_no(l, t))
                    act.activation(hx[:], xt[:, (t % 2) * D:(t % 2 + 1) * D], ACT.Square,
                                   accum_out=ss[:, n % 2:n % 2 + 1]).then_inc(sumsq, 1)

                def router_exp(t):
                    act.wait_ge(rmax_done, tile_no(l, t) + 1)
                    act.activation(aff_e, ps[:, 6, 0:NE], ACT.Exp, bias=rmx, accum_out=rsum).then_inc(rexp_done, 1)

                def affinity_store(t):
                    g = tile_no(l, t)
                    act.wait_ge(at_mm, g + 1)
                    act.copy(rtop[0:NE, t * P:(t + 1) * P], ps[0:NE, 7, 0:P]).then_inc(at_ev, 1)

                for t in range(nq(l)):
                    square_o(t)
                    router_exp(t)
                    affinity_store(t)
                norms += nq(l)
                rows = CAP_L + (CAP_C if nq(l) > LT else 0)
                act.wait_ge(gt_mm, l + 1)
                if l:
                    act.wait_ge(y_done, NE)
                if l == DEPTH - 1:
                    act.copy(gval[0:CAP_L, 0:PAIRS], ps[0:CAP_L, 6, 0:NE:2])
                    act.copy(gval[CAP_L:P, 0:PAIRS], ps[CAP_L:P, 6, 1:NE:2]).then_inc(gv_done, 1)
                    break
                act.copy(gval[0:rows, :], ps[0:rows, 6, 0:NE]).then_inc(gv_done, 1)

                def step(n, b, first):
                    if b < NE:
                        act.wait_ge(gate_mm, n + 1)
                        if not (l == 0 and first and b == 0):
                            act.wait_ge(hid_done, n)
                        act.activation(sg[0:rows, :], ps[0:rows, 2, :], ACT.Silu).then_inc(silu_done, 1)
                    if not first or b >= 1:
                        act.wait_ge(hidt_mm, n)
                        if not (l == 0 and first and b < 3):
                            act.wait_ge(down_mm, n - 2)
                        act.copy(hid_t[(b - 1) % 2][:, :, 0:rows],
                                 ps[:, 4, 0:4 * rows].rearrange("p (k t) -> p k t", k=4)).then_inc(hidt_ev, 1)

                for e in range(LOOP_E):
                    step(l * NE + e, e, True)
                with act.Fori(0, (NE - LOOP_E) // BODY) as it:
                    for b in range(BODY):
                        step(BODY * it + (l * NE + LOOP_E + b), LOOP_E + b, False)
                step(l * NE + NE, NE, False)

            with act.Fori(0, PAIRS // 2) as it:
                for b in range(2):
                    n = 2 * it + (PAIR_BASE + b)
                    act.wait_ge(gate_mm, n + 1)
                    act.wait_ge(hid_done, n)
                    act.activation(sg, ps[:, 2, :], ACT.Silu).then_inc(silu_done, 1)
                    act.wait_ge(hidt_mm, n + 1)
                    act.wait_ge(down_mm, n - 1)
                    act.copy(hid_t[b], ps[:, 4, :].rearrange("p (k t) -> p k t", k=4)).then_inc(hidt_ev, 1)

            for t in range(LT):
                n = norms + t
                wait_x(act, DEPTH * NT + t)
                act.wait_ge(ms_done, n - 1)
                act.wait_ge(xhat, n) if t == 0 else None
                act.wait_ge(t1_mm, norms) if t == 0 else None
                act.wait_ge(h2_stored, 16 * (tile_no(DEPTH - 1, LT - 1) + 1))
                if t:
                    act.wait_ge(sumsq, n)
                act.activation(hx[:], xt[:, (t % 2) * D:(t % 2 + 1) * D], ACT.Square,
                               accum_out=ss[:, n % 2:n % 2 + 1]).then_inc(sumsq, 1)

        @block.vector
        def _(dve):
            own = Steps(dve, dve_did)

            dve.wait_ge(csil_e, 1)
            own.did(dve.tensor_scalar(ctmp[:, 16:32], ctmp[:, 16:32], 1.0, None, ALU.add))
            own.did(dve.reciprocal(ctmp[:, 32:48], ctmp[:, 16:32]))
            dve.wait_ge(zeroed, 2)
            dve.tensor_tensor(csil[:].rearrange("p (k i) -> p k i", k=KT)[:, :, 0:2],
                              ctmp[:, 0:16].rearrange("p (i k) -> p k i", i=2),
                              ctmp[:, 32:48].rearrange("p (i k) -> p k i", i=2), ALU.mult).then_inc(csil_done, 1)
            NSK = DEPTH * A_HEADS

            def ada_copy(n):
                dve.wait_ge(ada_mm, n + 1)
                if n >= 1:
                    dve.wait_ge(ada_sum, n)
                dve.tensor_copy(modrow[:], ps[:, 7, :]).then_inc(ada_row, 1)

            def lambda_products(l):
                dve.wait_ge(wproj_in, 16 * 9 * (l + 1))
                q = lamb[:, 0:4 * C_DH].rearrange("p (n d) -> p n d", n=4)
                s = lamb[:, 4 * C_DH:]
                own.did(dve.tensor_tensor(q[:, 0:4:2, :], q[:, 0:4:2, :], q[:, 1:4:2, :], ALU.mult))
                dve.tensor_reduce(s[:, 0:2], q[:, 0:4:2, :], AX_X, ALU.add).then_inc(lam_p, 1)
                dve.wait_ge(lam_e, l + 1)
                own.did(dve.tensor_tensor(s[:, 4:5], s[:, 3:4], s[:, 2:3], ALU.subtract))
                own.did(dve.tensor_scalar(s[:, 5:6], s[:, 4:5], -lam_init(l), None, ALU.add))
                own.did(dve.tensor_scalar(dgain[:], dgain[:], 1.0 - lam_init(l), None, ALU.mult))

            neg_lam = lamb[:, 4 * C_DH + 5:4 * C_DH + 6]
            mc = modc[:].rearrange("p (v i k) -> p v i k", v=4, i=2)

            def first_columns(n):
                dve.wait_ge(ada_sum, n + 1)
                rows, v = slice(64 * (n % 2), 64 * (n % 2) + 64), n // 2
                dve.tensor_tensor(mc[rows, v].rearrange("p i k -> p k i"),
                                  ps[rows, 6, 0:2 * KT].rearrange("p (k i) -> p k i", i=2),
                                  bcol[rows, v * KT:(v + 1) * KT].unsqueeze(2).to_broadcast([64, KT, 2]), ALU.add
                                  ).then_inc(first_cols, 1)

            def modulation(l, part):
                if l or part:
                    dve.wait_ge(modc_in, 16 * 4 * (2 * l + part))
                else:
                    dve.wait_ge(first_cols, ADA_FIRST)
                gain = ncol[:, (2 * part + l) * KT:(2 * part + l + 1) * KT].unsqueeze(1).to_broadcast([P, 2, KT])
                dve.scalar_tensor_tensor(out=mc[:, 2 * part + 1], in0=mc[:, 2 * part + 1], scalar=1.0, in1=gain,
                                         op0=ALU.add, op1=ALU.mult).then_inc(modc_done, 1)
                dve.wait_ge(modc_done, 2 * l + part + 1)

            def mean_square(n):
                dve.wait_ge(sumsq, n + 1)
                if n >= 2:
                    dve.wait_ge(rstd_done, n - 1)
                dve.tensor_scalar(msq[:, n % 2:n % 2 + 1], ss[:, n % 2:n % 2 + 1], 1.0 / D, EPS,
                                  ALU.mult, ALU.add).then_inc(ms_done, 1)

            def normalise(n, buf, dst):
                dve.wait_ge(rstd_done, n + 1)
                return dve.tensor_scalar(dst, xt[:, buf * D:(buf + 1) * D], rstd[:, n % 2:n % 2 + 1], None, ALU.mult)

            def modulate(dst, src, part, i, width):
                a = mc[:, 2 * part + 1, i, :].unsqueeze(2).to_broadcast([P, KT, width])
                b = mc[:, 2 * part, i, :].unsqueeze(2).to_broadcast([P, KT, width])
                own.did(dve.tensor_tensor(dst, src, a, ALU.mult))
                return dve.tensor_tensor(dst, dst, b, ALU.add)

            def rope(v, units, nf, cos, sin):
                w = 4 * nf
                vv = v.rearrange("p (u w) -> p u w", w=w)
                v4 = v.rearrange("p (u a r f) -> p u a r f", a=2, r=2, f=nf)
                tm = rtmp[:, 0:units * w].rearrange("p (u a r f) -> p u a r f", a=2, r=2, f=nf)
                s4 = sin.rearrange("p (a r f) -> p a r f", a=2, r=2)
                for r in range(2):
                    own.did(dve.tensor_tensor(tm[:, :, :, r, :], v4[:, :, :, 1 - r, :],
                                              s4[:, :, r, :].unsqueeze(1).to_broadcast([P, units, 2, nf]), ALU.mult))
                own.did(dve.tensor_tensor(vv, vv, cos.unsqueeze(1).to_broadcast([P, units, w]), ALU.mult))
                return dve.tensor_tensor(v, v, rtmp[:, 0:units * w], ALU.add)

            norms = 0
            for l in range(DEPTH):
                def prepare(t):
                    n = norms + t
                    mean_square(n)
                    if n >= 1:
                        dve.wait_ge(t1_mm, n)
                    if l and t == 0:
                        dve.wait_ge(h2_stored, 16 * tile_no(0, NT))
                    normalise(n, t % 2, hx[:]).then_inc(xhat, 1)

                def modulated(t):
                    n = tile_no(l, t)
                    dve.wait_ge(t1_mm, norms + t + 1)
                    if n >= 2:
                        dve.wait_ge(main_mm, main_count(*tile_before(l, t, 2), 3))
                    if l and t < 2:
                        dve.wait_ge(gt_mm, l)
                    modulate(h_t[n % 2], bank(4, 2).rearrange("p (k t) -> p k t", k=KT), 0, int(t >= LT),
                             P).then_inc(h_done, 1)

                def finish_b(t):
                    n = tile_no(l, t)
                    p = pt[n % 2]
                    dve.wait_ge(small_ev, small_count(l, t, 2))
                    if t < LT:
                        tm = rtmp[:, 0:B_HEADS * B_ROPE].rearrange("p (h a r f) -> p h a r f", a=2, r=2, f=8)
                        cos = kc[:, K_CB + t * 32:K_CB + t * 32 + 32]
                        sin = kc[:, K_SB + t * 32:K_SB + t * 32 + 32].rearrange("p (a r f) -> p a r f", a=2, r=2)
                        qr = q96[:, :, B_NOPE:]
                        q5 = qr.rearrange("p h (a r f) -> p h a r f", a=2, r=2)
                        for r in range(2):
                            own.did(dve.tensor_tensor(
                                tm[:, :, :, r, :], q5[:, :, :, 1 - r, :],
                                sin[:, :, r, :].unsqueeze(1).to_broadcast([P, B_HEADS, 2, 8]), ALU.mult))
                        own.did(dve.tensor_tensor(qr, qr, cos.unsqueeze(1).to_broadcast([P, B_HEADS, 32]), ALU.mult))
                        own.did(dve.tensor_tensor(
                            qr, qr, rtmp[:, 0:B_HEADS * B_ROPE].rearrange("p (h d) -> p h d", h=B_HEADS), ALU.add))
                    dve.tensor_copy(k96[:, :, B_NOPE:], p[:, KR:QD].unsqueeze(1).to_broadcast([P, B_HEADS, B_ROPE])
                                    ).then_inc(rope_b, 1)

                def finish_main(t):
                    n = tile_no(l, t)
                    p = pt[n % 2]
                    dve.wait_ge(sq2, n + 1)
                    if n >= 1:
                        dve.wait_ge(rs2_done, n)
                    if not keys_only(l, t):
                        dve.tensor_scalar(ms2[:, 0:1], ss2[:, 0:1], 1.0 / B_QR, EPS, ALU.mult, ALU.add)
                    dve.tensor_scalar(ms2[:, 1:2], ss2[:, 1:2], 1.0 / B_KVR, EPS, ALU.mult, ALU.add
                                      ).then_inc(ms2_done, 1)
                    dve.wait_ge(rs2_done, n + 1)
                    if not keys_only(l, t):
                        dve.tensor_scalar(p[:, CQ:CKV], p[:, CQ:CKV], rs2[:, 0:1], None, ALU.mult)
                    dve.tensor_scalar(p[:, CKV:KR], p[:, CKV:KR], rs2[:, 1:2], None, ALU.mult).then_inc(cqn, 1)
                    if t < LT:
                        own.did(rope(p[:, QA:VA], A_HEADS + A_KV, 16, kc[:, K_CA + t * 64:K_CA + t * 64 + 64],
                                     kc[:, K_SA + t * 64:K_SA + t * 64 + 64]))
                    dve.wait_ge(main_ev, main_count(l, t, 3))
                    if t < LT:
                        rope(p[:, KR:VD], 1 + 2 * 2 * C_HEADS, 8, kc[:, K_CB + t * 32:K_CB + t * 32 + 32],
                             kc[:, K_SB + t * 32:K_SB + t * 32 + 32]).then_inc(rope_ac, 1)
                        dve.wait_ge(rope_ac, n + 1)
                    else:
                        dve.tensor_copy(rtmp[:, 0:2], p[:, KR:KR + 2]).then_inc(rope_ac, 1)
                        dve.wait_ge(rope_ac, n + 1)

                if l == 0:
                    for n in range(ADA_FIRST):
                        ada_copy(n)
                        if n == 0:
                            dve.wait_ge(cols_in, 16 * 3)
                        first_columns(n)
                        if n == 1:
                            prepare(0)
                else:
                    prepare(0)
                modulation(l, 0)
                modulated(0)
                lambda_products(l)
                if l == 0:
                    dve.wait_ge(sink_in, 16)
                    own.did(dve.tensor_scalar(sinkb[:, NSK:2 * NSK], sinkb[:, 0:NSK], -1.0, None, ALU.mult))
                for t in range(NT + 1):
                    if t + 1 < NT:
                        prepare(t + 1)
                    if t >= 1:
                        finish_b(t - 1)
                    if t + 1 < NT:
                        modulated(t + 1)
                    if t < NT:
                        finish_main(t)
                norms += NT

                NSKL = NSK + l * A_HEADS

                def row_max(s):
                    _, qi, j = s
                    n = step_no(l, qi, j)
                    kind, h, m = STEPS[j]
                    kt = key_tiles(l, qi, kind)
                    c0 = kt[0][1]
                    scale = {"A": HD, "B": B_QK, "C": C_DH}[kind] ** -0.5
                    sc = bank(2 * (n % 2), 2)
                    dve.wait_ge(s_mm, n + 1)
                    if kind == "A" and qi < LT:
                        if 0 < qi < LT - 1:
                            v = sc[:, 0:512].rearrange("p (b t) -> p b t", b=4)[:, 1:4:2, :]
                            mk = kc[:, K_MASK:K_MASK + 2 * P].rearrange("p (b t) -> p b t", b=2)
                        elif qi:
                            v, mk = sc[:, c0:c0 + P], kc[:, K_MASK:K_MASK + P]
                        else:
                            v, mk = sc[:, SEQ - P:SEQ], kc[:, K_MASK + P:K_MASK + 2 * P]
                        own.did(dve.tensor_tensor(v, v, mk, ALU.add))
                    own.did(dve.tensor_reduce(mx[:, 0:1], sc[:, c0:TOK], AX_X, ALU.max))
                    if kind == "A":
                        dve.tensor_scalar(negm[:, j:j + 1], mx[:, 0:1], -scale, sinkb[:, NSKL + h:NSKL + h + 1],
                                          ALU.mult, ALU.min).then_inc(neg_done, 1)
                    else:
                        dve.tensor_scalar(negm[:, j:j + 1], mx[:, 0:1], -scale, None, ALU.mult).then_inc(neg_done, 1)

                seq = [(l, qi, j) for qi in range(nq(l)) for j in range(NS)]
                def finish_item(s):
                    _, qi, j = s
                    g = ATT.index((l, qi))
                    kind, h, m = STEPS[j]
                    i = ITEM[j]
                    it = item_no(l, qi, i)
                    if kind == "A":
                        dve.wait_ge(sink_e, A_HEADS * (l * NT + qi) + h + 1)
                        own.did(dve.tensor_tensor(tot[:, h:h + 1], sums[:, j:j + 1], esink[:, h:h + 1], ALU.add))
                        own.did(dve.reciprocal(rinv[:, i:i + 1], tot[:, h:h + 1]))
                    elif kind == "B":
                        own.did(dve.reciprocal(rinv[:, i:i + 1], sums[:, j:j + 1]))
                    else:
                        own.did(dve.reciprocal(rinv[:, i:i + 1], sums[:, j - 1:j]))
                    dve.wait_ge(pv_mm, it + 1)
                    if i == 0 and g >= 2:
                        dve.wait_ge(ot_mm, g - 1)
                    dve.tensor_scalar(ob[g % 2][:, i * 64:(i + 1) * 64], ps[:, 6, 0:64], rinv[:, i:i + 1], None,
                                      ALU.mult).then_inc(o_ev, 1)

                def norm_c(qi):
                    g = ATT.index((l, qi))
                    dve.wait_ge(o_ev, item_no(l, qi, NI - 1) + 1)
                    oc = ob[g % 2][:, 768:1024].rearrange("p (h d) -> p h d", h=C_HEADS)
                    cq3 = csq.rearrange("p (h d) -> p h d", h=C_HEADS)
                    own.did(dve.tensor_tensor(cq3, oc, oc, ALU.mult))
                    own.did(dve.tensor_reduce(css, cq3, AX_X, ALU.add))
                    dve.tensor_scalar(cms, css, 1.0 / C_V, EPS, ALU.mult, ALU.add).then_inc(cms_done, 1)
                    own.did(dve.tensor_tensor(oc, oc, dgain[:].unsqueeze(1).to_broadcast([P, C_HEADS, C_V]),
                                              ALU.mult))
                    dve.wait_ge(crs_done, g + 1)
                    dve.tensor_tensor(oc, oc, crs.unsqueeze(2).to_broadcast([P, C_HEADS, C_V]), ALU.mult
                                      ).then_inc(on_done, 1)

                def output_half(qi):
                    g = ATT.index((l, qi))
                    dve.wait_ge(ot_mm, g + 1)
                    for b in range(4, 8):
                        last = dve.tensor_copy(qk_t[:, OT_BLOCK[b], qi * P:(qi + 1) * P],
                                               bank(5)[:, (b - 4) * P:(b - 3) * P])
                    last.then_inc(otd_ev, 1)

                row_max(seq[0])
                row_max(seq[1])
                waiting = None
                for k, s in enumerate(seq):
                    _, qi, j = s
                    n = step_no(l, qi, j)
                    kind, h, m = STEPS[j]
                    it = item_no(l, qi, ITEM[j])
                    if kind == "C" and m == 1:
                        dve.wait_ge(exp_done, n + 1)
                        own.did(dve.reciprocal(r1[:, h:h + 1], sums[:, j:j + 1]))
                        own.did(dve.scalar_tensor_tensor(out=cc[:, h:h + 1], in0=sums[:, j - 1:j], scalar=r1[:, h:h + 1],
                                                         in1=neg_lam, op0=ALU.mult, op1=ALU.mult))
                        c0 = key_tiles(l, qi, kind)[0][1]
                        dve.scalar_tensor_tensor(out=prob[(n - 1) % 3][:, c0:TOK], in0=prob[n % 3][:, c0:TOK],
                                                 scalar=cc[:, h:h + 1], in1=prob[(n - 1) % 3][:, c0:TOK],
                                                 op0=ALU.mult, op1=ALU.add).then_inc(comb, 1)
                    if k + 2 < len(seq):
                        row_max(seq[k + 2])
                    if LASTSTEP[j]:
                        nb = len(key_tiles(l, qi, kind))
                        a = nb // 2
                        dve.wait_ge(t_mm, it + 1)
                        if it >= 2:
                            dve.wait_ge(pv_mm, it - 1)
                        dve.tensor_copy(prob_t[it % 2][:, a:nb, :],
                                        bank(5)[:, 0:(nb - a) * P].rearrange("p (b t) -> p b t", b=nb - a)
                                        ).then_inc(ptd_ev, 1)
                        if waiting:
                            finish_item(waiting)
                            if waiting[2] == NS - 1:
                                norm_c(waiting[1])
                        waiting = s
                        if qi and ITEM[j] == OT_AFTER:
                            output_half(qi - 1)
                    a = ada_at(l, qi, j)
                    if a is not None:
                        ada_copy(a)
                finish_item(waiting)
                norm_c(waiting[1])
                output_half(nq(l) - 1)

                modulation(l, 1)
                dve.wait_ge(g1_in, 16 * 3 * (l + 1))

                for t in range(nq(l)):
                    g = tile_no(l, t)
                    n = norms + t
                    dve.wait_ge(xo_in[t % 2], 16 * (g // 2 + 1))
                    x2 = xt[:, (t % 2) * D:(t % 2 + 1) * D]
                    for h in range(2):
                        dve.wait_ge(wo_mm, 2 * g + h + 1)
                        own.did(dve.tensor_tensor(tmpo, ps[:, 2 * (g % 2) + h, :],
                                                  g1[:, int(t >= LT), h * 512:(h + 1) * 512], ALU.mult))
                        last = dve.tensor_tensor(x2[:, h * 512:(h + 1) * 512], x2[:, h * 512:(h + 1) * 512], tmpo,
                                                 ALU.add)
                        if h == 0:
                            own.did(last)
                        else:
                            last.then_inc(xo_done, 1)
                            dve.wait_ge(xo_done, g + 1)
                    mean_square(n)
                    normalise(n, t % 2, hx[:]).then_inc(xhat, 1)
                    dve.wait_ge(t1_mm, n + 1)
                    if t:
                        dve.wait_ge(lg_mm, g)
                    modulate(h2_t, bank(4, 2).rearrange("p (k t) -> p k t", k=KT), 1, int(t >= LT),
                             P).then_inc(h_done, 1)
                    dve.wait_ge(lg_mm, g + 1)
                    own.did(dve.tensor_reduce(rmx, ps[:, 6, 0:NE], AX_X, ALU.max))
                    dve.tensor_scalar(rmx, rmx, -1.0, None, ALU.mult).then_inc(rmax_done, 1)
                    dve.wait_ge(rexp_done, g + 1)
                    own.did(dve.reciprocal(rrec, rsum))
                    if t:
                        dve.wait_ge(at_mm, g)
                    dve.tensor_scalar(aff, aff_e, rrec, None, ALU.mult).then_inc(aff_done, 1)
                norms += nq(l)

                rows = CAP_L + (CAP_C if nq(l) > LT else 0)
                dve.wait_ge(at_ev, tile_no(l, nq(l) - 1) + 1)
                sets = [(0, SEQ, 0, CAP_L)] + ([(SEQ, TOK, CAP_L, CAP_C)] if nq(l) > LT else [])
                for a, b, c0, cap in sets:
                    for r in range(cap // 8):
                        o8 = slice(c0 + 8 * r, c0 + 8 * r + 8)
                        own.did(dve.max(sval[0:NE, o8], rtop[0:NE, a:b]))
                        own.did(dve.max_index(sidx[0:NE, o8], sval[0:NE, o8], rtop[0:NE, a:b]))
                        own.did(dve.match_replace(rtop[0:NE, a:b], sval[0:NE, o8], rtop[0:NE, a:b], -1.0))
                last = dve.tensor_copy(sidx_f[0:NE, 0:CAP_L], sidx[0:NE, 0:CAP_L])
                if nq(l) > LT:
                    own.did(dve.tensor_copy(sidx_f[0:NE, CAP_L:rows], sidx[0:NE, CAP_L:rows]))
                    last = dve.tensor_scalar(sidx_f[0:NE, CAP_L:rows], sidx_f[0:NE, CAP_L:rows], float(SEQ), None,
                                             ALU.add)
                if l == DEPTH - 1:
                    dve.tensor_copy(sval[0:NE, CAP_L:P], sval[0:NE, 0:CAP_L])
                    last = dve.tensor_copy(sidx_f[0:NE, CAP_L:P], sidx[0:NE, 0:CAP_L])
                last.then_inc(top_done, 1)
                dve.wait_ge(gt_mm, l + 1)
                if l:
                    dve.wait_ge(scattered, 16 * NE)
                dve.wait_ge(gv_done, l + 1)
                if l == DEPTH - 1:
                    dve.tensor_copy(gidx[0:CAP_L, 0:PAIRS], ps[0:CAP_L, 6, NE:2 * NE:2])
                    dve.tensor_copy(gidx[0:CAP_L, PAIRS:NE], ps[0:CAP_L, 6, NE + 1:2 * NE:2])
                    dve.tensor_copy(gidx[CAP_L:P, 0:PAIRS], ps[CAP_L:P, 6, NE + 1:2 * NE:2]).then_inc(gi_done, 1)
                    dve.wait_ge(g2_in, 32 * (l + 1))
                    break
                dve.tensor_copy(gidx[0:rows, :], ps[0:rows, 6, NE:2 * NE]).then_inc(gi_done, 1)
                dve.wait_ge(g2_in, 32 * (l + 1))


                def step(n, e, b, first):
                    if b < NE:
                        dve.wait_ge(xgt_mm, n + 1)
                        if not (l == 0 and first and b < 2):
                            dve.wait_ge(up_mm, n - 1)
                        for i, (r0, r1_) in enumerate([(0, CAP_L), (CAP_L, rows)][:1 + (rows > CAP_L)]):
                            src = ps[:, 0:2, 0:4 * rows].rearrange("p b (k t) -> p b k t", k=4)[:, :, :, r0:r1_]
                            dst = xg_t[b % 2].rearrange("p (b k) t -> p b k t", b=2)[:, :, :, r0:r1_]
                            w = r1_ - r0
                            for bb in range(2):
                                a_ = mc[:, 3, i, 4 * bb:4 * bb + 4].unsqueeze(2).to_broadcast([P, 4, w])
                                own.did(dve.tensor_tensor(dst[:, bb], src[:, bb], a_, ALU.mult))
                            d = xg_t[b % 2][:, :, r0:r1_]
                            last = dve.tensor_tensor(d, d, mc[:, 2, i, :].unsqueeze(2).to_broadcast([P, KT, w]),
                                                     ALU.add)
                            if i == 0 and rows > CAP_L:
                                own.did(last)
                        last.then_inc(xgt_ev, 1)
                    if not first or b >= 2:
                        dve.wait_ge(down_mm, n - 1)
                        if not (l == 0 and first and b < 4):
                            dve.wait_ge(scattered, (n - 3) * 16)
                        gv = gval[0:rows, bass.ds(e - 2, 1)] if not isinstance(e, int) else gval[0:rows, e - 2:e - 1]
                        dve.scalar_tensor_tensor(out=y[b % 2][0:rows, :], in0=bank(5, 2)[0:rows, :], scalar=gv,
                                                 in1=g2[0:rows, :], op0=ALU.mult, op1=ALU.mult).then_inc(y_done, 1)
                    if b < NE:
                        dve.wait_ge(up_mm, n + 1)
                        dve.wait_ge(silu_done, n + 1)
                        if not (l == 0 and first and b < 2):
                            dve.wait_ge(hidt_mm, n - 1)
                        dve.tensor_tensor(hid[b % 2][0:rows, :], ps[0:rows, 3, :], sg[0:rows, :], ALU.mult
                                          ).then_inc(hid_done, 1)

                for e in range(LOOP_E):
                    step(l * NE + e, e, e, True)
                per = (3 if rows > CAP_L else 0) + 2
                start = own.n
                with dve.Fori(0, (NE - LOOP_E) // BODY) as it:
                    own.base = it * (per * BODY)
                    for b in range(BODY):
                        step(BODY * it + (l * NE + LOOP_E + b), BODY * it + (LOOP_E + b), LOOP_E + b, False)
                    assert own.n - start == per * BODY
                own.base = 0
                own.n = start + per * (NE - LOOP_E)
                for e in range(NE, NE + 2):
                    step(l * NE + e, e, e, False)

            start = own.n
            with dve.Fori(0, PAIRS // 2) as it:
                own.base = 4 * it
                for b in range(2):
                    n = 2 * it + (PAIR_BASE + b)
                    dve.wait_ge(xgt_mm, n + 1)
                    dve.wait_ge(up_mm, n - 1)
                    for bb in range(2):
                        a_ = mc[:, 3, 0, 4 * bb:4 * bb + 4].unsqueeze(2).to_broadcast([P, 4, P])
                        own.did(dve.tensor_tensor(xg_t[b][:, 4 * bb:4 * bb + 4, :],
                                                  ps[:, bb, :].rearrange("p (k t) -> p k t", k=4), a_, ALU.mult))
                    dve.tensor_tensor(xg_t[b], xg_t[b], mc[:, 2, 0, :].unsqueeze(2).to_broadcast([P, KT, P]),
                                      ALU.add).then_inc(xgt_ev, 1)
                    dve.wait_ge(up_mm, n + 1)
                    dve.wait_ge(silu_done, n + 1)
                    dve.wait_ge(hidt_mm, n - 1)
                    dve.tensor_tensor(hid[b], ps[:, 3, :], sg, ALU.mult).then_inc(hid_done, 1)
                    dve.wait_ge(down_mm, n + 1)
                    dve.wait_ge(scattered, 16 * (2 * (2 * it + b) + (PAIR_BASE - 2)))
                    dve.scalar_tensor_tensor(out=y[b], in0=bank(5, 2), scalar=gval[:, bass.ds(2 * it + b, 1)],
                                             in1=g2, op0=ALU.mult, op1=ALU.mult).then_inc(y_done, 1)
            own.base, own.n = 0, start + 2 * PAIRS

            dve.wait_ge(g1_in, 16 * (3 * DEPTH + 1))
            for t in range(LT):
                n = norms + t
                mean_square(n)
                x2 = xt[:, (t % 2) * D:(t % 2 + 1) * D]
                own.did(normalise(n, t % 2, x2))
                dve.tensor_tensor(x2, x2, fgain, ALU.mult).then_inc(out_done, 1)

        @block.tensor
        def _(pe):
            def weights(item, width=512, k=KT):
                return slot(place[item])[:, 0:k * width].rearrange("p (k n) -> p k n", k=k)

            def ada_product(n):
                item = ada_items[n]
                if n > ADA_FIRST:
                    pe.wait_ge(ada_out, n - ADA_FIRST)
                wait_slot(pe, item)
                w = weights(item)
                for r in range(2):
                    for j in range(4):
                        k = 2 * j + r
                        last = pe.matmul(ps[32 * j:32 * j + 32, 7, :], csil[:, k * 32:(k + 1) * 32], w[:, k, :],
                                         start=(r == 0), stop=(r == 1))
                last.then_inc(ada_mm, 1)

            def ada_columns(n):
                pe.wait_ge(ada_row, n + 1)
                if n:
                    pe.wait_ge(first_cols, n)
                rows = slice(64 * (n % 2), 64 * (n % 2) + 64)
                for k in range(KT):
                    last = pe.matmul(ps[rows, 6, 2 * k:2 * k + 2], modrow[:, k:512:KT], sel[:, 0:2],
                                     start=True, stop=True)
                last.then_inc(ada_sum, 1)

            def ada_total(n):
                pe.wait_ge(ada_row, n + 1)
                pe.matmul(ps[0:32, 7, :], sel, modrow[:], start=True, stop=True).then_inc(ada_sum, 1)

            counts = [pe.alloc_register(f"pe_count{n}") for n in range(2)]
            pe.wait_ge(csil_done, 1)
            pe.wait_ge(consts_in, 16)

            norms = 0
            for l in range(DEPTH):
                def transpose_x(t):
                    n = norms + t
                    pe.wait_ge(xhat, n + 1)
                    if n:
                        pe.wait_ge(h_done, n)
                    for k in range(KT):
                        last = pe.transpose(bank(4, 2)[:, k * P:(k + 1) * P], hx[:, k:D:KT], ident)
                    last.then_inc(t1_mm, 1)

                def main(t, ch):
                    n = tile_no(l, t)
                    w = weights(("in", l, ch), IN_CHUNK[ch][1] - IN_CHUNK[ch][0])
                    a, b = chunk_cols(l, t, ch)
                    if ch == 0:
                        pe.wait_ge(h_done, norms + t + 1)
                    if a == b:
                        return
                    if t == 0:
                        wait_slot(pe, ("in", l, ch))
                    if n:
                        pe.wait_ge(main_ev, main_count(*tile_before(l, t), ch))
                        if ch == 3:
                            pe.wait_ge(sq2, n)
                    if l and t == 0:
                        pe.wait_ge(y_done, l * NE)
                    for k in range(KT):
                        last = pe.matmul(ps[:, ch, 0:b - a], h_t[n % 2][:, k, :], w[:, k, 0:b - a],
                                         start=(k == 0), stop=(k == KT - 1))
                    last.then_inc(main_mm, 1)

                def small(t, u):
                    n = tile_no(l, t)
                    p = pt[n % 2]
                    if u not in small_uses(l, t):
                        return
                    if small_before(l, t, u):
                        pe.wait_ge(small_ev, small_before(l, t, u))
                    dst = ps[:, 6 + u % 2, :]
                    if u == 0:
                        if n == 0:
                            pe.wait_ge(first_cols, ADA_FIRST)
                        pe.wait_ge(cqn, n + 1)
                        for k in range(0 if keys_only(l, t) else 2):
                            pe.transpose(dst[:, k * P:(k + 1) * P], p[:, CQ + k:CKV:2], ident)
                        last = pe.transpose(dst[:, 2 * P:3 * P], p[:, CKV:KR], ident)
                    elif u == 1:
                        pe.wait_ge(small_ev, small_count(l, t, 0))
                        if t == 0:
                            pe.wait_ge(wproj_in, 16 * 9 * (l + 1))
                        for k in range(2):
                            last = pe.matmul(dst[:, 0:384], c_t[:, k, :], wuq[:, k * 384:(k + 1) * 384],
                                             start=(k == 0), stop=(k == 1))
                    elif u == 2:
                        pe.wait_ge(small_ev, small_count(l, t, 0))
                        last = pe.matmul(dst, c_t[:, 2, :], wukv[:], start=True, stop=True)
                    else:
                        if u in (3, 4):
                            pe.wait_ge(rope_ac, n + 1)
                        if u in (6, 7):
                            pe.wait_ge(rope_b, n + 1)
                        if u == 3:
                            srcs = [p[:, QA + P * b:QA + P * (b + 1)] for b in range(4)]
                        elif u == 4:
                            srcs = [p[:, KA:VA], p[:, QD:QD + P], p[:, QD + P:KD], p[:, KD:KD + P]]
                        elif u == 5:
                            srcs = [p[:, KD + P:VD]]
                        else:
                            srcs = [(q96 if u == 6 else k96)[:, h] for h in range(B_HEADS)]
                        rows = P if u < 6 else B_QK
                        for b, s in enumerate(srcs):
                            if u == 4 and keys_only(l, t) and b in (1, 2):
                                continue
                            last = pe.transpose(dst[0:rows, b * P:(b + 1) * P], s, ident)
                    last.then_inc(small_mm, 1)

                if l == 0:
                    for n in range(ADA_FIRST):
                        ada_product(n)
                        ada_columns(n)
                        if n == 1:
                            transpose_x(0)
                else:
                    transpose_x(0)
                for t in range(NT + 1):
                    for ch in range(NCH):
                        if t < NT:
                            main(t, ch)
                        if t >= 1:
                            for u in ([0], [1, 2], [3, 4, 5, 6, 7], [])[ch]:
                                small(t - 1, u)
                        if ch == 1 and t + 1 < NT:
                            transpose_x(t + 1)
                norms += NT

                def scores(s):
                    _, qi, j = s
                    n = step_no(l, qi, j)
                    g = ATT.index((l, qi))
                    kind, h, m = STEPS[j]
                    if j == 0:
                        pe.wait_ge(qz_done, g + 1)
                    if n >= 2:
                        pe.wait_ge(exp_done, n - 1)
                    z = qz[:, (g % 2) * 16 * P:(g % 2 + 1) * 16 * P].rearrange("p (h t) -> p h t", h=16)
                    cols = slice(qi * P, (qi + 1) * P)
                    if kind == "A":
                        lhs, kb, rows = z[:, h, :], B_AK, P
                    elif kind == "B":
                        lhs, kb, rows = qk_t[0:B_QK, B_BQ + h, cols], B_BK + h, B_QK
                    else:
                        mm = 2 * h + m
                        lhs, kb, rows = z[:, 8 + mm, :], B_CK + mm // 4, P
                    kt = [t for t, _ in key_tiles(l, qi, kind)]
                    dst = bank(2 * (n % 2), 2)
                    lat = [t for t in kt if t < LT]
                    if lat:
                        w = len(lat) * P
                        pe.matmul(dst[:, SEQ - w:SEQ], lhs, qk_t[0:rows, kb, lat[0] * P:lat[0] * P + w],
                                  start=True, stop=True)
                    pe.matmul(dst[:, SEQ:TOK], lhs, qk_t[0:rows, kb, SEQ:TOK], start=True, stop=True
                              ).then_inc(s_mm, 1)

                seq = [(l, qi, j) for qi in range(nq(l)) for j in range(NS)]
                pe.wait_ge(main_ev, main_count(l, NT - 1, 3))
                pe.wait_ge(sq2, tile_no(l, NT - 1) + 1)
                pe.wait_ge(small_ev, small_count(l, NT - 1))
                scores(seq[0])
                scores(seq[1])

                def transpose_prob(s):
                    _, qi, j = s
                    n = step_no(l, qi, j)
                    kind, h, m = STEPS[j]
                    it = item_no(l, qi, ITEM[j])
                    if kind == "C":
                        pe.wait_ge(comb, C_HEADS * (l * NT + qi) + h + 1)
                        src = prob[(n - 1) % 3]
                    else:
                        pe.wait_ge(exp_done, n + 1)
                        src = prob[n % 3]
                    if ITEM[j] or qi:
                        pe.wait_ge(pta_ev, it)
                        pe.wait_ge(ptd_ev, it)
                    kt = key_tiles(l, qi, kind)
                    a = len(kt) // 2
                    for b, (_, c0) in enumerate(kt):
                        last = pe.transpose(ps[:, 4 + (b >= a), (b - a * (b >= a)) * P:][:, 0:P],
                                            src[:, c0:c0 + P], ident)
                    last.then_inc(t_mm, 1)

                def values(s):
                    _, qi, j = s
                    kind, h, m = STEPS[j]
                    it = item_no(l, qi, ITEM[j])
                    kt = key_tiles(l, qi, kind)
                    pe.wait_ge(pta_ev, it + 1)
                    pe.wait_ge(ptd_ev, it + 1)
                    if it:
                        pe.wait_ge(o_ev, it)
                    for b, (t, _) in enumerate(kt):
                        if kind == "A":
                            v = va[:, t, (h // 4) * HD:(h // 4 + 1) * HD]
                        else:
                            v = (vb if kind == "B" else vc)[:, t, h * 64:(h + 1) * 64]
                        last = pe.matmul(ps[:, 6, 0:64], prob_t[it % 2][:, b, :], v,
                                         start=(b == 0), stop=(b == len(kt) - 1))
                    last.then_inc(pv_mm, 1)

                def output_transposes(qi):
                    g = ATT.index((l, qi))
                    pe.wait_ge(on_done, g + 1)
                    it = item_no(l, qi, OT_AFTER) + NI if qi < nq(l) - 1 else item_no(l, qi, NI - 1)
                    pe.wait_ge(pta_ev, it + 1)
                    pe.wait_ge(ptd_ev, it + 1)
                    for kk in range(KT):
                        last = pe.transpose(bank(4, 2)[:, kk * P:(kk + 1) * P], ob[g % 2][:, kk:D:KT], ident)
                    last.then_inc(ot_mm, 1)

                waiting = None
                for k, s in enumerate(seq):
                    _, qi, j = s
                    if k + 2 < len(seq):
                        scores(seq[k + 2])
                    if LASTSTEP[j]:
                        if qi and ITEM[j] == OT_AFTER + 1:
                            g = ATT.index((l, qi))
                            pe.wait_ge(ota_ev, g)
                            pe.wait_ge(otd_ev, g)
                        transpose_prob(s)
                        if waiting:
                            values(waiting)
                        waiting = s
                        if qi and ITEM[j] == OT_AFTER:
                            output_transposes(qi - 1)
                    a = ada_at(l, qi, j)
                    if a is not None:
                        ada_product(a)
                    a = ada_sum_at(l, qi, j)
                    if a is not None:
                        ada_total(a)
                values(waiting)
                output_transposes(nq(l) - 1)

                def logits(t):
                    g = tile_no(l, t)
                    n = norms + t
                    transpose_x(t)
                    pe.wait_ge(h_done, n + 1)
                    if t == 0:
                        pe.wait_ge(g1_in, 16 * 3 * (l + 1))
                    for k in range(KT):
                        last = pe.matmul(ps[:, 6, 0:NE], h2_t[:, k, :], wr[:, k * NE:(k + 1) * NE],
                                         start=(k == 0), stop=(k == KT - 1))
                    last.then_inc(lg_mm, 1)

                def affinities(t):
                    g = tile_no(l, t)
                    pe.wait_ge(aff_done, g + 1)
                    if t:
                        pe.wait_ge(at_ev, g)
                    pe.transpose(ps[0:NE, 7, 0:P], aff, ident).then_inc(at_mm, 1)

                ng = len([a for a in ATT if a[0] <= l])
                pe.wait_ge(ota_ev, ng)
                pe.wait_ge(otd_ev, ng)
                pe.wait_ge(o_ev, item_no(l, nq(l) - 1, NI - 1) + 1)
                if l == 0:
                    pe.wait_ge(ada_out, len(ada_items) - ADA_FIRST)
                for t in range(nq(l) + 1):
                    g = tile_no(l, t)
                    for h in range(2):
                        if t < nq(l):
                            if t >= 2:
                                pe.wait_ge(xo_done, g - 1)
                            if t == 0:
                                wait_slot(pe, ("out", l, h))
                            w = weights(("out", l, h))
                            for k in range(KT):
                                last = pe.matmul(ps[:, 2 * (g % 2) + h, :], qk_t[:, OT_BLOCK[k], t * P:(t + 1) * P],
                                                 w[:, k, :], start=(k == 0), stop=(k == KT - 1))
                            last.then_inc(wo_mm, 1)
                        if t >= 1:
                            (logits if h == 0 else affinities)(t - 1)
                norms += nq(l)

                rows = CAP_L + (CAP_C if nq(l) > LT else 0)
                pe.wait_ge(top_done, l + 1)
                if l == DEPTH - 1:
                    pe.transpose(ps[:, 6, 0:NE], sval[0:NE, 0:P], ident[0:NE, 0:NE])
                    pe.transpose(ps[:, 6, NE:2 * NE], sidx_f[0:NE, 0:P], ident[0:NE, 0:NE]).then_inc(gt_mm, 1)
                    break
                pe.transpose(ps[0:rows, 6, 0:NE], sval[0:NE, 0:rows], ident[0:NE, 0:NE])
                pe.transpose(ps[0:rows, 6, NE:2 * NE], sidx_f[0:NE, 0:rows], ident[0:NE, 0:NE]).then_inc(gt_mm, 1)

                def step(n, b, r, first, pair):
                    def landed(q, pos):
                        pe.wait_ge(ring_in[q % NSLOT], pos)
                    if b < NE:
                        before = [] if l == 0 and first and b == 0 else [(xgt_ev, n)]
                        wait_in_loop(pe, counts, gt_mm, l + 1, (xg_in[b % 2], pair * 16 + 16), *before)
                        for k in range(KT):
                            last = pe.transpose(ps[:, k // 4, (k % 4) * rows:(k % 4 + 1) * rows],
                                                xg[b % 2][0:rows, k:D:KT], ident[0:rows, 0:rows])
                        last.then_inc(xgt_mm, 1)
                    if not first or b >= 2:
                        pe.wait_ge(hidt_ev, n - 1)
                        if not (l == 0 and first and b == 2):
                            pe.wait_ge(y_done, n - 2)
                        landed(*r[0])
                        w = slot(r[0][0]).rearrange("p (k n) -> p k n", k=4)
                        for h in range(2):
                            for k in range(4):
                                last = pe.matmul(ps[0:rows, 5 + h, :], hid_t[b % 2][:, k, 0:rows],
                                                 w[:, k, h * 512:(h + 1) * 512], start=(k == 0), stop=(k == 3))
                        last.then_inc(down_mm, 1)
                    if b < NE:
                        pe.wait_ge(xgt_ev, n + 1)
                        if not (l == 0 and first and b == 0):
                            pe.wait_ge(silu_done, n)
                        landed(*r[1])
                        w = slot(r[1][0]).rearrange("p (k n) -> p k n", k=KT)
                        for k in range(KT):
                            last = pe.matmul(ps[0:rows, 2, :], xg_t[b % 2][:, k, 0:rows], w[:, k, :],
                                             start=(k == 0), stop=(k == KT - 1))
                        last.then_inc(gate_mm, 1)
                    if not first or b >= 1:
                        if b <= NE:
                            before = [] if l == 0 and first and b == 1 else [(hidt_ev, n - 1)]
                            wait_in_loop(pe, counts, gt_mm, l + 1, (hid_done, n), *before)
                            for k in range(4):
                                last = pe.transpose(ps[:, 4, k * rows:(k + 1) * rows],
                                                    hid[(b - 1) % 2][0:rows, k:512:4], ident[0:rows, 0:rows])
                            last.then_inc(hidt_mm, 1)
                    if b < NE:
                        if not (l == 0 and first and b == 0):
                            pe.wait_ge(hid_done, n)
                        landed(*r[2])
                        w = slot(r[2][0]).rearrange("p (k n) -> p k n", k=KT)
                        for k in range(KT):
                            last = pe.matmul(ps[0:rows, 3, :], xg_t[b % 2][:, k, 0:rows], w[:, k, :],
                                             start=(k == 0), stop=(k == KT - 1))
                        last.then_inc(up_mm, 1)

                def at(item):
                    r_ = place.get(item)
                    return None if r_ is None else (r_, 16 * (r_ // NSLOT + 1))

                for e in range(LOOP_E):
                    step(l * NE + e, e, [at(("d", l, e - 2)), at(("g", l, e)), at(("u", l, e))], True,
                         (l * NE + e) // 2)
                turns = 3 * BODY // NSLOT
                with pe.Fori(0, (NE - LOOP_E) // BODY) as itr:
                    for b in range(BODY):
                        e = LOOP_E + b
                        where = [at(("d", l, e - 2)), at(("g", l, e)), at(("u", l, e))]
                        step(BODY * itr + (l * NE + e), e,
                             [(q, itr * (16 * turns) + v) for q, v in where], False,
                             itr * (BODY // 2) + (l * NE + e) // 2)
                step(l * NE + NE, NE, [at(("d", l, NE - 2)), None, None], False, None)
                step(l * NE + NE + 1, NE + 1, [at(("d", l, NE - 1)), None, None], False, None)

            halves = [slice(CAP_L * h, CAP_L * (h + 1)) for h in range(2)]
            with pe.Fori(0, PAIRS // 2) as it:
                for b in range(2):
                    n = 2 * it + (PAIR_BASE + b)
                    p = 2 * it + b
                    pair_w = []
                    for kind, h, dst, landed, loads, _ in PAIR_SLOTS:
                        pair_w.append((dst.rearrange("p (k n) -> p k n", k=4 if kind == "d" else KT), landed,
                                       16 * p + 16 * (loads + 1)))
                    wait_in_loop(pe, counts, gt_mm, DEPTH, (xg_in[b], 16 * it + 16 * (PAIR_BASE // 2 + 1)),
                                 (xgt_ev, n))
                    for k in range(KT):
                        last = pe.transpose(ps[:, k // 4, (k % 4) * P:(k % 4 + 1) * P], xg[b][:, k:D:KT], ident)
                    last.then_inc(xgt_mm, 1)
                    pe.wait_ge(xgt_ev, n + 1)
                    for g, (bk, read, done) in enumerate(((2, silu_done, gate_mm), (3, hid_done, up_mm))):
                        pe.wait_ge(read, n)
                        for w, landed, count in pair_w[2 * g:2 * g + 2]:
                            pe.wait_ge(landed, count)
                        for k in range(KT):
                            for h in range(2):
                                last = pe.matmul(ps[halves[h], bk, :], xg_t[b][:, k, halves[h]],
                                                 pair_w[2 * g + h][0][:, k, :], start=(k == 0), stop=(k == KT - 1))
                        last.then_inc(done, 1)
                    wait_in_loop(pe, counts, gt_mm, DEPTH, (hid_done, n + 1), (hidt_ev, n))
                    for k in range(4):
                        last = pe.transpose(ps[:, 4, k * P:(k + 1) * P], hid[b][:, k:512:4], ident)
                    last.then_inc(hidt_mm, 1)
                    pe.wait_ge(hidt_ev, n + 1)
                    pe.wait_ge(y_done, n)
                    for w, landed, count in pair_w[4:6]:
                        pe.wait_ge(landed, count)
                    for c0 in range(2):
                        for k in range(4):
                            for h in range(2):
                                last = pe.matmul(ps[halves[h], 5 + c0, :], hid_t[b][:, k, halves[h]],
                                                 pair_w[4 + h][0][:, k, c0 * 512:(c0 + 1) * 512],
                                                 start=(k == 0), stop=(k == 3))
                    last.then_inc(down_mm, 1)
    es.close()


_INS = ["x", "c", "ctx", "c_ctx", "norm1", "norm2", "w_ada", "b_ada", "w_in", "sink", "mla_q_norm", "w_uq",
        "mla_kv_norm", "w_ukv", "lam_q1", "lam_k1", "lam_q2", "lam_k2", "diff_norm", "w_out", "w_router",
        "w_gate", "w_up", "w_down", "final_norm"]


def kernel(**inputs):
    import concourse.bacc as _bacc
    from concourse.bass_utils import run_bass_kernel_spmd as _run

    nc = _bacc.Bacc("TRN2", target_bir_lowering=False, num_devices=1)
    arrays = {f"in_{name}_dram": np.ascontiguousarray(inputs[name]) for name in _INS}
    arrays["shape_constants"] = shape_constants()
    args = [nc.dram_tensor(name, a.shape, mybir.dt.from_np(a.dtype), kind="ExternalInput").ap()
            for name, a in arrays.items()]
    args.append(nc.dram_tensor("out_0_dram", (1, SEQ, D), F32, kind="ExternalOutput").ap())
    build(nc, *args)
    r = _run(nc, [arrays], core_ids=[0])
    return r.results[0]["out_0_dram"]
```

```python
from contextlib import ExitStack

import numpy as np

import concourse.bass as bass
from concourse import mybir

F32 = mybir.dt.float32
U32 = mybir.dt.uint32
ALU = mybir.AluOpType
ACT = mybir.ActivationFunctionType
AX_X = mybir.AxisListType.X

P = 128
D = 1024
KT = D // P
SEQ, CTX = 512, 256
TOK = SEQ + CTX
LT, CT = SEQ // P, CTX // P
NT = LT + CT
DEPTH = 2
EPS = 1e-6
NEG_INF = -1e30
GRID_W = 64
ROPE_BASE = 10000.0

A_HEADS, A_KV, HD = 8, 2, 64
B_HEADS, B_NOPE, B_ROPE, B_V, B_QR, B_KVR = 4, 64, 32, 64, 256, 128
B_QK = B_NOPE + B_ROPE
C_HEADS, C_DH, C_V = 4, 32, 64
IN_W = 1952
QA, KA, VA, CQ, CKV, KR, QD, KD, VD = 0, 512, 640, 768, 1024, 1152, 1184, 1440, 1696
IN_CHUNK = [(0, 512), (512, 1024), (1024, 1440), (1440, 1952)]
NCH = len(IN_CHUNK)

NE, FE = 16, 512
CAP_L, CAP_C = 2 * SEQ // NE, 2 * CTX // NE
NSLOT = 4
PAIRS = NE // 2
SLOT = KT * 512

N_ADA = 6 * D // 512
ADA_FIRST = 4

STEPS = [("A", h, 0) for h in range(A_HEADS)] + [("B", h, 0) for h in range(B_HEADS)]
STEPS += [("C", h, m) for h in range(C_HEADS) for m in range(2)]
NS = len(STEPS)
NI = A_HEADS + B_HEADS + C_HEADS
ITEM = [j if j < 12 else 12 + (j - 12) // 2 for j in range(NS)]
LASTSTEP = [j < 12 or j % 2 == 1 for j in range(NS)]
B_AQ, B_AK, B_CQ, B_CK, B_BQ, B_BK, NBLK = 0, 4, 5, 7, 9, 13, 17
OT_AFTER = 6
OT_BLOCK = [0, 1, 2, 3, 5, 6, 9, 10]

K_ID, K_MASK, K_SEL, K_CA, K_SA, K_CB, K_SB = 0, 128, 384, 416, 672, 928, 1056
NCONST = 1184


def shape_constants():
    k = np.zeros((P, NCONST), np.float32)
    k[:, K_ID:K_ID + P] = np.eye(P)
    q, j = np.arange(P)[:, None], np.arange(P)[None, :]
    k[:, K_MASK:K_MASK + P] = np.where(j >= q, 0.0, NEG_INF)
    k[:, K_MASK + P:K_MASK + 2 * P] = np.where(j <= q, 0.0, NEG_INF)
    for g in range(4):
        for i in range(2):
            k[32 * g + i, K_SEL + i] = 1.0
    for c0, s0, rot in ((K_CA, K_SA, HD), (K_CB, K_SB, B_ROPE)):
        nf = rot // 4
        inv = (np.float32(ROPE_BASE) ** (-np.arange(nf, dtype=np.float32) / np.float32(nf))).astype(np.float32)
        for t in range(LT):
            tok = t * P + np.arange(P)
            for axis, pos in enumerate((tok // GRID_W, tok % GRID_W)):
                ang = pos[:, None].astype(np.float32) * inv
                cos, sin = np.cos(ang), np.sin(ang)
                o = t * rot + axis * 2 * nf
                k[:, c0 + o:c0 + o + 2 * nf] = np.concatenate([cos, cos], 1)
                k[:, s0 + o:s0 + o + 2 * nf] = np.concatenate([-sin, sin], 1)
    return k


def lam_init(l):
    return 0.8 - 0.6 * float(np.exp(-0.3 * l))


def nq(l):
    return NT if l < DEPTH - 1 else LT


def wait_in_loop(eng, regs, known, count, *waits):
    values = []
    for reg, (sem, value) in zip(regs, waits):
        if not isinstance(value, int):
            eng.reg_mov(reg, value)
            value = eng.snap(reg)
        values.append((sem, value))
    eng.wait_ge(known, count)
    for sem, value in values:
        eng.wait_ge(sem, value)


class Steps:

    def __init__(self, eng, sem):
        self.eng, self.sem, self.base, self.n = eng, sem, 0, 0

    def did(self, ins):
        self.count(ins)
        self.wait()

    def count(self, ins):
        ins.then_inc(self.sem, 1)
        self.n += 1

    def wait(self, back=0):
        self.eng.wait_ge(self.sem, self.base + self.n - back)


def key_tiles(l, qi, kind):
    if qi >= LT:
        lat = []
    elif kind == "A":
        lat = list(range(max(0, qi - 1), min(LT - 1, qi + 1) + 1))
    else:
        lat = list(range(LT))
    c0 = SEQ - P * len(lat)
    return [(t, c0 + P * n) for n, t in enumerate(lat)] + [(LT + c, SEQ + P * c) for c in range(CT)]


def act_share(n):
    return min(4, n - 1)


def keys_only(l, t):
    return l == DEPTH - 1 and t >= LT


def chunk_cols(l, t, ch):
    a, b = IN_CHUNK[ch]
    if keys_only(l, t):
        b = {0: a, 1: CQ, 2: QD, 3: b}[ch]
    return a, b


def small_uses(l, t):
    return [0, 2, 4, 5, 7] if keys_only(l, t) else list(range(8))


MAIN = [(l, t, ch) for l in range(DEPTH) for t in range(NT) for ch in range(NCH)]
SMALL = [(l, t, u) for l in range(DEPTH) for t in range(NT) for u in small_uses(l, t)]


def main_count(l, t, ch):
    return sum(1 for m in MAIN if m <= (l, t, ch) and chunk_cols(*m)[1] > chunk_cols(*m)[0])


def small_count(l, t, u=7):
    return sum(1 for m in SMALL if m <= (l, t, u))


def small_before(l, t, u):
    return max([n + 1 for n, m in enumerate(SMALL) if m < (l, t, u) and m[2] % 2 == u % 2], default=0)


def tile_before(l, t, k=1):
    n = l * NT + t - k
    return n // NT, n % NT


def ring_plan():
    plan = [("ada", 0, c) for c in range(ADA_FIRST)] + [("in", 0, c) for c in range(NCH)]
    plan += [("ada", 0, c) for c in range(ADA_FIRST, N_ADA)] + [("ada", 1, c) for c in range(N_ADA)]
    for l in range(DEPTH):
        if l:
            plan += [("in", l, c) for c in range(NCH)]
        plan += [("out", l, h) for h in range(2)]
        if l == DEPTH - 1:
            break
        plan += [("g", l, 0), ("u", l, 0), ("g", l, 1), ("u", l, 1)]
        for e in range(2, NE):
            plan += [("d", l, e - 2), ("g", l, e), ("u", l, e)]
        plan += [("d", l, NE - 2), ("d", l, NE - 1)]
    return plan


def build(nc, x, c, ctx_in, c_ctx, norm1, norm2, w_ada, b_ada, w_in, sink, q_norm, w_uq, kv_norm, w_ukv,
          lam_q1, lam_k1, lam_q2, lam_k2, diff_norm, w_out, w_router, w_gate, w_up, w_down, final_norm,
          consts, out):
    es = ExitStack()

    def sb(name, n, dt=F32):
        return es.enter_context(nc.sbuf_tensor(name, [P, n], dt))

    def sem(name):
        return es.enter_context(nc.semaphore(name))

    x_s = nc.dram_tensor("x_s", (TOK, D), F32).ap()
    h2_s = nc.dram_tensor("h2_s", (TOK, D), F32).ap()
    mod_s = nc.dram_tensor("mod_s", (DEPTH, 2, 6 * D), F32).ap()

    ring = sb("ring", NSLOT * SLOT)
    qz = sb("qz", 2 * 16 * P)
    store = sb("store", NBLK * TOK + TOK + 2 * 2 * TOK)
    work = sb("work", 7744)
    xt = sb("xt", 2 * D)
    hx = sb("hx", D)
    kc = sb("kc", NCONST)
    wuq = sb("wuq", 2 * 384)
    wukv = sb("wukv", 512)
    wr = sb("wr", KT * NE)
    modrow = sb("modrow", 512)
    msum = sb("msum", 512)
    csil = sb("csil", KT * 32)
    ctmp = sb("ctmp", 3 * 16)
    modc = sb("modc", 4 * 2 * KT)
    ncol = sb("ncol", 2 * DEPTH * KT)
    bcol = sb("bcol", 2 * KT)
    gcol = sb("gcol", 2 + 1)
    dgain = sb("dgain", C_V)
    sinkb = sb("sinkb", 2 * DEPTH * A_HEADS)
    lamb = sb("lamb", 4 * C_DH + 8)
    half = sb("half", 8)
    st = sb("st", 160)
    gval = sb("gval", NE)
    gidx = sb("gidx", NE, U32)
    ix = sb("ix", 2 * PAIRS, U32)

    ps = es.enter_context(nc.psum_tensor("ps", [P, 8, 512], F32))

    def bank(b, n=1):
        return ps[:, b:b + n, :].rearrange("p b n -> p (b n)")

    ident = kc[:, K_ID:K_ID + P]
    sel = kc[:, K_SEL:K_SEL + 32]

    def slot(r):
        o = (r % NSLOT) * SLOT
        return ring[:, o:o + SLOT]

    spare = store[:, 10 * D:10 * D + SLOT]

    qk_t = store[:, 0:NBLK * TOK].rearrange("p (b t) -> p b t", b=NBLK)
    o = NBLK * TOK
    va = store[:, o:o + TOK].rearrange("p (t n) -> p t n", t=NT)
    vb = store[:, o + TOK:o + 3 * TOK].rearrange("p (t n) -> p t n", t=NT)
    vc = store[:, o + 3 * TOK:o + 5 * TOK].rearrange("p (t n) -> p t n", t=NT)
    xg = [store[:, n * D:(n + 1) * D] for n in range(2)]
    xg_t = [store[:, (2 + n) * D:(3 + n) * D].rearrange("p (k t) -> p k t", k=KT) for n in range(2)]
    y = [store[:, (4 + n) * D:(5 + n) * D] for n in range(2)]
    hid = [store[:, 6 * D + n * 512:6 * D + (n + 1) * 512] for n in range(2)]
    hid_t = [store[:, 7 * D + n * 512:7 * D + (n + 1) * 512].rearrange("p (k t) -> p k t", k=4) for n in range(2)]
    sg = store[:, 8 * D:8 * D + 512]
    g2 = store[:, 9 * D:10 * D]
    h_t = [work[:, n * D:(n + 1) * D].rearrange("p (k t) -> p k t", k=KT) for n in range(2)]
    pt = [work[:, 2048 + n * IN_W:2048 + (n + 1) * IN_W] for n in range(2)]
    o = 2048 + 2 * IN_W
    c_t = work[:, o:o + 384].rearrange("p (k t) -> p k t", k=3)
    q96 = work[:, o + 384:o + 768].rearrange("p (h d) -> p h d", h=B_HEADS)
    k96 = work[:, o + 768:o + 1152].rearrange("p (h d) -> p h d", h=B_HEADS)
    rtmp = work[:, o + 1152:o + 1152 + 640]
    pw = TOK + 8
    prob = [work[:, n * pw:(n + 1) * pw] for n in range(3)]
    o = 3 * pw
    prob_t = [work[:, o + n * TOK:o + (n + 1) * TOK].rearrange("p (b t) -> p b t", b=NT) for n in range(4)]
    o += 4 * TOK
    ob = [work[:, o + n * D:o + (n + 1) * D] for n in range(2)]
    ov = [hx[:, n * P:(n + 1) * P] for n in range(2)]
    csq = hx[:, 2 * P:2 * P + 256]
    g1 = work[:, 0:2 * D].rearrange("p (i n) -> p i n", i=2)
    h2_t = work[:, 2 * D:3 * D].rearrange("p (k t) -> p k t", k=KT)
    aff = work[:, 3 * D:3 * D + NE]
    aff_e = work[:, 3 * D + 32:3 * D + 32 + NE]
    rtop = work[:, 3 * D + 64:3 * D + 64 + TOK]
    rtop2 = work[:, 5 * D + 512:5 * D + 512 + TOK]
    sval = work[:, 4 * D:4 * D + P]
    sidx_f = work[:, 4 * D + P:4 * D + 2 * P]
    sidx = work[:, 4 * D + 2 * P:4 * D + 3 * P].bitcast(U32)
    tmpo = work[:, 5 * D:5 * D + 512]
    fgain = work[:, 0:D]
    fx = [work[:, (1 + t) * D:(2 + t) * D] for t in range(LT)]

    ss, msq, rstd = st[:, 0:2], st[:, 2:4], st[:, 4:6]
    ss2, ms2, rs2 = st[:, 6:8], st[:, 8:10], st[:, 10:12]
    mx, negm = st[:, 12:14], st[:, 14:34]
    sums, rinv = st[:, 34:54], st[:, 62:78]
    r1, cc = st[:, 78:82], st[:, 82:86]
    css, cms, crs = st[:, 94:98], st[:, 98:102], st[:, 102:106]
    fss, fms, frs = st[:, 110:114], st[:, 114:118], st[:, 118:122]
    rmx, rsum, rrec = st[:, 106:107], st[:, 107:108], st[:, 108:109]

    c_in, consts_in, cols_in, sink_in = sem("c_in"), sem("consts_in"), sem("cols_in"), sem("sink_in")
    ring_in = [sem(f"ring_in{n}") for n in range(NSLOT)]
    qz_in, spare_in = sem("qz_in"), sem("spare_in")
    mod_init, mod_stored = sem("mod_init"), sem("mod_stored")
    modc_in, wproj_in = sem("modc_in"), sem("wproj_in")
    g1_in, g2_in = sem("g1_in"), sem("g2_in")
    x_in = [sem(f"x_in{n}") for n in range(2)]
    xo_in = [sem(f"xo_in{n}") for n in range(2)]
    xg_in = [sem(f"xg_in{n}") for n in range(2)]
    fgain_in, fx_in = sem("fgain_in"), [sem(f"fx_in{t}") for t in range(LT)]
    fss_done, fms_done, frs_done = sem("fss_done"), sem("fms_done"), sem("frs_done")
    xs_stored, h2_stored, scattered, out_stored = (
        sem("xs_stored"), sem("h2_stored"), sem("scattered"), sem("out_stored"))
    pool_did, dve_did = sem("pool_did"), sem("dve_did")
    zeroed, csil_e, csil_done, first_cols = sem("zeroed"), sem("csil_e"), sem("csil_done"), sem("first_cols")
    lam_e, lam_p = sem("lam_e"), sem("lam_p")
    ada_mm, ada_row, ada_sum, ada_out = sem("ada_mm"), sem("ada_row"), sem("ada_sum"), sem("ada_out")
    modc_done = sem("modc_done")
    sumsq, ms_done, rstd_done, xhat, t1_mm, h_done = (
        sem("sumsq"), sem("ms_done"), sem("rstd_done"), sem("xhat"), sem("t1_mm"), sem("h_done"))
    t1_half, h_half = sem("t1_half"), sem("h_half")
    main_mm, main_ev, sq2, ms2_done, rs2_done, cqn = (
        sem("main_mm"), sem("main_ev"), sem("sq2"), sem("ms2_done"), sem("rs2_done"), sem("cqn"))
    small_mm, small_ev, rope_ac, rope_b = sem("small_mm"), sem("small_ev"), sem("rope_ac"), sem("rope_b")
    sink_done, qz_done, s_mm, neg_done, exp_done, comb = (
        sem("sink_done"), sem("qz_done"), sem("s_mm"), sem("neg_done"), sem("exp_done"), sem("comb"))
    t_mm, pta_ev, ptd_ev = sem("t_mm"), sem("pta_ev"), sem("ptd_ev")
    pv_mm, ov_ev, back_mm, o_ev = sem("pv_mm"), sem("ov_ev"), sem("back_mm"), sem("o_ev")
    cms_done, crs_done, on_done, ot_mm, ota_ev, otd_ev = (
        sem("cms_done"), sem("crs_done"), sem("on_done"), sem("ot_mm"), sem("ota_ev"), sem("otd_ev"))
    wo_mm, xo_done, lg_mm, rmax_done, rexp_done, aff_done, at_mm, at_ev = (
        sem("wo_mm"), sem("xo_done"), sem("lg_mm"), sem("rmax_done"), sem("rexp_done"), sem("aff_done"),
        sem("at_mm"), sem("at_ev"))
    top_done, gt_mm, gv_done, gi_done = sem("top_done"), sem("gt_mm"), sem("gv_done"), sem("gi_done")
    xgt_mm, xgt_ev, gate_mm, silu_done, up_mm, hid_done = (
        sem("xgt_mm"), sem("xgt_ev"), sem("gate_mm"), sem("silu_done"), sem("up_mm"), sem("hid_done"))
    hidt_mm, hidt_ev, down_mm, y_done, out_done = (
        sem("hidt_mm"), sem("hidt_ev"), sem("down_mm"), sem("y_done"), sem("out_done"))

    plan = ring_plan()
    place = {item: r for r, item in enumerate(plan)}
    ada_items = [it for it in plan if it[0] == "ada"]
    ada_no = {(it[1], it[2]): n for n, it in enumerate(ada_items)}

    def wait_slot(eng, item):
        r = place[item]
        eng.wait_ge(ring_in[r % NSLOT], 16 * (r // NSLOT + 1))

    def tile_no(l, t):
        return l * NT + t

    def step_no(l, qi, j):
        return (l * NT + qi) * NS + j

    def item_no(l, qi, i):
        return (l * NT + qi) * NI + i

    def pair_no(l, qi, i):
        return item_no(l, qi, i) // 2

    def pair_behind(l, qi, i, k):
        n = qi * NI // 2 + i // 2 - k
        return (n // (NI // 2), n % (NI // 2) * 2) if n >= 0 else None

    def tile_rows(l, t):
        if l:
            return x_s[t * P:(t + 1) * P, :]
        return x[0, t * P:(t + 1) * P, :] if t < LT else ctx_in[0, (t - LT) * P:(t - LT + 1) * P, :]

    NSK = DEPTH * A_HEADS
    ATT = [(l, qi) for l in range(DEPTH) for qi in range(nq(l))]
    R = len(plan)
    PAIR_SLOTS = [("g", 0, slot(R), ring_in[R % NSLOT], R // NSLOT, gate_mm),
                  ("g", 1, slot(R + 1), ring_in[(R + 1) % NSLOT], (R + 1) // NSLOT, gate_mm),
                  ("u", 0, qz[:], qz_in, 0, up_mm),
                  ("u", 1, spare, spare_in, 0, up_mm),
                  ("d", 0, slot(R + 2), ring_in[(R + 2) % NSLOT], (R + 2) // NSLOT, down_mm),
                  ("d", 1, slot(R + 3), ring_in[(R + 3) % NSLOT], (R + 3) // NSLOT, down_mm)]
    PAIR_BASE = (DEPTH - 1) * NE
    LOOP_E, BODY = 4, 4

    def ada_at(l, qi, j):
        n = (qi * NS + j) // 5
        if l == 0 and j % 5 == 4 and n < len(ada_items) - ADA_FIRST:
            return ADA_FIRST + n
        return None

    def ada_sum_at(l, qi, j):
        s = qi * NS + j - 2
        return ada_at(l, s // NS, s % NS) if s >= 0 else None

    with nc.Block() as block:

        @block.sync
        def _(sp):
            def source(item):
                kind, l, n = item
                if kind == "ada":
                    return w_ada[l].rearrange("(p k) n -> p k n", k=KT)[:, :, 512 * n:512 * n + 512], 512
                if kind == "in":
                    a, b = IN_CHUNK[n]
                    return w_in[l].rearrange("(p k) n -> p k n", k=KT)[:, :, a:b], b - a
                if kind == "out":
                    return w_out[l].rearrange("(p k) n -> p k n", k=KT)[:, :, 512 * n:512 * n + 512], 512

            def freed(item):
                kind, l, n = item
                if kind == "ada":
                    sp.wait_ge(ada_mm, ada_no[(l, n)] + 1)
                elif kind == "in":
                    sp.wait_ge(main_mm, main_count(l, NT - 1, n))
                elif kind == "out":
                    sp.wait_ge(wo_mm, 2 * tile_no(l, nq(l) - 1) + n + 1)
                else:
                    sp.wait_ge({"g": gate_mm, "u": up_mm, "d": down_mm}[kind], l * NE + n + 1)

            def expert_weights(kind, l, e):
                if kind == "d":
                    return w_down[l, e].rearrange("(p k) n -> p (k n)", k=4)
                return (w_gate if kind == "g" else w_up)[l, e].rearrange("(p k) n -> p (k n)", k=KT)

            def load(r):
                if r >= NSLOT:
                    freed(plan[r - NSLOT])
                kind, l, n = plan[r]
                if kind == "in" and l and n == NCH - 1:
                    for b in range(2):
                        sp.wait_ge(x_in[b], 16 * (tile_no(l, b) // 2 + 1))
                if kind in "gud":
                    sp.dma_start(slot(r), expert_weights(kind, l, n)).then_inc(ring_in[r % NSLOT], 16)
                else:
                    src, width = source(plan[r])
                    dst = slot(r)[:, 0:KT * width].rearrange("p (k n) -> p k n", k=KT)
                    sp.dma_start(dst, src).then_inc(ring_in[r % NSLOT], 16)

            counts = [sp.alloc_register(f"sp_count{n}") for n in range(2)]
            with nc.allow_non_contiguous_dma(reason="a few columns"):
                sp.dma_start(ctmp[:, 0:KT], c[0].rearrange("(p k) -> p k", k=KT)).then_inc(c_in, 16)
                sp.dma_start(ctmp[:, KT:2 * KT], c_ctx.rearrange("(p k) -> p k", k=KT)).then_inc(c_in, 16)
            load(0)
            sp.dma_start(kc[:], consts[:, :]).then_inc(consts_in, 16)
            load(1)
            sp.dma_start(xt[:, 0:D], x[0, 0:P, :]).then_inc(x_in[0], 16)
            load(2)
            with nc.allow_non_contiguous_dma(reason="a few columns"):
                sp.dma_start(bcol[:].rearrange("p (v k) -> p v k", v=2),
                             b_ada[0, 0:2 * D].rearrange("(v p k) -> p v k", v=2, k=KT)).then_inc(cols_in, 16)
                for i, w in enumerate((norm1, norm2)):
                    sp.dma_start(ncol[:, i * DEPTH * KT:(i + 1) * DEPTH * KT].rearrange("p (l k) -> p l k", k=KT),
                                 w.rearrange("l (p k) -> p l k", k=KT)).then_inc(cols_in, 16)
            load(3)
            sp.dma_start(xt[:, D:2 * D], x[0, P:2 * P, :]).then_inc(x_in[1], 16)

            r = 4
            for l in range(DEPTH - 1):
                first = place[("d", l, LOOP_E - 2)]
                while r < first:
                    load(r)
                    r += 1
                with sp.Fori(0, (NE - LOOP_E) // BODY) as it:
                    for b in range(BODY):
                        e = BODY * it + (LOOP_E + b)
                        for n, (kind, src, back, seen) in enumerate((
                                ("d", -2, up_mm, -1),
                                ("g", 0, down_mm, -2),
                                ("u", 0, gate_mm, 0))):
                            q = r + 3 * b + n
                            sp.wait_ge(back, e + (l * NE + seen))
                            w = {"d": w_down, "g": w_gate, "u": w_up}[kind][l, bass.ds(e + src, 1)]
                            k = 4 if kind == "d" else KT
                            sp.dma_start(slot(q), w.rearrange("e (p k) n -> (e p) (k n)", k=k)
                                         ).then_inc(ring_in[q % NSLOT], 16)
                r += 3 * (NE - LOOP_E)
            while r < len(plan):
                load(r)
                r += 1

            for n, (kind, half_, dst, landed, _, _) in enumerate(PAIR_SLOTS):
                if kind == "u":
                    sp.wait_ge(pv_mm, pair_no(DEPTH - 1, LT - 1, NI - 1) + 1)
                else:
                    freed(plan[R - NSLOT + (n if kind == "g" else n - 2)])
                sp.dma_start(dst, expert_weights(kind, DEPTH - 1, half_)).then_inc(landed, 16)
            with sp.Fori(0, PAIRS - 1) as it:
                for n, (kind, half_, dst, landed, _, read) in enumerate(PAIR_SLOTS):
                    older, loads = PAIR_SLOTS[n - 2][3:5]
                    wait_in_loop(sp, counts, c_in, 32, (read, it + (PAIR_BASE + 1)),
                                 (older, 16 * it + 16 * (loads + (2 if n >= 2 else 1))))
                    w = {"d": w_down, "g": w_gate, "u": w_up}[kind][DEPTH - 1, bass.ds(2 * it + (2 + half_), 1)]
                    k = 4 if kind == "d" else KT
                    sp.dma_start(dst, w.rearrange("e (p k) n -> (e p) (k n)", k=k)).then_inc(landed, 16)

            sp.wait_ge(gt_mm, DEPTH)
            sp.dma_start(fgain, final_norm.partition_broadcast(P)).then_inc(fgain_in, 16)
            sp.wait_ge(scattered, 16 * NE * DEPTH)
            for t in range(LT):
                sp.dma_start(fx[t], x_s[t * P:(t + 1) * P, :]).then_inc(fx_in[t], 16)
            for t in range(LT):
                sp.wait_ge(out_done, t + 1)
                sp.dma_start(out[0, t * P:(t + 1) * P, :], fx[t]).then_inc(out_stored, 16)
            sp.wait_ge(out_stored, 16 * LT)

        @block.gpsimd
        def _(pool):
            own = Steps(pool, pool_did)
            counts = [pool.alloc_register(f"pool_count{n}") for n in range(2)]

            def power(dst, src, n):
                return pool.tensor_tensor(dst, src, half[:, 0:n], ALU.pow)

            pool.memset(half[:], -0.5).then_inc(zeroed, 1)
            pool.memset(csil[:], 0.0).then_inc(zeroed, 1)
            pool.memset(qz[:], 0.0).then_inc(zeroed, 1)
            col = "(p k) -> p k"
            def projection_weights(l):
                with nc.allow_non_contiguous_dma(reason="a few columns"):
                    pool.dma_start(wuq[:].rearrange("p (k n) -> p k n", k=2),
                                   w_uq[l].rearrange("(p k) n -> p k n", k=2)).then_inc(wproj_in, 16)
                    pool.dma_start(wukv[:], w_ukv[l]).then_inc(wproj_in, 16)
                    pool.dma_start(gcol[:, 0:2], q_norm[l].rearrange(col, k=2)).then_inc(wproj_in, 16)
                    pool.dma_start(gcol[:, 2:3], kv_norm[l].rearrange(col, k=1)).then_inc(wproj_in, 16)
                    pool.dma_start(dgain[:], diff_norm[l].partition_broadcast(P)).then_inc(wproj_in, 16)
                    for n, v in enumerate((lam_q1, lam_k1, lam_q2, lam_k2)):
                        pool.dma_start(lamb[:, n * C_DH:(n + 1) * C_DH],
                                       v[l].partition_broadcast(P)).then_inc(wproj_in, 16)

            def later_inputs():
                pool.dma_start(sinkb[:, 0:DEPTH * A_HEADS],
                               sink.rearrange("l h -> (l h)").partition_broadcast(P)).then_inc(sink_in, 16)
                for i in range(2):
                    for l in range(DEPTH):
                        pool.dma_start(mod_s[l, i:i + 1, :], b_ada[l:l + 1, :]).then_inc(mod_init, 16)

            def modulation_columns(l, part):
                for n in range(2):
                    for i in range(2):
                        m = 3 * part + n
                        pool.dma_start(modc[:, ((2 * part + n) * 2 + i) * KT:((2 * part + n) * 2 + i + 1) * KT],
                                       mod_s[l, i, m * D:(m + 1) * D].rearrange(col, k=KT)).then_inc(modc_in, 16)

            def store_modulation(n):
                l, ch = ada_items[n][1:]
                pool.wait_ge(ada_out, n - ADA_FIRST + 1)
                if n == ADA_FIRST:
                    pool.wait_ge(mod_init, 64)
                pool.dma_start(mod_s[l, :, 512 * ch:512 * ch + 512], msum[0:2, :],
                               accum_op=ALU.add).then_inc(mod_stored, 16)

            def norm_power(n):
                pool.wait_ge(ms_done, n + 1)
                power(rstd[:, n % 2:n % 2 + 1], msq[:, n % 2:n % 2 + 1], 1).then_inc(rstd_done, 1)

            norms = 0
            for l in range(DEPTH):
                if l == 0:
                    norm_power(0)
                    projection_weights(0)
                    later_inputs()
                def pad_queries(qi):
                    pool.wait_ge(small_ev, small_count(l, qi))
                    g = ATT.index((l, qi))
                    if g >= 2:
                        pl, pq = ATT[g - 2]
                        pool.wait_ge(s_mm, step_no(pl, pq, NS - 1) + 1)
                    z = qz[:, (g % 2) * 16 * P:(g % 2 + 1) * 16 * P].rearrange("p (h t) -> p h t", h=16)
                    cols = slice(qi * P, (qi + 1) * P)
                    for k in range(2):
                        own.did(pool.tensor_copy(z[64 * k:64 * k + 64, 4 * k:4 * k + 4, :],
                                                 qk_t[64 * k:64 * k + 64, B_AQ:B_AQ + 4, cols]))
                    for r in range(4):
                        last = pool.tensor_copy(z[32 * r:32 * r + 32, 8 + r:16:4, :],
                                                qk_t[32 * r:32 * r + 32, B_CQ:B_CQ + 2, cols])
                        if r < 3:
                            own.did(last)
                    last.then_inc(qz_done, 1)
                    pool.wait_ge(qz_done, g + 1)

                if l == 0:
                    pool.wait_ge(zeroed, 3)
                for t in range(NT + 1):
                    if t < NT:
                        if norms + t:
                            norm_power(norms + t)
                    if t >= 1:
                        n = tile_no(l, t - 1)
                        pool.wait_ge(ms2_done, n + 1)
                        a = int(keys_only(l, t - 1))
                        power(rs2[:, a:2], ms2[:, a:2], 2 - a).then_inc(rs2_done, 1)
                    if t in (3, 4):
                        pad_queries(t - 3)
                norms += NT

                for qi in range(nq(l)):
                    g = ATT.index((l, qi))
                    if 2 <= qi + 1 < nq(l):
                        pad_queries(qi + 1)
                    for j in range(NS):
                        n = ada_sum_at(l, qi, j)
                        if n is not None:
                            store_modulation(n)
                    pool.wait_ge(cms_done, g + 1)
                    power(crs, cms, 4).then_inc(crs_done, 1)

                pool.wait_ge(mod_stored, 16 * (len(ada_items) - ADA_FIRST))
                modulation_columns(l, 1)
                pool.wait_ge(otd_ev, len([a for a in ATT if a[0] <= l]))
                pool.wait_ge(ota_ev, len([a for a in ATT if a[0] <= l]))
                for i in range(2):
                    pool.dma_start(g1[:, i, :], mod_s[l, i, 2 * D:3 * D].partition_broadcast(P)).then_inc(g1_in, 16)
                pool.dma_start(wr[:].rearrange("p (k n) -> p k n", k=KT),
                               w_router[l].rearrange("(p k) n -> p k n", k=KT)).then_inc(g1_in, 16)
                for t in range(nq(l) + 1):
                    g = tile_no(l, t)
                    if t < nq(l):
                        pool.wait_ge(xhat, norms + max(0, t - 1))
                        if t >= 2:
                            pool.wait_ge(xs_stored, 16 * (g - 1))
                        pool.dma_start(xt[:, (t % 2) * D:(t % 2 + 1) * D], tile_rows(l, t)).then_inc(xo_in[t % 2], 16)
                    if t >= 1:
                        g = tile_no(l, t - 1)
                        b = (t - 1) % 2
                        pool.wait_ge(xo_done, g + 1)
                        pool.dma_start(x_s[(t - 1) * P:t * P, :], xt[:, b * D:(b + 1) * D]).then_inc(xs_stored, 16)
                        norm_power(norms + t - 1)
                        pool.wait_ge(xhat, norms + t)
                        pool.dma_start(h2_s[(t - 1) * P:t * P, :], hx[:]).then_inc(h2_stored, 16)
                norms += nq(l)

                pool.wait_ge(wo_mm, 2 * tile_no(l, nq(l) - 1) + 2)
                pool.dma_start(g2[0:CAP_L, :], mod_s[l, 0, 5 * D:6 * D].partition_broadcast(CAP_L)).then_inc(g2_in, 16)
                more, i = (CAP_C, 1) if nq(l) > LT else (CAP_L, 0)
                pool.dma_start(g2[CAP_L:CAP_L + more, :],
                               mod_s[l, i, 5 * D:6 * D].partition_broadcast(more)).then_inc(g2_in, 16)
                pool.wait_ge(h2_stored, 16 * (tile_no(l, nq(l) - 1) + 1))
                pool.wait_ge(xs_stored, 16 * (tile_no(l, nq(l) - 1) + 1))
                pool.wait_ge(gi_done, l + 1)
                rows = CAP_L + (CAP_C if nq(l) > LT else 0)

                def step(e, n, bidx, first):
                    if bidx < NE:
                        if not (l == 0 and first and bidx < 2):
                            pool.wait_ge(xgt_mm, n - 1)
                        if not (l == 0 and first and bidx < 4):
                            pool.wait_ge(scattered, (n - 3) * 16)
                        ic = ix[0:rows, bidx % 4:bidx % 4 + 1]
                        ins = pool.tensor_copy(ic, gidx[0:rows, bass.ds(e, 1)])
                        ins.then_inc(pool_did, 1)
                        own.n += 1
                        wait_in_loop(pool, counts, gi_done, l + 1, (pool_did, own.base + own.n))
                        pool.indirect_dma_start(
                            out=xg[bidx % 2][0:rows, :], out_offset=None, in_=h2_s[:, :],
                            in_offset=bass.IndirectOffsetOnAxis(ap=ic, axis=0)).then_inc(xg_in[bidx % 2], 16)
                    if not first or bidx >= 3:
                        before = [] if l == 0 and first and bidx == 3 else [(scattered, (n - 3) * 16)]
                        wait_in_loop(pool, counts, gi_done, l + 1, (y_done, n - 2), *before)
                        pool.indirect_dma_start(
                            out=x_s[:, :],
                            out_offset=bass.IndirectOffsetOnAxis(
                                ap=ix[0:rows, (bidx - 3) % 4:(bidx - 3) % 4 + 1], axis=0),
                            in_=y[(bidx - 3) % 2][0:rows, :], in_offset=None, compute_op=ALU.add
                        ).then_inc(scattered, 16)

                if l == DEPTH - 1:
                    break
                for e in range(LOOP_E):
                    step(e, l * NE + e, e, True)
                projection_weights(l + 1)
                modulation_columns(l + 1, 0)
                start = own.n
                with pool.Fori(0, (NE - LOOP_E) // BODY) as it:
                    own.base = it * BODY
                    for b in range(BODY):
                        e = BODY * it + (LOOP_E + b)
                        step(e, e + l * NE, LOOP_E + b, False)
                own.base, own.n = 0, start + NE - LOOP_E
                for e in range(NE, NE + 3):
                    step(e, l * NE + e, e, False)

            def gather(p):
                ic = ix[:, 2 * p:2 * p + 1]
                pool.tensor_copy(ic, gidx[:, p:p + 1])
                own.did(pool.tensor_copy(ix[0:CAP_L, 2 * p + 1:2 * p + 2], gidx[0:CAP_L, PAIRS + p:PAIRS + p + 1]))
                pool.wait_ge(xgt_mm, PAIR_BASE + p - 1)
                pool.indirect_dma_start(
                    out=xg[p % 2], out_offset=None, in_=h2_s[:, :],
                    in_offset=bass.IndirectOffsetOnAxis(ap=ic, axis=0)).then_inc(xg_in[p % 2], 16)

            def scatter(p):
                for h in range(2):
                    pool.wait_ge(y_done, PAIR_BASE + p + 1)
                    pool.wait_ge(scattered, 16 * (PAIR_BASE + 2 * p + h))
                    pool.indirect_dma_start(
                        out=x_s[:, :],
                        out_offset=bass.IndirectOffsetOnAxis(ap=ix[0:CAP_L, 2 * p + h:2 * p + h + 1], axis=0),
                        in_=y[p % 2][CAP_L * h:CAP_L * (h + 1), :], in_offset=None, compute_op=ALU.add
                    ).then_inc(scattered, 16)

            gather(0)
            gather(1)
            for p in range(PAIRS):
                scatter(p)
                if p + 2 < PAIRS:
                    gather(p + 2)

            for t in range(LT):
                pool.wait_ge(fms_done, t + 1)
                power(frs[:, t:t + 1], fms[:, t:t + 1], 1).then_inc(frs_done, 1)

        @block.scalar
        def _(act):
            act.wait_ge(c_in, 32)
            act.activation(ctmp[:, 16:32], ctmp[:, 0:16], ACT.Exp, scale=-1.0).then_inc(csil_e, 1)

            def ada_evacuate(n):
                act.wait_ge(ada_sum, n + 1)
                if n > ADA_FIRST:
                    act.wait_ge(mod_stored, 16 * (n - ADA_FIRST))
                act.copy(msum[0:2, :], ps[0:2, 7, :]).then_inc(ada_out, 1)

            def lambda_exps(l):
                act.wait_ge(lam_p, l + 1)
                act.activation(lamb[:, 4 * C_DH + 2:4 * C_DH + 4], lamb[:, 4 * C_DH:4 * C_DH + 2],
                               ACT.Exp).then_inc(lam_e, 1)

            norms = 0
            for l in range(DEPTH):
                def square(t):
                    act.wait_ge(x_in[t % 2], 16 * (tile_no(l, t) // 2 + 1))
                    if norms + t >= 2:
                        act.wait_ge(ms_done, norms + t - 1)
                    if norms + t >= 1:
                        act.wait_ge(xhat, norms + t)
                        act.wait_ge(t1_mm, norms + t)
                    if l and t == 0:
                        act.wait_ge(h2_stored, 16 * tile_no(0, NT))
                    act.activation(hx[:], xt[:, (t % 2) * D:(t % 2 + 1) * D], ACT.Square,
                                   accum_out=ss[:, (norms + t) % 2:(norms + t) % 2 + 1]).then_inc(sumsq, 1)

                def main_evacuate(t, ch):
                    n = tile_no(l, t)
                    p = pt[n % 2]
                    if ch == 0 and n >= 2:
                        act.wait_ge(small_mm, small_count(*tile_before(l, t, 2)))
                    if chunk_cols(l, t, ch)[0] == chunk_cols(l, t, ch)[1]:
                        return
                    act.wait_ge(main_mm, main_count(l, t, ch))
                    if ch == 0 and l and t < 2:
                        act.wait_ge(gt_mm, l)
                    if l and t == 0 and ch == 1:
                        act.wait_ge(down_mm, l * NE)
                        act.wait_ge(scattered, 16 * NE * l)
                    src = ps[:, ch, :]
                    if ch == 0:
                        last = act.copy(p[:, QA:KA].rearrange("p (h k d) -> p k h d", k=2, d=HD),
                                        src.rearrange("p (k h d) -> p k h d", k=2, d=HD))
                    elif ch == 1:
                        act.copy(p[:, KA:VA], src[:, 0:VA - 512])
                        last = act.copy(va[:, t, :], src[:, VA - 512:CQ - 512])
                        if not keys_only(l, t):
                            last = act.copy(p[:, CQ:CKV], src[:, CQ - 512:512])
                    elif ch == 2:
                        b = chunk_cols(l, t, ch)[1]
                        last = act.copy(p[:, CKV:b], src[:, 0:b - CKV])
                    else:
                        act.copy(p[:, KD:VD], src[:, 0:VD - KD])
                        last = act.copy(vc[:, t, :], src[:, VD - KD:512])
                    last.then_inc(main_ev, 1)

                def squares2(t):
                    n = tile_no(l, t)
                    p = pt[n % 2]
                    act.wait_ge(main_ev, main_count(l, t, 3))
                    if n >= 1:
                        act.wait_ge(ms2_done, n)
                        act.wait_ge(sq2, n)
                    last = act.activation(ps[:, 3, 256:384], p[:, CKV:KR], ACT.Square, accum_out=ss2[:, 1:2])
                    if not keys_only(l, t):
                        last = act.activation(ps[:, 3, 0:256], p[:, CQ:CKV], ACT.Square, accum_out=ss2[:, 0:1])
                    last.then_inc(sq2, 1)

                def small_evacuate(t, u):
                    if u not in small_uses(l, t):
                        return
                    n = tile_no(l, t)
                    act.wait_ge(small_mm, small_count(l, t, u))
                    src = ps[:, 6 + u % 2, :]
                    cols = slice(t * P, (t + 1) * P)
                    if u == 0:
                        if t == 0:
                            act.wait_ge(wproj_in, 16 * 9 * (l + 1))
                        if n >= 1:
                            act.wait_ge(small_mm, small_count(*tile_before(l, t), 2))
                        for k in range(2 if keys_only(l, t) else 0, 3):
                            last = act.activation(c_t[:, k, :], src[:, k * P:(k + 1) * P], ACT.Identity,
                                                  scale=gcol[:, k:k + 1])
                    elif u == 1:
                        if n >= 1:
                            act.wait_ge(small_mm, small_count(*tile_before(l, t)))
                        last = act.copy(q96, src[:, 0:384].rearrange("p (h d) -> p h d", h=B_HEADS))
                    elif u == 2:
                        if keys_only(l, t):
                            act.wait_ge(small_mm, small_count(*tile_before(l, t)))
                        kv = src.rearrange("p (h d) -> p h d", h=B_HEADS)
                        act.copy(k96[:, :, 0:B_NOPE], kv[:, :, 0:B_NOPE])
                        last = act.copy(vb[:, t, :].rearrange("p (h d) -> p h d", h=B_HEADS), kv[:, :, B_NOPE:])
                    else:
                        b0, nb, rows = [(0, 4, P), (4, 4, P), (8, 1, P), (9, 4, B_QK), (13, 4, B_QK)][u - 3]
                        gap = 3 if u == 4 and keys_only(l, t) else 1
                        last = act.copy(qk_t[0:rows, b0:b0 + nb:gap, cols],
                                        src[0:rows, 0:nb * P].rearrange("p (b t) -> p b t", b=nb)[:, ::gap, :])
                    last.then_inc(small_ev, 1)

                def load_x(t):
                    act.dma_start(xt[:, (t % 2) * D:(t % 2 + 1) * D], tile_rows(l, t)).then_inc(x_in[t % 2], 16)

                if l:
                    act.wait_ge(xs_stored, 16 * tile_no(0, NT))
                    act.wait_ge(scattered, 16 * NE * l)
                    load_x(0)
                    load_x(1)
                square(0)
                lambda_exps(l)
                for t in range(NT + 1):
                    if t + 1 < NT:
                        square(t + 1)
                    for ch in range(NCH):
                        if t < NT:
                            main_evacuate(t, ch)
                        if ch == 0 and t + 2 < NT:
                            act.wait_ge(xhat, norms + t + 1)
                            load_x(t + 2)
                        if t >= 1:
                            if ch == 0:
                                small_evacuate(t - 1, 0)
                            elif ch == 1:
                                small_evacuate(t - 1, 1)
                                small_evacuate(t - 1, 2)
                            elif ch == 2:
                                for u in range(3, 8):
                                    small_evacuate(t - 1, u)
                        if t < NT and ch == 3:
                            squares2(t)
                norms += NT

                def softmax(s):
                    ll, qi, j = s
                    n = step_no(ll, qi, j)
                    kind, h, m = STEPS[j]
                    kt = key_tiles(ll, qi, kind)
                    c0, c1 = kt[0][1], TOK + (kind == "A")
                    scale = {"A": HD, "B": B_QK, "C": C_DH}[kind] ** -0.5
                    act.wait_ge(neg_done, n + 1)
                    if n >= 3:
                        pl, pq, pj = sprev(s, 3)
                        act.wait_ge(t_mm, item_no(pl, pq, ITEM[pj]) + 1)
                    act.activation(prob[n % 3][:, c0:c1], bank(2 * (n % 2), 2)[:, c0:c1], ACT.Exp,
                                   bias=negm[:, j:j + 1], scale=scale,
                                   accum_out=sums[:, j:j + 1]).then_inc(exp_done, 1)

                seq = [(l, qi, j) for qi in range(nq(l)) for j in range(NS)]

                def sprev(s, k):
                    full = [(a, b, jj) for a, b in ATT for jj in range(NS)]
                    return full[full.index(s) - k]

                def output_half(qi):
                    g = ATT.index((l, qi))
                    act.wait_ge(ot_mm, g + 1)
                    act.copy(qk_t[:, OT_BLOCK[0]:OT_BLOCK[3] + 1, qi * P:(qi + 1) * P],
                             bank(4).rearrange("p (b t) -> p b t", b=4)).then_inc(ota_ev, 1)

                def values_evacuate(pair):
                    if pair is None:
                        return
                    n = pair_no(l, *pair)
                    act.wait_ge(pv_mm, n + 1)
                    if n >= 2:
                        act.wait_ge(back_mm, n - 1)
                    act.copy(ov[n % 2], ps[:, 6, 0:P]).then_inc(ov_ev, 1)

                softmax(seq[0])
                softmax(seq[1])
                for k, s in enumerate(seq):
                    _, qi, j = s
                    kind = STEPS[j][0]
                    if k + 2 < len(seq) and kind == "C":
                        softmax(seq[k + 2])
                    if LASTSTEP[j]:
                        i = item_no(l, qi, ITEM[j])
                        nb = act_share(len(key_tiles(l, qi, kind)))
                        act.wait_ge(t_mm, i + 1)
                        if i >= 4:
                            act.wait_ge(pv_mm, i // 2 - 1)
                        act.copy(prob_t[i % 4][:, 0:nb, :],
                                 bank(4)[:, 0:nb * P].rearrange("p (b t) -> p b t", b=nb)).then_inc(pta_ev, 1)
                    if k + 2 < len(seq) and kind != "C":
                        softmax(seq[k + 2])
                    if LASTSTEP[j] and ITEM[j] % 2 == 0:
                        values_evacuate(pair_behind(l, qi, ITEM[j], 1))
                    if qi and LASTSTEP[j] and ITEM[j] == OT_AFTER:
                        output_half(qi - 1)
                    n = ada_sum_at(l, qi, j)
                    if n is not None:
                        ada_evacuate(n)
                values_evacuate((nq(l) - 1, NI - 2))
                output_half(nq(l) - 1)

                def square_o(t):
                    n = norms + t
                    act.wait_ge(xo_done, tile_no(l, t) + 1)
                    act.wait_ge(ms_done, n - 1)
                    act.wait_ge(t1_mm, n)
                    if t:
                        act.wait_ge(h2_stored, 16 * tile_no(l, t))
                    act.activation(hx[:], xt[:, (t % 2) * D:(t % 2 + 1) * D], ACT.Square,
                                   accum_out=ss[:, n % 2:n % 2 + 1]).then_inc(sumsq, 1)

                def router_exp(t):
                    act.wait_ge(rmax_done, tile_no(l, t) + 1)
                    act.activation(aff_e, ps[:, 6, 0:NE], ACT.Exp, bias=rmx, accum_out=rsum).then_inc(rexp_done, 1)

                def affinity_store(t):
                    g = tile_no(l, t)
                    act.wait_ge(at_mm, g + 1)
                    act.copy(rtop[0:NE, t * P:(t + 1) * P], ps[0:NE, 7, 0:P]).then_inc(at_ev, 1)

                for t in range(nq(l) + 2):
                    if t >= 2:
                        affinity_store(t - 2)
                    if t < nq(l):
                        square_o(t)
                    if 1 <= t <= nq(l):
                        router_exp(t - 1)
                norms += nq(l)
                rows = CAP_L + (CAP_C if nq(l) > LT else 0)
                act.wait_ge(gt_mm, l + 1)
                if l:
                    act.wait_ge(y_done, NE)
                if l == DEPTH - 1:
                    act.copy(gval[0:CAP_L, 0:PAIRS], ps[0:CAP_L, 6, 0:NE:2])
                    act.copy(gval[CAP_L:P, 0:PAIRS], ps[CAP_L:P, 6, 1:NE:2]).then_inc(gv_done, 1)
                    break
                act.copy(gval[0:rows, :], ps[0:rows, 6, 0:NE]).then_inc(gv_done, 1)

                def step(n, b, first):
                    if b < NE:
                        act.wait_ge(gate_mm, n + 1)
                        if not (l == 0 and first and b == 0):
                            act.wait_ge(hid_done, n)
                        act.activation(sg[0:rows, :], ps[0:rows, 2, :], ACT.Silu).then_inc(silu_done, 1)
                    if not first or b >= 1:
                        act.wait_ge(hidt_mm, n)
                        if not (l == 0 and first and b < 3):
                            act.wait_ge(down_mm, n - 2)
                        act.copy(hid_t[(b - 1) % 2][:, :, 0:rows],
                                 ps[:, 4, 0:4 * rows].rearrange("p (k t) -> p k t", k=4)).then_inc(hidt_ev, 1)

                for e in range(LOOP_E):
                    step(l * NE + e, e, True)
                with act.Fori(0, (NE - LOOP_E) // BODY) as it:
                    for b in range(BODY):
                        step(BODY * it + (l * NE + LOOP_E + b), LOOP_E + b, False)
                step(l * NE + NE, NE, False)

            with act.Fori(0, PAIRS // 2) as it:
                for b in range(2):
                    n = 2 * it + (PAIR_BASE + b)
                    act.wait_ge(gate_mm, n + 1)
                    act.wait_ge(hid_done, n)
                    act.activation(sg, ps[:, 2, :], ACT.Silu).then_inc(silu_done, 1)
                    act.wait_ge(hidt_mm, n + 1)
                    act.wait_ge(down_mm, n - 1)
                    act.copy(hid_t[b], ps[:, 4, :].rearrange("p (k t) -> p k t", k=4)).then_inc(hidt_ev, 1)

            act.wait_ge(xgt_ev, PAIR_BASE + PAIRS)
            for t in range(LT):
                act.wait_ge(fx_in[t], 16)
                if t:
                    act.wait_ge(fss_done, t)
                act.activation(bank(0, 2), fx[t], ACT.Square, accum_out=fss[:, t:t + 1]).then_inc(fss_done, 1)

        @block.vector
        def _(dve):
            own = Steps(dve, dve_did)

            dve.wait_ge(csil_e, 1)
            own.did(dve.tensor_scalar(ctmp[:, 16:32], ctmp[:, 16:32], 1.0, None, ALU.add))
            own.did(dve.reciprocal(ctmp[:, 32:48], ctmp[:, 16:32]))
            dve.wait_ge(zeroed, 2)
            dve.tensor_tensor(csil[:].rearrange("p (k i) -> p k i", k=KT)[:, :, 0:2],
                              ctmp[:, 0:16].rearrange("p (i k) -> p k i", i=2),
                              ctmp[:, 32:48].rearrange("p (i k) -> p k i", i=2), ALU.mult).then_inc(csil_done, 1)

            def ada_copy(n):
                dve.wait_ge(ada_mm, n + 1)
                if n >= 1:
                    dve.wait_ge(ada_sum, n)
                dve.tensor_copy(modrow[:], ps[:, 7, :]).then_inc(ada_row, 1)

            def lambda_products(l):
                dve.wait_ge(wproj_in, 16 * 9 * (l + 1))
                q = lamb[:, 0:4 * C_DH].rearrange("p (n d) -> p n d", n=4)
                s = lamb[:, 4 * C_DH:]
                own.did(dve.tensor_tensor(q[:, 0:4:2, :], q[:, 0:4:2, :], q[:, 1:4:2, :], ALU.mult))
                dve.tensor_reduce(s[:, 0:2], q[:, 0:4:2, :], AX_X, ALU.add).then_inc(lam_p, 1)
                dve.wait_ge(lam_e, l + 1)
                own.did(dve.tensor_tensor(s[:, 4:5], s[:, 3:4], s[:, 2:3], ALU.subtract))
                own.did(dve.tensor_scalar(s[:, 5:6], s[:, 4:5], -lam_init(l), None, ALU.add))
                own.did(dve.tensor_scalar(dgain[:], dgain[:], 1.0 - lam_init(l), None, ALU.mult))

            neg_lam = lamb[:, 4 * C_DH + 5:4 * C_DH + 6]
            mc = modc[:].rearrange("p (v i k) -> p v i k", v=4, i=2)

            def first_columns(n):
                dve.wait_ge(ada_sum, n + 1)
                rows, v = slice(64 * (n % 2), 64 * (n % 2) + 64), n // 2
                dve.tensor_tensor(mc[rows, v].rearrange("p i k -> p k i"),
                                  ps[rows, 6, 0:2 * KT].rearrange("p (k i) -> p k i", i=2),
                                  bcol[rows, v * KT:(v + 1) * KT].unsqueeze(2).to_broadcast([64, KT, 2]), ALU.add
                                  ).then_inc(first_cols, 1)

            def modulation(l, part):
                if l or part:
                    dve.wait_ge(modc_in, 16 * 4 * (2 * l + part))
                else:
                    dve.wait_ge(first_cols, ADA_FIRST)
                gain = ncol[:, (2 * part + l) * KT:(2 * part + l + 1) * KT].unsqueeze(1).to_broadcast([P, 2, KT])
                dve.scalar_tensor_tensor(out=mc[:, 2 * part + 1], in0=mc[:, 2 * part + 1], scalar=1.0, in1=gain,
                                         op0=ALU.add, op1=ALU.mult).then_inc(modc_done, 1)
                dve.wait_ge(modc_done, 2 * l + part + 1)

            def mean_square(n):
                dve.wait_ge(sumsq, n + 1)
                if n >= 2:
                    dve.wait_ge(rstd_done, n - 1)
                dve.tensor_scalar(msq[:, n % 2:n % 2 + 1], ss[:, n % 2:n % 2 + 1], 1.0 / D, EPS,
                                  ALU.mult, ALU.add).then_inc(ms_done, 1)

            def normalise(n, buf, dst):
                dve.wait_ge(rstd_done, n + 1)
                return dve.tensor_scalar(dst, xt[:, buf * D:(buf + 1) * D], rstd[:, n % 2:n % 2 + 1], None, ALU.mult)

            def modulate(n, dst, part, i):
                src = bank(4, 2).rearrange("p (k t) -> p k t", k=KT)
                halves = [slice(0, KT // 2), slice(KT // 2, KT)]

                def column(v, k):
                    return mc[:, v, i, k].unsqueeze(2).to_broadcast([P, KT // 2, P])

                for k, ready in zip(halves, (t1_half, t1_mm)):
                    dve.wait_ge(ready, n + 1)
                    own.count(dve.tensor_tensor(dst[:, k], src[:, k], column(2 * part + 1, k), ALU.mult))
                for back, k, done in zip((1, 0), halves, (h_half, h_done)):
                    own.wait(back)
                    dve.tensor_tensor(dst[:, k], dst[:, k], column(2 * part, k), ALU.add).then_inc(done, 1)

            def rope(v, units, nf, cos, sin):
                w = 4 * nf
                vv = v.rearrange("p (u w) -> p u w", w=w)
                v4 = v.rearrange("p (u a r f) -> p u a r f", a=2, r=2, f=nf)
                tm = rtmp[:, 0:units * w].rearrange("p (u a r f) -> p u a r f", a=2, r=2, f=nf)
                s4 = sin.rearrange("p (a r f) -> p a r f", a=2, r=2)
                for r in range(2):
                    own.did(dve.tensor_tensor(tm[:, :, :, r, :], v4[:, :, :, 1 - r, :],
                                              s4[:, :, r, :].unsqueeze(1).to_broadcast([P, units, 2, nf]), ALU.mult))
                own.did(dve.tensor_tensor(vv, vv, cos.unsqueeze(1).to_broadcast([P, units, w]), ALU.mult))
                return dve.tensor_tensor(v, v, rtmp[:, 0:units * w], ALU.add)

            norms = 0
            for l in range(DEPTH):
                def prepare(t):
                    n = norms + t
                    mean_square(n)
                    if n >= 1:
                        dve.wait_ge(t1_mm, n)
                    if l and t == 0:
                        dve.wait_ge(h2_stored, 16 * tile_no(0, NT))
                    normalise(n, t % 2, hx[:]).then_inc(xhat, 1)

                def modulated(t):
                    n = tile_no(l, t)
                    if n >= 2:
                        dve.wait_ge(main_mm, main_count(*tile_before(l, t, 2), 3))
                    if l and t < 2:
                        dve.wait_ge(gt_mm, l)
                    modulate(norms + t, h_t[n % 2], 0, int(t >= LT))

                def finish_b(t):
                    n = tile_no(l, t)
                    p = pt[n % 2]
                    dve.wait_ge(small_ev, small_count(l, t, 2))
                    if t < LT:
                        tm = rtmp[:, 0:B_HEADS * B_ROPE].rearrange("p (h a r f) -> p h a r f", a=2, r=2, f=8)
                        cos = kc[:, K_CB + t * 32:K_CB + t * 32 + 32]
                        sin = kc[:, K_SB + t * 32:K_SB + t * 32 + 32].rearrange("p (a r f) -> p a r f", a=2, r=2)
                        qr = q96[:, :, B_NOPE:]
                        q5 = qr.rearrange("p h (a r f) -> p h a r f", a=2, r=2)
                        for r in range(2):
                            own.did(dve.tensor_tensor(
                                tm[:, :, :, r, :], q5[:, :, :, 1 - r, :],
                                sin[:, :, r, :].unsqueeze(1).to_broadcast([P, B_HEADS, 2, 8]), ALU.mult))
                        own.did(dve.tensor_tensor(qr, qr, cos.unsqueeze(1).to_broadcast([P, B_HEADS, 32]), ALU.mult))
                        own.did(dve.tensor_tensor(
                            qr, qr, rtmp[:, 0:B_HEADS * B_ROPE].rearrange("p (h d) -> p h d", h=B_HEADS), ALU.add))
                    dve.tensor_copy(k96[:, :, B_NOPE:], p[:, KR:QD].unsqueeze(1).to_broadcast([P, B_HEADS, B_ROPE])
                                    ).then_inc(rope_b, 1)

                def finish_main(t):
                    n = tile_no(l, t)
                    p = pt[n % 2]
                    dve.wait_ge(sq2, n + 1)
                    if n >= 1:
                        dve.wait_ge(rs2_done, n)
                    if not keys_only(l, t):
                        dve.tensor_scalar(ms2[:, 0:1], ss2[:, 0:1], 1.0 / B_QR, EPS, ALU.mult, ALU.add)
                    dve.tensor_scalar(ms2[:, 1:2], ss2[:, 1:2], 1.0 / B_KVR, EPS, ALU.mult, ALU.add
                                      ).then_inc(ms2_done, 1)
                    dve.wait_ge(rs2_done, n + 1)
                    if not keys_only(l, t):
                        dve.tensor_scalar(p[:, CQ:CKV], p[:, CQ:CKV], rs2[:, 0:1], None, ALU.mult)
                    dve.tensor_scalar(p[:, CKV:KR], p[:, CKV:KR], rs2[:, 1:2], None, ALU.mult).then_inc(cqn, 1)
                    if t < LT:
                        own.did(rope(p[:, QA:VA], A_HEADS + A_KV, 16, kc[:, K_CA + t * 64:K_CA + t * 64 + 64],
                                     kc[:, K_SA + t * 64:K_SA + t * 64 + 64]))
                    dve.wait_ge(main_ev, main_count(l, t, 3))
                    if t < LT:
                        rope(p[:, KR:VD], 1 + 2 * 2 * C_HEADS, 8, kc[:, K_CB + t * 32:K_CB + t * 32 + 32],
                             kc[:, K_SB + t * 32:K_SB + t * 32 + 32]).then_inc(rope_ac, 1)
                        dve.wait_ge(rope_ac, n + 1)
                    else:
                        dve.tensor_copy(rtmp[:, 0:2], p[:, KR:KR + 2]).then_inc(rope_ac, 1)
                        dve.wait_ge(rope_ac, n + 1)

                if l == 0:
                    for n in range(ADA_FIRST):
                        ada_copy(n)
                        if n == 0:
                            dve.wait_ge(cols_in, 16 * 3)
                        first_columns(n)
                        if n == 1:
                            prepare(0)
                else:
                    prepare(0)
                modulation(l, 0)
                modulated(0)
                lambda_products(l)
                if l == 0:
                    dve.wait_ge(sink_in, 16)
                    dve.tensor_scalar(sinkb[:, NSK:2 * NSK], sinkb[:, 0:NSK], float(HD ** 0.5), None, ALU.mult
                                      ).then_inc(sink_done, 1)
                for t in range(NT + 1):
                    if t + 1 < NT:
                        prepare(t + 1)
                    if t >= 1:
                        finish_b(t - 1)
                    if t + 1 < NT:
                        modulated(t + 1)
                    if t < NT:
                        finish_main(t)
                norms += NT

                def row_max(s):
                    _, qi, j = s
                    n = step_no(l, qi, j)
                    kind, h, m = STEPS[j]
                    kt = key_tiles(l, qi, kind)
                    c0, c1 = kt[0][1], TOK + (kind == "A")
                    scale = {"A": HD, "B": B_QK, "C": C_DH}[kind] ** -0.5
                    sc = bank(2 * (n % 2), 2)
                    dve.wait_ge(s_mm, n + 1)
                    if kind == "A" and qi < LT:
                        if 0 < qi < LT - 1:
                            v = sc[:, 0:512].rearrange("p (b t) -> p b t", b=4)[:, 1:4:2, :]
                            mk = kc[:, K_MASK:K_MASK + 2 * P].rearrange("p (b t) -> p b t", b=2)
                        elif qi:
                            v, mk = sc[:, c0:c0 + P], kc[:, K_MASK:K_MASK + P]
                        else:
                            v, mk = sc[:, SEQ - P:SEQ], kc[:, K_MASK + P:K_MASK + 2 * P]
                        own.did(dve.tensor_tensor(v, v, mk, ALU.add))
                    own.did(dve.tensor_reduce(mx[:, n % 2:n % 2 + 1], sc[:, c0:c1], AX_X, ALU.max))
                    dve.tensor_scalar(negm[:, j:j + 1], mx[:, n % 2:n % 2 + 1], -scale, None, ALU.mult
                                      ).then_inc(neg_done, 1)

                seq = [(l, qi, j) for qi in range(nq(l)) for j in range(NS)]
                def finish_pair(pair):
                    if pair is None:
                        return
                    qi, i = pair
                    g = ATT.index((l, qi))
                    n = pair_no(l, qi, i)
                    j = ITEM.index(i)
                    src = sums[:, j:j + 2] if i < 12 else sums[:, j:j + 3:2]
                    own.did(dve.reciprocal(rinv[:, i:i + 2], src))
                    dve.wait_ge(back_mm, n + 1)
                    if i == 0 and g >= 2:
                        dve.wait_ge(ot_mm, g - 1)
                    dve.tensor_tensor(ob[g % 2][:, i * 64:(i + 2) * 64].rearrange("p (h d) -> p h d", h=2),
                                      ps[:, 6, P:2 * P].rearrange("p (h d) -> p h d", h=2),
                                      rinv[:, i:i + 2].unsqueeze(2).to_broadcast([P, 2, 64]), ALU.mult
                                      ).then_inc(o_ev, 1)
                    if i == NI - 2:
                        norm_c(qi)

                def norm_c(qi):
                    g = ATT.index((l, qi))
                    dve.wait_ge(o_ev, pair_no(l, qi, NI - 1) + 1)
                    oc = ob[g % 2][:, 768:1024].rearrange("p (h d) -> p h d", h=C_HEADS)
                    cq3 = csq.rearrange("p (h d) -> p h d", h=C_HEADS)
                    own.did(dve.tensor_tensor(cq3, oc, oc, ALU.mult))
                    own.did(dve.tensor_reduce(css, cq3, AX_X, ALU.add))
                    dve.tensor_scalar(cms, css, 1.0 / C_V, EPS, ALU.mult, ALU.add).then_inc(cms_done, 1)
                    own.did(dve.tensor_tensor(oc, oc, dgain[:].unsqueeze(1).to_broadcast([P, C_HEADS, C_V]),
                                              ALU.mult))

                def scale_c(qi):
                    g = ATT.index((l, qi))
                    oc = ob[g % 2][:, 768:1024].rearrange("p (h d) -> p h d", h=C_HEADS)
                    dve.wait_ge(crs_done, g + 1)
                    dve.tensor_tensor(oc, oc, crs.unsqueeze(2).to_broadcast([P, C_HEADS, C_V]), ALU.mult
                                      ).then_inc(on_done, 1)

                def output_half(qi):
                    g = ATT.index((l, qi))
                    dve.wait_ge(ot_mm, g + 1)
                    for b in (4, 6):
                        last = dve.tensor_copy(qk_t[:, OT_BLOCK[b]:OT_BLOCK[b] + 2, qi * P:(qi + 1) * P],
                                               bank(5)[:, (b - 4) * P:(b - 2) * P].rearrange("p (b t) -> p b t", b=2))
                    last.then_inc(otd_ev, 1)

                row_max(seq[0])
                row_max(seq[1])
                for k, s in enumerate(seq):
                    _, qi, j = s
                    n = step_no(l, qi, j)
                    kind, h, m = STEPS[j]
                    it = item_no(l, qi, ITEM[j])
                    if kind == "C" and m == 0:
                        dve.wait_ge(exp_done, n + 2)
                        own.did(dve.reciprocal(r1[:, h:h + 1], sums[:, j + 1:j + 2]))
                        own.did(dve.scalar_tensor_tensor(out=cc[:, h:h + 1], in0=sums[:, j:j + 1], scalar=r1[:, h:h + 1],
                                                         in1=neg_lam, op0=ALU.mult, op1=ALU.mult))
                        c0 = key_tiles(l, qi, kind)[0][1]
                        dve.scalar_tensor_tensor(out=prob[n % 3][:, c0:TOK], in0=prob[(n + 1) % 3][:, c0:TOK],
                                                 scalar=cc[:, h:h + 1], in1=prob[n % 3][:, c0:TOK],
                                                 op0=ALU.mult, op1=ALU.add).then_inc(comb, 1)
                    if k + 2 < len(seq):
                        row_max(seq[k + 2])
                    if LASTSTEP[j]:
                        nb = len(key_tiles(l, qi, kind))
                        a = act_share(nb)
                        dve.wait_ge(t_mm, it + 1)
                        if it >= 4:
                            dve.wait_ge(pv_mm, it // 2 - 1)
                        dve.tensor_copy(prob_t[it % 4][:, a:nb, :],
                                        bank(5)[:, 0:(nb - a) * P].rearrange("p (b t) -> p b t", b=nb - a)
                                        ).then_inc(ptd_ev, 1)
                        if ITEM[j] % 2:
                            finish_pair(pair_behind(l, qi, ITEM[j], 1))
                        if qi and ITEM[j] == OT_AFTER - 1:
                            scale_c(qi - 1)
                        if qi and ITEM[j] == OT_AFTER:
                            output_half(qi - 1)
                    a = ada_at(l, qi, j)
                    if a is not None:
                        ada_copy(a)
                finish_pair((nq(l) - 1, NI - 2))
                scale_c(nq(l) - 1)
                output_half(nq(l) - 1)

                modulation(l, 1)
                dve.wait_ge(g1_in, 16 * 3 * (l + 1))

                def residual(t, extra):
                    g = tile_no(l, t)
                    n = norms + t
                    dve.wait_ge(xo_in[t % 2], 16 * (g // 2 + 1))
                    x2 = xt[:, (t % 2) * D:(t % 2 + 1) * D]
                    for h in range(2):
                        dve.wait_ge(wo_mm, 2 * g + h + 1)
                        own.did(dve.tensor_tensor(tmpo, ps[:, 2 * (g % 2) + h, :],
                                                  g1[:, int(t >= LT), h * 512:(h + 1) * 512], ALU.mult))
                        last = dve.tensor_tensor(x2[:, h * 512:(h + 1) * 512], x2[:, h * 512:(h + 1) * 512], tmpo,
                                                 ALU.add)
                        if h == 0:
                            own.did(last)
                            top_rounds(extra)
                        else:
                            last.then_inc(xo_done, 1)
                            dve.wait_ge(xo_done, g + 1)
                    mean_square(n)
                    normalise(n, t % 2, hx[:]).then_inc(xhat, 1)

                def modulated_rows(t):
                    if t:
                        dve.wait_ge(lg_mm, tile_no(l, t))
                    modulate(norms + t, h2_t, 1, int(t >= LT))

                def router_softmax(t):
                    g = tile_no(l, t)
                    dve.wait_ge(lg_mm, g + 1)
                    own.did(dve.tensor_reduce(rmx, ps[:, 6, 0:NE], AX_X, ALU.max))
                    dve.tensor_scalar(rmx, rmx, -1.0, None, ALU.mult).then_inc(rmax_done, 1)
                    dve.wait_ge(rexp_done, g + 1)
                    own.did(dve.reciprocal(rrec, rsum))
                    if t:
                        dve.wait_ge(at_mm, g)
                    dve.tensor_scalar(aff, aff_e, rrec, None, ALU.mult).then_inc(aff_done, 1)

                rows = CAP_L + (CAP_C if nq(l) > LT else 0)
                sets = [(0, SEQ, 0, CAP_L)] + ([(SEQ, TOK, CAP_L, CAP_C)] if nq(l) > LT else [])
                rounds = [(a, b, c0, r, r == cap // 8 - 1) for a, b, c0, cap in sets for r in range(cap // 8)]

                def top_rounds(n):
                    for _ in range(min(n, len(rounds))):
                        a, b, c0, r, done = rounds.pop(0)
                        if r == 0:
                            dve.wait_ge(at_ev, tile_no(l, b // P - 1) + 1)
                        o8 = slice(c0 + 8 * r, c0 + 8 * r + 8)
                        src, dst = (rtop, rtop2) if r % 2 == 0 else (rtop2, rtop)
                        own.did(dve.max(sval[0:NE, o8], src[0:NE, a:b]))
                        if not done:
                            own.count(dve.match_replace(dst[0:NE, a:b], sval[0:NE, o8], src[0:NE, a:b], -1.0))
                        own.count(dve.max_index(sidx[0:NE, o8], sval[0:NE, o8], src[0:NE, a:b]))
                        own.wait(0 if done else 1)

                beside = nq(l) > LT
                for t in range(nq(l)):
                    last_tile = beside and t == NT - 1
                    residual(t, 3 if last_tile else 0)
                    if t:
                        router_softmax(t - 1)
                    if last_tile:
                        top_rounds(1)
                    modulated_rows(t)
                if beside:
                    top_rounds(2)
                router_softmax(nq(l) - 1)
                norms += nq(l)
                top_rounds(len(rounds))
                last = dve.tensor_copy(sidx_f[0:NE, 0:CAP_L], sidx[0:NE, 0:CAP_L])
                if nq(l) > LT:
                    own.did(dve.tensor_copy(sidx_f[0:NE, CAP_L:rows], sidx[0:NE, CAP_L:rows]))
                    last = dve.tensor_scalar(sidx_f[0:NE, CAP_L:rows], sidx_f[0:NE, CAP_L:rows], float(SEQ), None,
                                             ALU.add)
                if l == DEPTH - 1:
                    dve.tensor_copy(sval[0:NE, CAP_L:P], sval[0:NE, 0:CAP_L])
                    last = dve.tensor_copy(sidx_f[0:NE, CAP_L:P], sidx[0:NE, 0:CAP_L])
                last.then_inc(top_done, 1)
                dve.wait_ge(gt_mm, l + 1)
                if l:
                    dve.wait_ge(scattered, 16 * NE)
                dve.wait_ge(gv_done, l + 1)
                if l == DEPTH - 1:
                    dve.tensor_copy(gidx[0:CAP_L, 0:PAIRS], ps[0:CAP_L, 6, NE:2 * NE:2])
                    dve.tensor_copy(gidx[0:CAP_L, PAIRS:NE], ps[0:CAP_L, 6, NE + 1:2 * NE:2])
                    dve.tensor_copy(gidx[CAP_L:P, 0:PAIRS], ps[CAP_L:P, 6, NE + 1:2 * NE:2]).then_inc(gi_done, 1)
                    dve.wait_ge(g2_in, 32 * (l + 1))
                    break
                dve.tensor_copy(gidx[0:rows, :], ps[0:rows, 6, NE:2 * NE]).then_inc(gi_done, 1)
                dve.wait_ge(g2_in, 32 * (l + 1))


                def step(n, e, b, first):
                    if b < NE:
                        dve.wait_ge(xgt_mm, n + 1)
                        if not (l == 0 and first and b < 2):
                            dve.wait_ge(up_mm, n - 1)
                        for i, (r0, r1_) in enumerate([(0, CAP_L), (CAP_L, rows)][:1 + (rows > CAP_L)]):
                            src = ps[:, 0:2, 0:4 * rows].rearrange("p b (k t) -> p b k t", k=4)[:, :, :, r0:r1_]
                            dst = xg_t[b % 2].rearrange("p (b k) t -> p b k t", b=2)[:, :, :, r0:r1_]
                            w = r1_ - r0
                            for bb in range(2):
                                a_ = mc[:, 3, i, 4 * bb:4 * bb + 4].unsqueeze(2).to_broadcast([P, 4, w])
                                own.did(dve.tensor_tensor(dst[:, bb], src[:, bb], a_, ALU.mult))
                            d = xg_t[b % 2][:, :, r0:r1_]
                            last = dve.tensor_tensor(d, d, mc[:, 2, i, :].unsqueeze(2).to_broadcast([P, KT, w]),
                                                     ALU.add)
                            if i == 0 and rows > CAP_L:
                                own.did(last)
                        last.then_inc(xgt_ev, 1)
                    if not first or b >= 2:
                        dve.wait_ge(down_mm, n - 1)
                        if not (l == 0 and first and b < 4):
                            dve.wait_ge(scattered, (n - 3) * 16)
                        gv = gval[0:rows, bass.ds(e - 2, 1)] if not isinstance(e, int) else gval[0:rows, e - 2:e - 1]
                        dve.scalar_tensor_tensor(out=y[b % 2][0:rows, :], in0=bank(5, 2)[0:rows, :], scalar=gv,
                                                 in1=g2[0:rows, :], op0=ALU.mult, op1=ALU.mult).then_inc(y_done, 1)
                    if b < NE:
                        dve.wait_ge(up_mm, n + 1)
                        dve.wait_ge(silu_done, n + 1)
                        if not (l == 0 and first and b < 2):
                            dve.wait_ge(hidt_mm, n - 1)
                        dve.tensor_tensor(hid[b % 2][0:rows, :], ps[0:rows, 3, :], sg[0:rows, :], ALU.mult
                                          ).then_inc(hid_done, 1)

                for e in range(LOOP_E):
                    step(l * NE + e, e, e, True)
                per = (3 if rows > CAP_L else 0) + 2
                start = own.n
                with dve.Fori(0, (NE - LOOP_E) // BODY) as it:
                    own.base = it * (per * BODY)
                    for b in range(BODY):
                        step(BODY * it + (l * NE + LOOP_E + b), BODY * it + (LOOP_E + b), LOOP_E + b, False)
                    assert own.n - start == per * BODY
                own.base = 0
                own.n = start + per * (NE - LOOP_E)
                for e in range(NE, NE + 2):
                    step(l * NE + e, e, e, False)

            start = own.n
            with dve.Fori(0, PAIRS // 2) as it:
                own.base = 4 * it
                for b in range(2):
                    n = 2 * it + (PAIR_BASE + b)
                    dve.wait_ge(xgt_mm, n + 1)
                    dve.wait_ge(up_mm, n - 1)
                    for bb in range(2):
                        a_ = mc[:, 3, 0, 4 * bb:4 * bb + 4].unsqueeze(2).to_broadcast([P, 4, P])
                        own.did(dve.tensor_tensor(xg_t[b][:, 4 * bb:4 * bb + 4, :],
                                                  ps[:, bb, :].rearrange("p (k t) -> p k t", k=4), a_, ALU.mult))
                    dve.tensor_tensor(xg_t[b], xg_t[b], mc[:, 2, 0, :].unsqueeze(2).to_broadcast([P, KT, P]),
                                      ALU.add).then_inc(xgt_ev, 1)
                    dve.wait_ge(up_mm, n + 1)
                    dve.wait_ge(silu_done, n + 1)
                    dve.wait_ge(hidt_mm, n - 1)
                    dve.tensor_tensor(hid[b], ps[:, 3, :], sg, ALU.mult).then_inc(hid_done, 1)
                    dve.wait_ge(down_mm, n + 1)
                    dve.wait_ge(scattered, 16 * (2 * (2 * it + b) + (PAIR_BASE - 2)))
                    dve.scalar_tensor_tensor(out=y[b], in0=bank(5, 2), scalar=gval[:, bass.ds(2 * it + b, 1)],
                                             in1=g2, op0=ALU.mult, op1=ALU.mult).then_inc(y_done, 1)
            own.base, own.n = 0, start + 2 * PAIRS

            def final_mean(t):
                dve.wait_ge(fss_done, t + 1)
                dve.tensor_scalar(fms[:, t:t + 1], fss[:, t:t + 1], 1.0 / D, EPS, ALU.mult, ALU.add
                                  ).then_inc(fms_done, 1)

            dve.wait_ge(fgain_in, 16)
            final_mean(0)
            for t in range(LT):
                if t + 1 < LT:
                    final_mean(t + 1)
                dve.wait_ge(frs_done, t + 1)
                dve.scalar_tensor_tensor(out=fx[t], in0=fx[t], scalar=frs[:, t:t + 1], in1=fgain,
                                         op0=ALU.mult, op1=ALU.mult).then_inc(out_done, 1)

        @block.tensor
        def _(pe):
            def weights(item, width=512, k=KT):
                return slot(place[item])[:, 0:k * width].rearrange("p (k n) -> p k n", k=k)

            def ada_product(n):
                item = ada_items[n]
                if n > ADA_FIRST:
                    pe.wait_ge(ada_out, n - ADA_FIRST)
                wait_slot(pe, item)
                w = weights(item)
                for r in range(2):
                    for j in range(4):
                        k = 2 * j + r
                        last = pe.matmul(ps[32 * j:32 * j + 32, 7, :], csil[:, k * 32:(k + 1) * 32], w[:, k, :],
                                         start=(r == 0), stop=(r == 1))
                last.then_inc(ada_mm, 1)

            def ada_columns(n):
                pe.wait_ge(ada_row, n + 1)
                if n:
                    pe.wait_ge(first_cols, n)
                rows = slice(64 * (n % 2), 64 * (n % 2) + 64)
                for k in range(KT):
                    last = pe.matmul(ps[rows, 6, 2 * k:2 * k + 2], modrow[:, k:512:KT], sel[:, 0:2],
                                     start=True, stop=True)
                last.then_inc(ada_sum, 1)

            def ada_total(n):
                pe.wait_ge(ada_row, n + 1)
                pe.matmul(ps[0:32, 7, :], sel, modrow[:], start=True, stop=True).then_inc(ada_sum, 1)

            counts = [pe.alloc_register(f"pe_count{n}") for n in range(2)]
            pe.wait_ge(csil_done, 1)
            pe.wait_ge(consts_in, 16)

            norms = 0
            for l in range(DEPTH):
                def transpose_x(t):
                    n = norms + t
                    pe.wait_ge(xhat, n + 1)
                    if n:
                        pe.wait_ge(h_done, n)
                    for k in range(KT):
                        last = pe.transpose(bank(4, 2)[:, k * P:(k + 1) * P], hx[:, k:D:KT], ident)
                        if k == KT // 2 - 1:
                            last.then_inc(t1_half, 1)
                    last.then_inc(t1_mm, 1)

                def main(t, ch):
                    n = tile_no(l, t)
                    w = weights(("in", l, ch), IN_CHUNK[ch][1] - IN_CHUNK[ch][0])
                    a, b = chunk_cols(l, t, ch)
                    if a == b:
                        pe.wait_ge(h_done, norms + t + 1)
                        return
                    if ch == 0:
                        pe.wait_ge(h_half, norms + t + 1)
                    if t == 0:
                        wait_slot(pe, ("in", l, ch))
                    if n:
                        pe.wait_ge(main_ev, main_count(*tile_before(l, t), ch))
                        if ch == 3:
                            pe.wait_ge(sq2, n)
                    if l and t == 0:
                        pe.wait_ge(y_done, l * NE)
                    for k in range(KT):
                        if k == KT // 2:
                            pe.wait_ge(h_done, norms + t + 1)
                        last = pe.matmul(ps[:, ch, 0:b - a], h_t[n % 2][:, k, :], w[:, k, 0:b - a],
                                         start=(k == 0), stop=(k == KT - 1))
                    last.then_inc(main_mm, 1)

                def small(t, u):
                    n = tile_no(l, t)
                    p = pt[n % 2]
                    if u not in small_uses(l, t):
                        return
                    if small_before(l, t, u):
                        pe.wait_ge(small_ev, small_before(l, t, u))
                    dst = ps[:, 6 + u % 2, :]
                    if u == 0:
                        if n == 0:
                            pe.wait_ge(first_cols, ADA_FIRST)
                        pe.wait_ge(cqn, n + 1)
                        for k in range(0 if keys_only(l, t) else 2):
                            pe.transpose(dst[:, k * P:(k + 1) * P], p[:, CQ + k:CKV:2], ident)
                        last = pe.transpose(dst[:, 2 * P:3 * P], p[:, CKV:KR], ident)
                    elif u == 1:
                        pe.wait_ge(small_ev, small_count(l, t, 0))
                        if t == 0:
                            pe.wait_ge(wproj_in, 16 * 9 * (l + 1))
                        for k in range(2):
                            last = pe.matmul(dst[:, 0:384], c_t[:, k, :], wuq[:, k * 384:(k + 1) * 384],
                                             start=(k == 0), stop=(k == 1))
                    elif u == 2:
                        pe.wait_ge(small_ev, small_count(l, t, 0))
                        last = pe.matmul(dst, c_t[:, 2, :], wukv[:], start=True, stop=True)
                    else:
                        if u in (3, 4):
                            pe.wait_ge(rope_ac, n + 1)
                        if u in (6, 7):
                            pe.wait_ge(rope_b, n + 1)
                        if u == 3:
                            srcs = [p[:, QA + P * b:QA + P * (b + 1)] for b in range(4)]
                        elif u == 4:
                            srcs = [p[:, KA:VA], p[:, QD:QD + P], p[:, QD + P:KD], p[:, KD:KD + P]]
                        elif u == 5:
                            srcs = [p[:, KD + P:VD]]
                        else:
                            srcs = [(q96 if u == 6 else k96)[:, h] for h in range(B_HEADS)]
                        rows = P if u < 6 else B_QK
                        for b, s in enumerate(srcs):
                            if u == 4 and keys_only(l, t) and b in (1, 2):
                                continue
                            last = pe.transpose(dst[0:rows, b * P:(b + 1) * P], s, ident)
                    last.then_inc(small_mm, 1)

                if l == 0:
                    for n in range(ADA_FIRST):
                        ada_product(n)
                        ada_columns(n)
                        if n == 1:
                            transpose_x(0)
                else:
                    transpose_x(0)
                for t in range(NT + 1):
                    for ch in range(NCH):
                        if t < NT:
                            main(t, ch)
                        if t >= 1:
                            for u in ([0], [1, 2], [3, 4, 5, 6, 7], [])[ch]:
                                small(t - 1, u)
                        if ch == 1 and t + 1 < NT:
                            transpose_x(t + 1)
                norms += NT

                def scores(s):
                    _, qi, j = s
                    n = step_no(l, qi, j)
                    g = ATT.index((l, qi))
                    kind, h, m = STEPS[j]
                    if j == 0:
                        pe.wait_ge(qz_done, g + 1)
                    if n >= 2:
                        pe.wait_ge(exp_done, n - 1)
                    z = qz[:, (g % 2) * 16 * P:(g % 2 + 1) * 16 * P].rearrange("p (h t) -> p h t", h=16)
                    cols = slice(qi * P, (qi + 1) * P)
                    if kind == "A":
                        lhs, kb, rows = z[:, h, :], B_AK, P
                    elif kind == "B":
                        lhs, kb, rows = qk_t[0:B_QK, B_BQ + h, cols], B_BK + h, B_QK
                    else:
                        mm = 2 * h + m
                        lhs, kb, rows = z[:, 8 + mm, :], B_CK + mm // 4, P
                    kt = [t for t, _ in key_tiles(l, qi, kind)]
                    dst = bank(2 * (n % 2), 2)
                    lat = [t for t in kt if t < LT]
                    if lat:
                        w = len(lat) * P
                        pe.matmul(dst[:, SEQ - w:SEQ], lhs, qk_t[0:rows, kb, lat[0] * P:lat[0] * P + w],
                                  start=True, stop=True)
                    last = pe.matmul(dst[:, SEQ:TOK], lhs, qk_t[0:rows, kb, SEQ:TOK], start=True, stop=True)
                    if kind == "A":
                        if n == 0:
                            pe.wait_ge(sink_done, 1)
                        c = NSK + l * A_HEADS + h
                        last = pe.matmul(dst[:, TOK:TOK + 1], ident, sinkb[:, c:c + 1], start=True, stop=True)
                    last.then_inc(s_mm, 1)

                seq = [(l, qi, j) for qi in range(nq(l)) for j in range(NS)]
                pe.wait_ge(main_ev, main_count(l, NT - 1, 3))
                pe.wait_ge(sq2, tile_no(l, NT - 1) + 1)
                pe.wait_ge(small_ev, small_count(l, NT - 1))
                scores(seq[0])
                scores(seq[1])

                def transpose_prob(s):
                    _, qi, j = s
                    n = step_no(l, qi, j)
                    kind, h, m = STEPS[j]
                    it = item_no(l, qi, ITEM[j])
                    if kind == "C":
                        pe.wait_ge(comb, C_HEADS * (l * NT + qi) + h + 1)
                        src = prob[(n - 1) % 3]
                    else:
                        pe.wait_ge(exp_done, n + 1)
                        src = prob[n % 3]
                    if ITEM[j] or qi:
                        pe.wait_ge(pta_ev, it)
                        pe.wait_ge(ptd_ev, it)
                    kt = key_tiles(l, qi, kind)
                    a = act_share(len(kt))
                    for b, (_, c0) in enumerate(kt):
                        last = pe.transpose(ps[:, 4 + (b >= a), (b - a * (b >= a)) * P:][:, 0:P],
                                            src[:, c0:c0 + P], ident)
                    last.then_inc(t_mm, 1)

                def values(pair):
                    if pair is None:
                        return
                    qi, i = pair
                    kind = STEPS[ITEM.index(i)][0]
                    it = item_no(l, qi, i)
                    kt = key_tiles(l, qi, kind)
                    pe.wait_ge(pta_ev, it + 2)
                    pe.wait_ge(ptd_ev, it + 2)
                    if it:
                        pe.wait_ge(o_ev, it // 2)
                    for b, (t, _) in enumerate(kt):
                        for n in range(2):
                            h = STEPS[ITEM.index(i + n)][1]
                            if kind == "A":
                                v = va[:, t, (h // 4) * HD:(h // 4 + 1) * HD]
                            else:
                                v = (vb if kind == "B" else vc)[:, t, h * 64:(h + 1) * 64]
                            last = pe.matmul(ps[64 * n:64 * n + 64, 6, 0:P], v, prob_t[(it + n) % 4][:, b, :],
                                             start=(b == 0), stop=(b == len(kt) - 1))
                    last.then_inc(pv_mm, 1)

                def back(pair):
                    if pair is None:
                        return
                    n = pair_no(l, *pair)
                    pe.wait_ge(ov_ev, n + 1)
                    pe.transpose(ps[:, 6, P:2 * P], ov[n % 2], ident).then_inc(back_mm, 1)

                def output_transposes(qi):
                    g = ATT.index((l, qi))
                    pe.wait_ge(on_done, g + 1)
                    it = item_no(l, qi, OT_AFTER) + NI if qi < nq(l) - 1 else item_no(l, qi, NI - 1)
                    pe.wait_ge(pta_ev, it + 1)
                    pe.wait_ge(ptd_ev, it + 1)
                    for kk in range(KT):
                        last = pe.transpose(bank(4, 2)[:, kk * P:(kk + 1) * P], ob[g % 2][:, kk:D:KT], ident)
                    last.then_inc(ot_mm, 1)

                for k, s in enumerate(seq):
                    _, qi, j = s
                    if k + 2 < len(seq):
                        scores(seq[k + 2])
                    if LASTSTEP[j]:
                        if qi and ITEM[j] == OT_AFTER + 1:
                            g = ATT.index((l, qi))
                            pe.wait_ge(ota_ev, g)
                            pe.wait_ge(otd_ev, g)
                        transpose_prob(s)
                        (back if ITEM[j] % 2 else values)(pair_behind(l, qi, ITEM[j], 1))
                        if qi and ITEM[j] == OT_AFTER:
                            output_transposes(qi - 1)
                    a = ada_at(l, qi, j)
                    if a is not None:
                        ada_product(a)
                    a = ada_sum_at(l, qi, j)
                    if a is not None:
                        ada_total(a)
                values((nq(l) - 1, NI - 2))
                back((nq(l) - 1, NI - 2))
                output_transposes(nq(l) - 1)

                def logits(t):
                    g = tile_no(l, t)
                    pe.wait_ge(h_half, norms + t + 1)
                    if t == 0:
                        pe.wait_ge(g1_in, 16 * 3 * (l + 1))
                    if t:
                        pe.wait_ge(rexp_done, g)
                    for k in range(KT):
                        if k == KT // 2:
                            pe.wait_ge(h_done, norms + t + 1)
                        last = pe.matmul(ps[:, 6, 0:NE], h2_t[:, k, :], wr[:, k * NE:(k + 1) * NE],
                                         start=(k == 0), stop=(k == KT - 1))
                    last.then_inc(lg_mm, 1)

                def affinities(t):
                    g = tile_no(l, t)
                    pe.wait_ge(aff_done, g + 1)
                    if t:
                        pe.wait_ge(at_ev, g)
                    pe.transpose(ps[0:NE, 7, 0:P], aff, ident).then_inc(at_mm, 1)

                ng = len([a for a in ATT if a[0] <= l])
                pe.wait_ge(ota_ev, ng)
                pe.wait_ge(otd_ev, ng)
                pe.wait_ge(o_ev, pair_no(l, nq(l) - 1, NI - 1) + 1)
                if l == 0:
                    pe.wait_ge(ada_out, len(ada_items) - ADA_FIRST)
                for t in range(nq(l) + 2):
                    g = tile_no(l, t)
                    for h in range(2):
                        if t < nq(l):
                            if t >= 2:
                                pe.wait_ge(xo_done, g - 1)
                            if t == 0:
                                wait_slot(pe, ("out", l, h))
                            w = weights(("out", l, h))
                            for k in range(KT):
                                last = pe.matmul(ps[:, 2 * (g % 2) + h, :], qk_t[:, OT_BLOCK[k], t * P:(t + 1) * P],
                                                 w[:, k, :], start=(k == 0), stop=(k == KT - 1))
                            last.then_inc(wo_mm, 1)
                        if h == 0 and t >= 2:
                            affinities(t - 2)
                        if 1 <= t <= nq(l):
                            (logits if h else transpose_x)(t - 1)
                norms += nq(l)

                rows = CAP_L + (CAP_C if nq(l) > LT else 0)
                pe.wait_ge(top_done, l + 1)
                if l == DEPTH - 1:
                    pe.transpose(ps[:, 6, 0:NE], sval[0:NE, 0:P], ident[0:NE, 0:NE])
                    pe.transpose(ps[:, 6, NE:2 * NE], sidx_f[0:NE, 0:P], ident[0:NE, 0:NE]).then_inc(gt_mm, 1)
                    break
                pe.transpose(ps[0:rows, 6, 0:NE], sval[0:NE, 0:rows], ident[0:NE, 0:NE])
                pe.transpose(ps[0:rows, 6, NE:2 * NE], sidx_f[0:NE, 0:rows], ident[0:NE, 0:NE]).then_inc(gt_mm, 1)

                def step(n, b, r, first, pair):
                    def landed(q, pos):
                        pe.wait_ge(ring_in[q % NSLOT], pos)
                    if b < NE:
                        before = [] if l == 0 and first and b == 0 else [(xgt_ev, n)]
                        wait_in_loop(pe, counts, gt_mm, l + 1, (xg_in[b % 2], pair * 16 + 16), *before)
                        for k in range(KT):
                            last = pe.transpose(ps[:, k // 4, (k % 4) * rows:(k % 4 + 1) * rows],
                                                xg[b % 2][0:rows, k:D:KT], ident[0:rows, 0:rows])
                        last.then_inc(xgt_mm, 1)
                    if not first or b >= 2:
                        pe.wait_ge(hidt_ev, n - 1)
                        if not (l == 0 and first and b == 2):
                            pe.wait_ge(y_done, n - 2)
                        landed(*r[0])
                        w = slot(r[0][0]).rearrange("p (k n) -> p k n", k=4)
                        for h in range(2):
                            for k in range(4):
                                last = pe.matmul(ps[0:rows, 5 + h, :], hid_t[b % 2][:, k, 0:rows],
                                                 w[:, k, h * 512:(h + 1) * 512], start=(k == 0), stop=(k == 3))
                        last.then_inc(down_mm, 1)
                    if b < NE:
                        pe.wait_ge(xgt_ev, n + 1)
                        if not (l == 0 and first and b == 0):
                            pe.wait_ge(silu_done, n)
                        landed(*r[1])
                        w = slot(r[1][0]).rearrange("p (k n) -> p k n", k=KT)
                        for k in range(KT):
                            last = pe.matmul(ps[0:rows, 2, :], xg_t[b % 2][:, k, 0:rows], w[:, k, :],
                                             start=(k == 0), stop=(k == KT - 1))
                        last.then_inc(gate_mm, 1)
                    if not first or b >= 1:
                        if b <= NE:
                            before = [] if l == 0 and first and b == 1 else [(hidt_ev, n - 1)]
                            wait_in_loop(pe, counts, gt_mm, l + 1, (hid_done, n), *before)
                            for k in range(4):
                                last = pe.transpose(ps[:, 4, k * rows:(k + 1) * rows],
                                                    hid[(b - 1) % 2][0:rows, k:512:4], ident[0:rows, 0:rows])
                            last.then_inc(hidt_mm, 1)
                    if b < NE:
                        if not (l == 0 and first and b == 0):
                            pe.wait_ge(hid_done, n)
                        landed(*r[2])
                        w = slot(r[2][0]).rearrange("p (k n) -> p k n", k=KT)
                        for k in range(KT):
                            last = pe.matmul(ps[0:rows, 3, :], xg_t[b % 2][:, k, 0:rows], w[:, k, :],
                                             start=(k == 0), stop=(k == KT - 1))
                        last.then_inc(up_mm, 1)

                def at(item):
                    r_ = place.get(item)
                    return None if r_ is None else (r_, 16 * (r_ // NSLOT + 1))

                for e in range(LOOP_E):
                    step(l * NE + e, e, [at(("d", l, e - 2)), at(("g", l, e)), at(("u", l, e))], True,
                         (l * NE + e) // 2)
                turns = 3 * BODY // NSLOT
                with pe.Fori(0, (NE - LOOP_E) // BODY) as itr:
                    for b in range(BODY):
                        e = LOOP_E + b
                        where = [at(("d", l, e - 2)), at(("g", l, e)), at(("u", l, e))]
                        step(BODY * itr + (l * NE + e), e,
                             [(q, itr * (16 * turns) + v) for q, v in where], False,
                             itr * (BODY // 2) + (l * NE + e) // 2)
                step(l * NE + NE, NE, [at(("d", l, NE - 2)), None, None], False, None)
                step(l * NE + NE + 1, NE + 1, [at(("d", l, NE - 1)), None, None], False, None)

            halves = [slice(CAP_L * h, CAP_L * (h + 1)) for h in range(2)]
            with pe.Fori(0, PAIRS // 2) as it:
                for b in range(2):
                    n = 2 * it + (PAIR_BASE + b)
                    p = 2 * it + b
                    pair_w = []
                    for kind, h, dst, landed, loads, _ in PAIR_SLOTS:
                        pair_w.append((dst.rearrange("p (k n) -> p k n", k=4 if kind == "d" else KT), landed,
                                       16 * p + 16 * (loads + 1)))
                    wait_in_loop(pe, counts, gt_mm, DEPTH, (xg_in[b], 16 * it + 16 * (PAIR_BASE // 2 + 1)),
                                 (xgt_ev, n))
                    for k in range(KT):
                        last = pe.transpose(ps[:, k // 4, (k % 4) * P:(k % 4 + 1) * P], xg[b][:, k:D:KT], ident)
                    last.then_inc(xgt_mm, 1)
                    pe.wait_ge(xgt_ev, n + 1)
                    for g, (bk, read, done) in enumerate(((2, silu_done, gate_mm), (3, hid_done, up_mm))):
                        pe.wait_ge(read, n)
                        for w, landed, count in pair_w[2 * g:2 * g + 2]:
                            pe.wait_ge(landed, count)
                        for k in range(KT):
                            for h in range(2):
                                last = pe.matmul(ps[halves[h], bk, :], xg_t[b][:, k, halves[h]],
                                                 pair_w[2 * g + h][0][:, k, :], start=(k == 0), stop=(k == KT - 1))
                        last.then_inc(done, 1)
                    wait_in_loop(pe, counts, gt_mm, DEPTH, (hid_done, n + 1), (hidt_ev, n))
                    for k in range(4):
                        last = pe.transpose(ps[:, 4, k * P:(k + 1) * P], hid[b][:, k:512:4], ident)
                    last.then_inc(hidt_mm, 1)
                    pe.wait_ge(hidt_ev, n + 1)
                    pe.wait_ge(y_done, n)
                    for w, landed, count in pair_w[4:6]:
                        pe.wait_ge(landed, count)
                    for c0 in range(2):
                        for k in range(4):
                            for h in range(2):
                                last = pe.matmul(ps[halves[h], 5 + c0, :], hid_t[b][:, k, halves[h]],
                                                 pair_w[4 + h][0][:, k, c0 * 512:(c0 + 1) * 512],
                                                 start=(k == 0), stop=(k == 3))
                    last.then_inc(down_mm, 1)
    es.close()


_INS = ["x", "c", "ctx", "c_ctx", "norm1", "norm2", "w_ada", "b_ada", "w_in", "sink", "mla_q_norm", "w_uq",
        "mla_kv_norm", "w_ukv", "lam_q1", "lam_k1", "lam_q2", "lam_k2", "diff_norm", "w_out", "w_router",
        "w_gate", "w_up", "w_down", "final_norm"]


def kernel(**inputs):
    import concourse.bacc as _bacc
    from concourse.bass_utils import run_bass_kernel_spmd as _run

    nc = _bacc.Bacc("TRN2", target_bir_lowering=False, num_devices=1)
    arrays = {f"in_{name}_dram": np.ascontiguousarray(inputs[name]) for name in _INS}
    arrays["shape_constants"] = shape_constants()
    args = [nc.dram_tensor(name, a.shape, mybir.dt.from_np(a.dtype), kind="ExternalInput").ap()
            for name, a in arrays.items()]
    args.append(nc.dram_tensor("out_0_dram", (1, SEQ, D), F32, kind="ExternalOutput").ap())
    build(nc, *args)
    r = _run(nc, [arrays], core_ids=[0])
    return r.results[0]["out_0_dram"]
```
